# Optimizing a Trainium2 kernel written in Bass

```python
import math
import jax, jax.numpy as jnp
from jax import lax
import numpy as np

D_MODEL = 2048
BATCH = 1
SEQ = 256
DEPTH = 1

ATTN_WIDTH = D_MODEL // 2
ATTN_HEAD_DIM = 128
ATTN_HEADS = ATTN_WIDTH // ATTN_HEAD_DIM
DILATED_BRANCHES = ((128, 1), (512, 4), (2048, 16))
ROPE_THETA = 500000.0
ROPE_DIM = ATTN_HEAD_DIM // 4
HG_WIDTH = D_MODEL - ATTN_WIDTH
HG_EXPAND = 128
HG_HEADS = HG_WIDTH // HG_EXPAND
HG_CHUNK = 64
MIX_WIDTH = ATTN_WIDTH + HG_WIDTH
IN_COLS = 3 * ATTN_WIDTH + 4 * HG_WIDTH
D_FF = 4 * D_MODEL
N_MOD = 6
EPS = 1e-6


def rms_norm(x, w):
    xf = x.astype(jnp.float32)
    y = xf * lax.rsqrt(jnp.mean(xf * xf, axis=-1, keepdims=True) + EPS)
    return y * w.astype(jnp.float32)

def rope_partial(x, pos):
    half = ROPE_DIM // 2
    inv_freq = ROPE_THETA ** (-(jnp.arange(half, dtype=jnp.float32) * 2.0) / ROPE_DIM)
    ang = pos.astype(jnp.float32)[..., None] * inv_freq
    cos = jnp.cos(ang)[:, :, None, :]
    sin = jnp.sin(ang)[:, :, None, :]
    x1 = x[..., :half]
    x2 = x[..., half:ROPE_DIM]
    return jnp.concatenate([x1 * cos - x2 * sin, x2 * cos + x1 * sin, x[..., ROPE_DIM:]], axis=-1)

def dilated_branch(q, k, v, window, dilation):
    blk = window // dilation
    B, S, H, Dh = q.shape
    span = blk * dilation
    L = -(-S // span) * span
    M = L // dilation
    nb = M // blk

    def to_blocks(t):
        t = jnp.pad(t, ((0, 0), (0, L - S), (0, 0), (0, 0)))
        t = t.reshape(B, M, dilation, H, Dh).transpose(0, 2, 3, 1, 4)
        return t.reshape(B, dilation, H, nb, blk, Dh)

    def with_prev(t):
        prev = jnp.pad(t[:, :, :, :-1], ((0, 0), (0, 0), (0, 0), (1, 0), (0, 0), (0, 0)))
        return jnp.concatenate([prev, t], axis=4)

    qb = to_blocks(q)
    kk = with_prev(to_blocks(k))
    vv = with_prev(to_blocks(v))
    s = jnp.einsum('brhnqd,brhnkd->brhnqk', qb, kk) / math.sqrt(Dh)
    i = jnp.arange(blk)[:, None]
    j = jnp.arange(2 * blk)[None, :]
    dist = blk + i - j
    band = (dist >= 0) & (dist <= blk)
    not_before_start = (jnp.arange(nb)[:, None, None] > 0) | (j[None] >= blk)
    mask = band[None] & not_before_start
    s = jnp.where(mask, s, -jnp.inf)
    m = jnp.max(s, axis=-1, keepdims=True)
    p = jnp.exp(s - m)
    l = jnp.sum(p, axis=-1, keepdims=True)
    o = jnp.einsum('brhnqk,brhnkd->brhnqd', p, vv) / l
    lse = (m + jnp.log(l))[..., 0]
    o = o.reshape(B, dilation, H, M, Dh).transpose(0, 3, 1, 2, 4).reshape(B, L, H, Dh)[:, :S]
    lse = lse.reshape(B, dilation, H, M).transpose(0, 3, 1, 2).reshape(B, L, H)[:, :S]
    return o, lse

def dilated_attention(q, k, v):
    outs, lses = [], []
    for window, dilation in DILATED_BRANCHES:
        o, lse = dilated_branch(q, k, v, window, dilation)
        outs.append(o)
        lses.append(lse)
    w = jax.nn.softmax(jnp.stack(lses, axis=0), axis=0)
    return jnp.sum(w[..., None] * jnp.stack(outs, axis=0), axis=0)

def hgrn2(q, f_logit, inp, lb):
    B, S, _ = q.shape
    C, Hh, dk = HG_CHUNK, HG_HEADS, HG_EXPAND
    f = lb + (1.0 - lb) * jax.nn.sigmoid(f_logit)
    logf = jnp.log(f)
    key = 1.0 - f
    qf = jax.nn.silu(q) * (dk ** -0.5)

    def chunks(t):
        return t.reshape(B, S // C, C, Hh, dk).transpose(1, 0, 3, 2, 4)

    causal = jnp.tril(jnp.ones((C, C), dtype=bool))[..., None]

    def step(state, xs):
        qc, kc, vc, lfc = xs
        b = jnp.cumsum(lfc, axis=2)
        o_inter = jnp.einsum('bhck,bhkv->bhcv', qc * jnp.exp(b), state)
        diff = b[:, :, :, None, :] - b[:, :, None, :, :]
        decay = jnp.exp(jnp.where(causal, diff, -jnp.inf))
        a = jnp.einsum('bhtk,bhsk,bhtsk->bhts', qc, kc, decay)
        o = o_inter + jnp.einsum('bhts,bhsv->bhtv', a, vc)
        b_last = b[:, :, -1:, :]
        new_state = jnp.exp(b_last[:, :, 0, :])[..., None] * state + jnp.einsum(
            'bhsk,bhsv->bhkv', kc * jnp.exp(b_last - b), vc)
        return new_state, o

    state0 = jnp.zeros((B, Hh, dk, dk), dtype=jnp.float32)
    _, o = lax.scan(step, state0, (chunks(qf), chunks(key), chunks(inp), chunks(logf)))
    return o.transpose(1, 0, 3, 2, 4).reshape(B, S, Hh, dk)

def first_inputs(seed: int = 0) -> dict:
    key = jax.random.key(seed)
    ks = jax.random.split(key, 20)
    f32 = jnp.float32
    nrm = lambda k, shape, scale: jax.random.normal(k, shape, f32) * scale
    gain = lambda k, shape: 1.0 + 0.05 * jax.random.normal(k, shape, f32)
    x = jax.random.normal(ks[0], (BATCH, SEQ, D_MODEL), f32)
    c = jax.random.normal(ks[1], (BATCH, D_MODEL), f32)
    positions = (jnp.arange(SEQ, dtype=jnp.int32)[None, :]
                 + jax.random.randint(ks[2], (BATCH, 1), 0, 4096, dtype=jnp.int32))
    return {
        'x': x,
        'c': c,
        'positions': positions,
        'norm1_w': gain(ks[3], (DEPTH, D_MODEL)),
        'w_ada': nrm(ks[4], (DEPTH, D_MODEL, N_MOD * D_MODEL), 0.5 * D_MODEL ** -0.5),
        'b_ada': nrm(ks[5], (DEPTH, N_MOD * D_MODEL), 0.02),
        'w_in': nrm(ks[6], (DEPTH, D_MODEL, IN_COLS), D_MODEL ** -0.5),
        'q_norm_w': gain(ks[7], (DEPTH, ATTN_HEAD_DIM)),
        'k_norm_w': gain(ks[8], (DEPTH, ATTN_HEAD_DIM)),
        'attn_out_norm_w': gain(ks[9], (DEPTH, ATTN_WIDTH)),
        'hg_lb_logits': nrm(ks[10], (DEPTH + 1, HG_WIDTH), 0.5),
        'hg_norm_w': gain(ks[11], (DEPTH, HG_EXPAND)),
        'w_out': nrm(ks[12], (DEPTH, MIX_WIDTH, D_MODEL), MIX_WIDTH ** -0.5),
        'norm2_w': gain(ks[13], (DEPTH, D_MODEL)),
        'w_ff1': nrm(ks[14], (DEPTH, D_MODEL, D_FF), D_MODEL ** -0.5),
        'w_ff2': nrm(ks[15], (DEPTH, D_FF, D_MODEL), D_FF ** -0.5),
    }

def first_block(x, c, positions, norm1_w, w_ada, b_ada, w_in, q_norm_w, k_norm_w, attn_out_norm_w,
              hg_lb_logits, hg_norm_w, w_out, norm2_w, w_ff1, w_ff2):
    dt = x.dtype
    B, S, _ = x.shape
    lb_all = jnp.cumsum(jax.nn.softmax(hg_lb_logits.astype(jnp.float32), axis=0), axis=0)
    split_at = [ATTN_WIDTH, 2 * ATTN_WIDTH, 3 * ATTN_WIDTH, 3 * ATTN_WIDTH + HG_WIDTH,
                3 * ATTN_WIDTH + 2 * HG_WIDTH, 3 * ATTN_WIDTH + 3 * HG_WIDTH]
    for l in range(DEPTH):
        mod = (jax.nn.silu(c) @ w_ada[l] + b_ada[l]).astype(jnp.float32)
        shift1, scale1, gate1, shift2, scale2, gate2 = [m[:, None, :] for m in jnp.split(mod, N_MOD, axis=-1)]

        h = rms_norm(x, norm1_w[l]) * (1.0 + scale1) + shift1
        proj = (h.astype(dt) @ w_in[l]).astype(jnp.float32)
        aq, ak, av, gq, gf, gi, gg = jnp.split(proj, split_at, axis=-1)

        hs = (B, S, ATTN_HEADS, ATTN_HEAD_DIM)
        aq = rope_partial(rms_norm(aq.reshape(hs), q_norm_w[l]), positions)
        ak = rope_partial(rms_norm(ak.reshape(hs), k_norm_w[l]), positions)
        attn = dilated_attention(aq, ak, av.reshape(hs)).reshape(B, S, ATTN_WIDTH)
        attn = rms_norm(attn, attn_out_norm_w[l])

        ho = hgrn2(gq, gf, gi, lb_all[l])
        hg = rms_norm(ho, hg_norm_w[l]) * jax.nn.silu(gg.reshape(B, S, HG_HEADS, HG_EXPAND))
        hg = hg.reshape(B, S, HG_WIDTH)

        mix = jnp.concatenate([attn, hg], axis=-1).astype(dt) @ w_out[l]
        x = x + (gate1 * mix.astype(jnp.float32)).astype(dt)

        h2 = rms_norm(x, norm2_w[l]) * (1.0 + scale2) + shift2
        ff = jnp.square(jax.nn.relu(h2.astype(dt) @ w_ff1[l])) @ w_ff2[l]
        x = x + (gate2 * ff.astype(jnp.float32)).astype(dt)
    return x


N_MIXERS = 3
SB_HEADS = 16
SB_HEAD_DIM = D_MODEL // SB_HEADS
SB_WIDTH = SB_HEADS * SB_HEAD_DIM
Q_BLOCK = 128
GM_CHUNK = 128
GM_GROUPS = 16
GM_WIDTH = D_MODEL
GM_GROUP_DIM = GM_WIDTH // GM_GROUPS
SSD_INNER = 2 * D_MODEL
SSD_HEAD_DIM = 64
SSD_HEADS = SSD_INNER // SSD_HEAD_DIM
SSD_GROUPS = 8
SSD_HPG = SSD_HEADS // SSD_GROUPS
SSD_STATE = 128
SSD_CONV = 4
SSD_CHUNK = 128
SSD_CONV_DIM = SSD_INNER + 2 * SSD_GROUPS * SSD_STATE
SSD_PROJ = SSD_INNER + SSD_CONV_DIM + SSD_HEADS
MLP_HIDDEN = 4 * D_MODEL
N_A = len(range(0, DEPTH, N_MIXERS))
N_B = len(range(1, DEPTH, N_MIXERS))
N_C = len(range(2, DEPTH, N_MIXERS))


def rms_norm_2(x, g):
    xf = x.astype(jnp.float32)
    y = xf * lax.rsqrt(jnp.mean(xf * xf, axis=-1, keepdims=True) + EPS)
    return (y * g.astype(jnp.float32)).astype(x.dtype)

def stick_breaking_attention(h, w_qkv, q_g, k_g, w_o):
    b, s, _ = h.shape
    q, k, v = jnp.split(h @ w_qkv, 3, axis=-1)
    q = rms_norm_2(q.reshape(b, s, SB_HEADS, SB_HEAD_DIM), q_g).transpose(0, 2, 1, 3)
    k = rms_norm_2(k.reshape(b, s, SB_HEADS, SB_HEAD_DIM), k_g).transpose(0, 2, 1, 3)
    v = v.reshape(b, s, SB_HEADS, SB_HEAD_DIM).transpose(0, 2, 1, 3)
    scale = SB_HEAD_DIM ** -0.5
    n_blk = s // Q_BLOCK
    q_blocks = q.reshape(b, SB_HEADS, n_blk, Q_BLOCK, SB_HEAD_DIM).transpose(2, 0, 1, 3, 4)
    k_pos = jnp.arange(s)

    def one_block(args):
        qb, start = args
        z = jnp.einsum('bhqd,bhkd->bhqk', qb, k).astype(jnp.float32) * scale
        q_pos = start + jnp.arange(Q_BLOCK)
        mask = k_pos[None, :] < q_pos[:, None]
        log_beta = jax.nn.log_sigmoid(z)
        log_1m = jnp.where(mask, jax.nn.log_sigmoid(-z), 0.0)
        suffix = lax.cumsum(log_1m, axis=3, reverse=True) - log_1m
        a = jnp.where(mask, jnp.exp(log_beta + suffix), 0.0)
        return jnp.einsum('bhqk,bhkd->bhqd', a.astype(v.dtype), v)

    starts = jnp.arange(n_blk, dtype=jnp.int32) * Q_BLOCK
    o = lax.map(one_block, (q_blocks, starts))
    o = o.transpose(1, 0, 3, 2, 4).reshape(b, s, SB_WIDTH)
    return o @ w_o

def chunked_spatial_gating(h, w_in, v_g, w_s, b_s, w_o):
    b, s, _ = h.shape
    u, v = jnp.split(jax.nn.gelu(h @ w_in, approximate=False), 2, axis=-1)
    v = rms_norm_2(v, v_g)
    n_chunk = s // GM_CHUNK
    v = v.reshape(b, n_chunk, GM_CHUNK, GM_GROUPS, GM_GROUP_DIM)
    u = u.reshape(b, n_chunk, GM_CHUNK, GM_GROUPS, GM_GROUP_DIM)
    causal = jnp.tril(jnp.ones((GM_CHUNK, GM_CHUNK), dtype=bool))
    w = jnp.where(causal[None], w_s, 0.0)
    mixed = jnp.einsum('gts,bcsgd->bctgd', w.astype(v.dtype), v) + b_s.T[:, :, None]
    y = (u * mixed).reshape(b, s, GM_WIDTH)
    return y @ w_o

def ssd_chunked_scan(x, dt, a, bm, cm):
    b, s = x.shape[:2]
    c, L = s // SSD_CHUNK, SSD_CHUNK
    xs = (x * dt[..., None]).reshape(b, c, L, SSD_GROUPS, SSD_HPG, SSD_HEAD_DIM)
    da = (dt * a).reshape(b, c, L, SSD_GROUPS, SSD_HPG).transpose(0, 3, 4, 1, 2)
    bc = bm.reshape(b, c, L, SSD_GROUPS, SSD_STATE)
    cc = cm.reshape(b, c, L, SSD_GROUPS, SSD_STATE)
    a_cum = jnp.cumsum(da, axis=-1)
    seg = a_cum[..., :, None] - a_cum[..., None, :]
    tri = jnp.tril(jnp.ones((L, L), dtype=bool))
    decay = jnp.exp(jnp.where(tri, seg, -jnp.inf))
    cb = jnp.einsum('bclgn,bcsgn->bgcls', cc, bc)
    y_diag = jnp.einsum('bgcls,bgrcls,bcsgrp->bclgrp', cb, decay, xs)
    decay_states = jnp.exp(a_cum[..., -1:] - a_cum)
    states = jnp.einsum('bclgn,bgrcl,bclgrp->cbgrpn', bc, decay_states, xs)
    chunk_decay = jnp.exp(a_cum[..., -1]).transpose(3, 0, 1, 2)

    def step(carry, inp):
        st, dec = inp
        return carry * dec[..., None, None] + st, carry

    _, prev = lax.scan(step, jnp.zeros_like(states[0]), (states, chunk_decay))
    y_off = jnp.einsum('bclgn,cbgrpn,bgrcl->bclgrp', cc, prev, jnp.exp(a_cum))
    return (y_diag + y_off).reshape(b, s, SSD_GROUPS, SSD_HPG, SSD_HEAD_DIM)

def ssd_mixer(h, w_in, conv_w, conv_b, dt_bias, a_log, d_skip, norm_g, w_o):
    b, s, _ = h.shape
    z, xbc, dt = jnp.split(h @ w_in, [SSD_INNER, SSD_INNER + SSD_CONV_DIM], axis=-1)
    xbc = lax.conv_general_dilated(xbc, conv_w[:, None, :].astype(xbc.dtype), window_strides=(1,),
                                   padding=[(SSD_CONV - 1, 0)],
                                   dimension_numbers=('NWC', 'WIO', 'NWC'),
                                   feature_group_count=SSD_CONV_DIM) + conv_b
    xbc = jax.nn.silu(xbc)
    xi, bm, cm = jnp.split(xbc, [SSD_INNER, SSD_INNER + SSD_GROUPS * SSD_STATE], axis=-1)
    f32 = jnp.float32
    dt = jax.nn.softplus(dt.astype(f32) + dt_bias.astype(f32))
    a = -jnp.exp(a_log.astype(f32))
    xi = xi.astype(f32).reshape(b, s, SSD_GROUPS, SSD_HPG, SSD_HEAD_DIM)
    y = ssd_chunked_scan(xi, dt.reshape(b, s, SSD_GROUPS, SSD_HPG), a.reshape(SSD_GROUPS, SSD_HPG),
                         bm.astype(f32).reshape(b, s, SSD_GROUPS, SSD_STATE),
                         cm.astype(f32).reshape(b, s, SSD_GROUPS, SSD_STATE))
    y = y + d_skip.astype(f32).reshape(SSD_GROUPS, SSD_HPG)[:, :, None] * xi
    y = y.reshape(b, s, SSD_INNER).astype(h.dtype) * jax.nn.silu(z)
    y = rms_norm_2(y.reshape(b, s, SSD_GROUPS, SSD_INNER // SSD_GROUPS),
                 norm_g.reshape(SSD_GROUPS, SSD_INNER // SSD_GROUPS)).reshape(b, s, SSD_INNER)
    return y @ w_o

def squared_relu_mlp(h, w_in, w_out):
    return jnp.square(jax.nn.relu(h @ w_in)) @ w_out

def second_inputs(seed: int = 0) -> dict:
    key = jax.random.key(seed)
    ks = jax.random.split(key, 24)
    nrm = jax.random.normal
    f32 = jnp.float32
    d = D_MODEL
    dt = jnp.exp(jax.random.uniform(ks[14], (N_C, SSD_HEADS), f32, np.log(1e-3), np.log(1e-1)))
    return {
        "x": nrm(ks[0], (BATCH, SEQ, d), f32),
        "norm_mix_g": 1.0 + 0.02 * nrm(ks[1], (DEPTH, d), f32),
        "norm_mlp_g": 1.0 + 0.02 * nrm(ks[2], (DEPTH, d), f32),
        "sb_w_qkv": nrm(ks[3], (N_A, d, 3 * SB_WIDTH), f32) * d ** -0.5,
        "sb_q_norm_g": 1.0 + 0.02 * nrm(ks[4], (N_A, SB_HEAD_DIM), f32),
        "sb_k_norm_g": 1.0 + 0.02 * nrm(ks[5], (N_A, SB_HEAD_DIM), f32),
        "sb_w_o": nrm(ks[6], (N_A, SB_WIDTH, d), f32) * SB_WIDTH ** -0.5,
        "gm_w_in": nrm(ks[7], (N_B, d, 2 * GM_WIDTH), f32) * d ** -0.5,
        "gm_v_norm_g": 1.0 + 0.02 * nrm(ks[8], (N_B, GM_WIDTH), f32),
        "gm_w_s": nrm(ks[9], (N_B, GM_GROUPS, GM_CHUNK, GM_CHUNK), f32) * (1.0 / GM_CHUNK),
        "gm_b_s": 1.0 + 0.02 * nrm(ks[10], (N_B, GM_GROUPS, GM_CHUNK), f32),
        "gm_w_o": nrm(ks[11], (N_B, GM_WIDTH, d), f32) * GM_WIDTH ** -0.5,
        "ssd_w_in": nrm(ks[12], (N_C, d, SSD_PROJ), f32) * d ** -0.5,
        "ssd_conv_w": nrm(ks[13], (N_C, SSD_CONV, SSD_CONV_DIM), f32) * SSD_CONV ** -0.5,
        "ssd_conv_b": 0.02 * nrm(ks[15], (N_C, SSD_CONV_DIM), f32),
        "ssd_dt_bias": dt + jnp.log(-jnp.expm1(-dt)),
        "ssd_a_log": jnp.log(jax.random.uniform(ks[16], (N_C, SSD_HEADS), f32, 1.0, 16.0)),
        "ssd_d": 1.0 + 0.02 * nrm(ks[17], (N_C, SSD_HEADS), f32),
        "ssd_norm_g": 1.0 + 0.02 * nrm(ks[18], (N_C, SSD_INNER), f32),
        "ssd_w_o": nrm(ks[19], (N_C, SSD_INNER, d), f32) * SSD_INNER ** -0.5,
        "mlp_w_in": nrm(ks[20], (DEPTH, d, MLP_HIDDEN), f32) * d ** -0.5,
        "mlp_w_out": nrm(ks[21], (DEPTH, MLP_HIDDEN, d), f32) * MLP_HIDDEN ** -0.5,
    }

def second_block(x, norm_mix_g, norm_mlp_g, sb_w_qkv, sb_q_norm_g, sb_k_norm_g, sb_w_o,
              gm_w_in, gm_v_norm_g, gm_w_s, gm_b_s, gm_w_o,
              ssd_w_in, ssd_conv_w, ssd_conv_b, ssd_dt_bias, ssd_a_log, ssd_d, ssd_norm_g, ssd_w_o,
              mlp_w_in, mlp_w_out):
    h = x
    for i in range(DEPTH):
        kind, j = i % N_MIXERS, i // N_MIXERS
        hn = rms_norm_2(h, norm_mix_g[i])
        if kind == 0:
            mix = stick_breaking_attention(hn, sb_w_qkv[j], sb_q_norm_g[j], sb_k_norm_g[j], sb_w_o[j])
        elif kind == 1:
            mix = chunked_spatial_gating(hn, gm_w_in[j], gm_v_norm_g[j], gm_w_s[j], gm_b_s[j], gm_w_o[j])
        else:
            mix = ssd_mixer(hn, ssd_w_in[j], ssd_conv_w[j], ssd_conv_b[j], ssd_dt_bias[j],
                            ssd_a_log[j], ssd_d[j], ssd_norm_g[j], ssd_w_o[j])
        h = h + mix
        h = h + squared_relu_mlp(rms_norm_2(h, norm_mlp_g[i]), mlp_w_in[i], mlp_w_out[i])
    return h


def setup_inputs(seed=0):
    out = dict(first_inputs(seed))
    for name, value in second_inputs(seed + 1).items():
        if name != "x":
            out[name + "_2"] = value
    return out


def reference(
    x, c, positions, norm1_w, w_ada, b_ada, w_in, q_norm_w, k_norm_w, attn_out_norm_w,
    hg_lb_logits, hg_norm_w, w_out, norm2_w, w_ff1, w_ff2, norm_mix_g_2, norm_mlp_g_2,
    sb_w_qkv_2, sb_q_norm_g_2, sb_k_norm_g_2, sb_w_o_2, gm_w_in_2, gm_v_norm_g_2, gm_w_s_2,
    gm_b_s_2, gm_w_o_2, ssd_w_in_2, ssd_conv_w_2, ssd_conv_b_2, ssd_dt_bias_2, ssd_a_log_2,
    ssd_d_2, ssd_norm_g_2, ssd_w_o_2, mlp_w_in_2, mlp_w_out_2,
):
    x = first_block(
        x, c, positions, norm1_w, w_ada, b_ada, w_in, q_norm_w, k_norm_w, attn_out_norm_w,
        hg_lb_logits, hg_norm_w, w_out, norm2_w, w_ff1, w_ff2,
    )
    return second_block(
        x, norm_mix_g_2, norm_mlp_g_2, sb_w_qkv_2, sb_q_norm_g_2, sb_k_norm_g_2, sb_w_o_2,
        gm_w_in_2, gm_v_norm_g_2, gm_w_s_2, gm_b_s_2, gm_w_o_2, ssd_w_in_2, ssd_conv_w_2,
        ssd_conv_b_2, ssd_dt_bias_2, ssd_a_log_2, ssd_d_2, ssd_norm_g_2, ssd_w_o_2, mlp_w_in_2,
        mlp_w_out_2,
    )


_drawn_inputs = setup_inputs


def setup_inputs(seed=0):
    import zlib

    import numpy as np

    out = dict(_drawn_inputs(seed))
    spreads = {}
    factors = {'norm1_w': 4.108,
     'q_norm_w': 8.0,
     'k_norm_w': 8.0,
     'attn_out_norm_w': 4.353,
     'hg_lb_logits': 6.899,
     'hg_norm_w': 6.569,
     'norm_mix_g_2': 4.396,
     'norm_mlp_g_2': 3.654,
     'sb_q_norm_g_2': 8.0,
     'sb_k_norm_g_2': 8.0}
    for name, (base, spread) in spreads.items():
        noise = np.random.default_rng([zlib.crc32(name.encode()), seed]).standard_normal(out[name].shape)
        drawn = base * np.exp(spread * noise) if base else spread * noise
        out[name] = __import__('jax').numpy.asarray(drawn.astype(out[name].dtype))
    for name, factor in factors.items():
        out[name] = (out[name] * factor).astype(out[name].dtype)
    return out
```

```python
from contextlib import ExitStack

import concourse.bass as bass
import numpy as np
from concourse import mybir

F32 = mybir.dt.float32
F32R = mybir.dt.float32r
I32 = mybir.dt.int32
U8 = mybir.dt.uint8
ALU = mybir.AluOpType
ACT = mybir.ActivationFunctionType
AX_X = mybir.AxisListType.X

P = 128
S, D = 256, 2048
T = S // P
KT = D // P
NC_ = 512
CH = 4
HD = 128
GH = NC_ // HD
AW = D // 2
HW = D - AW
NU = 4 * D // NC_
EPS = 1e-6
HALF = HD // 8
THETA = 500000.0
NEG = -1e30
SCALE = float(HD) ** -0.5

HG_GROUPS, AT_GROUPS, SB_GROUPS = HW // NC_, AW // NC_, D // NC_
PROJ0 = 0
OUT0 = PROJ0 + 4 * HG_GROUPS + 3 * AT_GROUPS
MLP0 = OUT0 + D // NC_
QKV0 = MLP0 + 2 * NU
WO0 = QKV0 + 3 * SB_GROUPS
MLP1 = WO0 + D // NC_
END = MLP1 + 2 * NU

RA = {"b_ada": (0, 96), "norm1": (96, 16), "norm2": (112, 16)}
RB = {"attn_out": (0, 8), "hgw": (8, 1), "lb": (9, 16), "nmix": (25, 16), "nmlp": (41, 16), "c": (57, 16)}
NRB = 73
SHIFT1, SCALE1, GATE1, SHIFT2, SCALE2, GATE2 = range(6)
LEVELS = (64, 32, 16, 8, 4, 2, 1)
NLV = 2 + len(LEVELS)


def build(nc, a, out):
    ctx = ExitStack()
    with ctx:
        def sb(name, shape, dt=F32, c=ctx):
            return c.enter_context(nc.sbuf_tensor(name, shape, dt))

        def sem(name):
            return ctx.enter_context(nc.semaphore(name))

        X = sb("X", [P, T, D])
        A_hi, A_lo = sb("A_hi", [P, KT, S], F32R), sb("A_lo", [P, KT, S], F32R)
        raw = sb("raw", [P, CH, CH, NC_])
        w_hi, w_lo = sb("w_hi", [P, CH, CH, NC_], F32R), sb("w_lo", [P, CH, CH, NC_], F32R)
        ident, ones = sb("ident", [P, P]), sb("ones", [P, P])
        neg_s = sb("neg_s", [P, P])
        below, above = sb("below", [P, P]), sb("above", [P, P])
        count, maskadd = sb("count", [P, 3 * P]), sb("maskadd", [P, 3 * P])
        lv_mask = sb("lv_mask", [P, 1 + len(LEVELS), P], U8)
        wq_b, wk_b = sb("wq_b", [P, P]), sb("wk_b", [P, P])
        colA, colB = sb("colA", [P, P]), sb("colB", [P, NRB])
        mod = sb("mod", [P, 6, KT])
        g1, g2, gmix, zero_c, one_c = (sb(n, [P, KT]) for n in ("g1", "g2", "gmix", "zero_c", "one_c"))
        sc = sb("sc", [P, KT])
        lb, lb1 = sb("lb", [P, 8]), sb("lb1", [P, 8])
        cos, sin = sb("cos", [P, T, HALF]), sb("sin", [P, T, HALF])
        rt = sb("rt", [P, 4, T * GH * HALF])
        ssq, rstd, mhalf = sb("ssq", [P, 8]), sb("rstd", [P, 8]), sb("mhalf", [P, 8])
        mx, nmx, l_, rl = sb("mx", [P, T]), sb("nmx", [P, T]), sb("l_", [P, T]), sb("rl", [P, 2, T])
        over = ExitStack()
        MIX = sb("MIX", [P, T, D], c=over)
        QN, KN, VN, GN = (sb(n, [P, T, NC_], c=over) for n in ("QN", "KN", "VN", "GN"))
        qT, bT, kT, E0 = (sb(n, [P, GH, S], c=over) for n in ("qT", "bT", "kT", "E0"))
        AM = sb("AM", [P, 3, GH, P], c=over)
        over.close()
        start = ExitStack()
        MS = sb("MS", [P, 2, D], c=start)
        ada_raw = sb("ada_raw", [P, CH, D], c=start)
        start.close()
        H_hi, H_lo = sb("H_hi", [P, 2, CH, S], F32R), sb("H_lo", [P, 2, CH, S], F32R)
        ACC = sb("ACC", [P, T, D])
        RE, SQ = sb("RE", [P, T, NC_]), sb("SQ", [P, T, NC_])
        mixf = MIX[:, :, :].rearrange("p t d -> p (t d)")
        setup = MS[:, :, :].rearrange("p a n -> p (a n)")
        E1 = MIX[:, 0, 0:D // 2].rearrange("p (h s) -> p h s", h=GH)
        QK = MIX[:, 1, 0:D // 2].rearrange("p (h s) -> p h s", h=GH)

        PS = ctx.enter_context(nc.psum_tensor("PS", [P, 8, NC_], F32))

        params_in, bcast_in, x_in = sem("params_in"), sem("bcast_in"), sem("x_in")
        sbw_in = sem("sbw_in")
        raw_in = [sem(f"raw_in{j}") for j in range(CH)]
        hi_rdy, lo_rdy, chunk_done = sem("hi_rdy"), sem("lo_rdy"), sem("chunk_done")
        pool_const, dve_const, act_const, pe_const = (sem(n) for n in ("pool_const", "dve_const", "act_const", "pe_const"))
        ada_in = [sem(f"ada_in{j}") for j in range(CH)]
        ada_used, ada_sum, arg_rdy = sem("ada_used"), sem("ada_sum"), sem("arg_rdy")
        sum_rdy, rstd_rdy = sem("sum_rdy"), sem("rstd_rdy")
        y_rdy_v = sem("y_rdy_v")
        a_tr, a_aff, a_hi, a_lo = sem("a_tr"), sem("a_aff"), sem("a_hi"), sem("a_lo")
        pair_read = [sem(f"pair_read{i}") for i in range(3)]
        gate_diag, gate_mm, gate_rdy = sem("gate_diag"), sem("gate_mm"), sem("gate_rdy")
        x_final = sem("x_final")
        relu_rdy, sq_rdy, h_tr, h_hi, h_lo, acc_read = (sem(n) for n in ("relu_rdy", "sq_rdy", "h_tr", "h_hi", "h_lo", "acc_read"))
        q_sig, f_rdy, f_log, g_sig = (sem(n) for n in ("q_sig", "f_rdy", "f_log", "g_sig"))
        hg_tr, diff_rdy, exp_rdy, lv_rdy, lv_mm, lv_cp = (sem(n) for n in ("hg_tr", "diff_rdy", "exp_rdy", "lv_rdy", "lv_mm", "lv_cp"))
        o_mm, o_sq, o_out = sem("o_mm"), sem("o_sq"), sem("o_out")
        sq_act, n_rdy, n_tr = sem("sq_act"), sem("n_rdy"), sem("n_tr")
        s_mm, s_max, p_exp, p_rdy, pT_mm, pT_rdy, pv_mm, pv_out = (
            sem(n) for n in ("s_mm", "s_max", "p_exp", "p_rdy", "pT_mm", "pT_rdy", "pv_mm", "pv_out"))
        stored = sem("stored")

        pairs = (0, 2, 4)

        def bank(i, lo=0, hi=NC_):
            return PS[:, i, lo:hi]

        def heads_t(tile, i):
            return tile[:, 2 * i:2 * i + 2, :].rearrange("p h s -> p (h s)")

        def split_hi(act, B, j):
            act.wait_ge(raw_in[j], 16 * (B + 1))
            if not isinstance(B, int) or B >= 1:
                act.wait_ge(chunk_done, 4 * (B - 1) + j + 1)
            act.activation(w_hi[:, j, :, :], raw[:, j, :, :], ACT.Copy).then_inc(hi_rdy, 1)

        def split_lo(dve, B, j):
            dve.wait_ge(hi_rdy, 4 * B + j + 1)
            dve.tensor_tensor(w_lo[:, j, :, :], raw[:, j, :, :], w_hi[:, j, :, :].bitcast(F32),
                              ALU.subtract).then_inc(lo_rdy, 1)

        def chunk(pe, B, j, pair, hi, lo, start, stop):
            pe.wait_ge(lo_rdy, 4 * B + j + 1)
            for t in range(T):
                for k in range(CH):
                    h, l = hi(k, t), lo(k, t)
                    first, last = start and k == 0, stop and k == CH - 1
                    pe.matmul(bank(pair + t), h, w_hi[:, j, k, :], start=first, stop=False)
                    pe.matmul(bank(pair + t), h, w_lo[:, j, k, :], start=False, stop=False)
                    mm = pe.matmul(bank(pair + t), l, w_hi[:, j, k, :], start=False, stop=last)
            mm.then_inc(chunk_done, 1)

        def a_chunk(pe, B, j, pair):
            chunk(pe, B, j, pair, lambda k, t: A_hi[:, CH * j + k, P * t:P * t + P],
                  lambda k, t: A_lo[:, CH * j + k, P * t:P * t + P], j == 0, j == CH - 1)

        def turn_pe(pe, n, src):
            for i in range(KT // 2):
                if i >= 2:
                    pe.wait_ge(a_aff, KT // 2 * n + i - 1)
                for q in range(4):
                    kt, t = 2 * i + q // 2, q % 2
                    mm = pe.transpose(bank(6 + i % 2, P * q, P * q + P), src[:, t, kt * P:kt * P + P], ident[:, :])
                mm.then_inc(a_tr, 1)

        def turn_act(act, n, tmp):
            for i in range(KT // 2):
                act.wait_ge(a_aff, KT // 2 * n + i + 1)
                act.activation(A_hi[:, 2 * i:2 * i + 2, :].rearrange("p k s -> p (k s)"), tmp[:, i % 2, :],
                               ACT.Copy).then_inc(a_hi, 1)

        def turn_dve(dve, n, g, s, tmp):
            for i in range(KT // 2 + 1):
                if i < KT // 2:
                    dve.wait_ge(a_tr, KT // 2 * n + i + 1)
                    if i >= 2:
                        dve.wait_ge(a_lo, KT // 2 * n + i - 1)
                    for k in range(2):
                        kt = 2 * i + k
                        ins = dve.tensor_scalar(tmp[:, i % 2, S * k:S * k + S], bank(6 + i % 2, S * k, S * k + S),
                                                g[:, kt:kt + 1], s[:, kt:kt + 1], ALU.mult, ALU.add)
                    ins.then_inc(a_aff, 1)
                if i:
                    dve.wait_ge(a_hi, KT // 2 * n + i)
                    flat = "p k s -> p (k s)"
                    dve.tensor_tensor(A_lo[:, 2 * i - 2:2 * i, :].rearrange(flat), tmp[:, (i - 1) % 2, :],
                                      A_hi[:, 2 * i - 2:2 * i, :].rearrange(flat).bitcast(F32),
                                      ALU.subtract).then_inc(a_lo, 1)

        class Jobs:
            def __init__(self):
                self.base, self.n = 0, 0

        jobs = Jobs()

        def rsqrt(dve, w, mul, add):
            dve.drain()
            dve.tensor_scalar(ssq[:, 0:w], ssq[:, 0:w], mul, add, ALU.mult, ALU.add).then_inc(sum_rdy, 1)
            jobs.n += 1
            dve.wait_ge(rstd_rdy, jobs.base + jobs.n)

        block = ctx.enter_context(nc.Block())

        @block.sync
        def _(sp):
            pa, pb = setup[:, 0:P], setup[:, P:2 * P]
            rows = [(pa, RA["b_ada"], a["b_ada"]), (pa, RA["norm1"], a["norm1_w"]), (pa, RA["norm2"], a["norm2_w"]),
                    (pb, RB["attn_out"], a["attn_out_norm_w"]), (pb, RB["hgw"], a["hg_norm_w"]),
                    (pb, RB["lb"], a["hg_lb_logits"]), (pb, RB["nmix"], a["norm_mix_g_2"]),
                    (pb, RB["nmlp"], a["norm_mlp_g_2"]), (pb, RB["c"], a["c"])]
            for tile, (r0, n), src in rows:
                sp.dma_start(tile[r0:r0 + n, :], src.rearrange("a (r p) -> (a r) p", p=P)).then_inc(params_in, 16)
            for t in range(T):
                sp.dma_start(rt[:, 0, t:t + 1].bitcast(I32),
                             a["positions"][0:1, P * t:P * t + P].rearrange("a (p b) -> (a p) b", b=1)).then_inc(params_in, 16)
            sp.dma_start(wq_b[:, :], a["q_norm_w"].to_broadcast([P, P])).then_inc(bcast_in, 16)
            sp.dma_start(wk_b[:, :], a["k_norm_w"].to_broadcast([P, P])).then_inc(bcast_in, 16)
            sp.dma_start(X[:, :, :], a["x"].rearrange("a (t p) d -> p (a t) d", p=P)).then_inc(x_in, 16)
            ada = a["w_ada"].rearrange("a (k p) (s n) -> p (a k) s n", p=P, n=D)
            with sp.Fori(0, 6) as i:
                for k in range(KT):
                    sp.wait_ge(ada_used, KT * i + k + 1)
                    sp.dma_start(ada_raw[:, k % CH, :], ada[:, k, i, :]).then_inc(ada_in[k % CH], 16)

            def load(B, j, src):
                if not isinstance(B, int) or B >= 1:
                    sp.wait_ge(lo_rdy, 4 * (B - 1) + j + 1)
                sp.dma_start(raw[:, j, :, :], src).then_inc(raw_in[j], 16)

            w_in = a["w_in"].rearrange("a (j k p) n -> p (a j) k n", j=CH, p=P)
            for B, c0 in enumerate(proj_columns()):
                for j in range(CH):
                    load(B, j, w_in[:, j, :, c0:c0 + NC_])

            def square(B0, w):
                v = w.rearrange("a (j k p) (b n) -> p (a j) k b n", j=CH, p=P, n=NC_)
                with sp.Fori(0, D // NC_) as b:
                    for j in range(CH):
                        load(B0 + b, j, v[:, j, :, b, :])

            def mlp(M, w1, w2):
                v1 = w1.rearrange("a (j k p) (u n) -> p (a j) k u n", j=CH, p=P, n=NC_)
                v2 = w2.rearrange("a (u k p) (j n) -> p (a u) k j n", k=CH, p=P, n=NC_)

                def up(B, u):
                    for j in range(CH):
                        load(B, j, v1[:, j, :, u, :])

                def down(B, u):
                    for j in range(CH):
                        load(B, j, v2[:, u, :, j, :])

                up(M, 0)
                with sp.Fori(0, NU - 1) as u:
                    up(M + 1 + 2 * u, u + 1)
                    down(M + 2 + 2 * u, u)
                down(M + 2 * NU - 1, NU - 1)

            square(OUT0, a["w_out"])
            mlp(MLP0, a["w_ff1"], a["w_ff2"])
            qkv = a["sb_w_qkv_2"].rearrange("a (j k p) (s g n) -> p (a j) k s g n", j=CH, p=P, s=3, n=NC_)
            sp.dma_start(wq_b[:, :], a["sb_q_norm_g_2"].to_broadcast([P, P])).then_inc(sbw_in, 16)
            sp.dma_start(wk_b[:, :], a["sb_k_norm_g_2"].to_broadcast([P, P])).then_inc(sbw_in, 16)
            with sp.Fori(0, SB_GROUPS) as g:
                for s_ in range(3):
                    for j in range(CH):
                        load(QKV0 + 3 * g + s_, j, qkv[:, j, :, s_, g, :])
            square(WO0, a["sb_w_o_2"])
            mlp(MLP1, a["mlp_w_in_2"], a["mlp_w_out_2"])
            for t in range(T):
                sp.wait_ge(x_final, t + 1)
                sp.dma_start(out[0, P * t:P * t + P, :], X[:, t, :]).then_inc(stored, 16)
            sp.wait_ge(stored, 16 * T)

        ints = setup[:, 256:1024].bitcast(I32)
        dist, tmp_i = ints[:, 0:384], ints[:, 384:768]
        rows_i, cols_i, xor_i = (setup[:, c:c + P].bitcast(I32) for c in (1024, 1152, 1280))
        f_a, f_b = setup[:, 1408:1792], setup[:, 1792:2176]
        invf = setup[:, 2176:2176 + HALF]
        pos_i = rt[:, 0, 0:T].bitcast(I32)
        ang = setup[:, 2304:2304 + T * HALF].rearrange("p (t f) -> p t f", t=T)
        kk = setup[:, 2432:2432 + T * HALF].rearrange("p (t f) -> p t f", t=T)
        posf, lbt = setup[:, 2500:2502], setup[:, 2560:2584]

        N_CONST = 15
        JOBS = 1 + HG_GROUPS + 2 * AT_GROUPS + 1 + 1 + 1 + 2 * SB_GROUPS + 1

        @block.gpsimd
        def _(pool):
            def const(ins):
                ins.then_inc(pool_const, 1)

            const(pool.memset(ident[:, :], 0.0))
            const(pool.memset(ones[:, :], 1.0))
            const(pool.memset(below[:, :], 1.0))
            const(pool.memset(above[:, :], 1.0))
            const(pool.memset(mhalf[:, :], -0.5))
            const(pool.memset(zero_c[:, :], 0.0))
            const(pool.memset(one_c[:, :], 1.0))
            for f in range(HALF):
                ins = pool.memset(invf[:, f:f + 1], float(np.float32(THETA ** (-2.0 * f / (2 * HALF)))))
            const(ins)
            pool.wait_ge(pool_const, 8)
            const(pool.affine_select(out=ident[:, :], in_=ident[:, :], compare_op=ALU.not_equal, fill=1.0,
                                     base=0, pattern=[[-1, P]], channel_multiplier=1))
            const(pool.affine_select(out=below[:, :], in_=below[:, :], compare_op=ALU.is_gt, fill=0.0,
                                     base=0, pattern=[[-1, P]], channel_multiplier=1))
            const(pool.affine_select(out=above[:, :], in_=above[:, :], compare_op=ALU.is_gt, fill=0.0,
                                     base=0, pattern=[[1, P]], channel_multiplier=-1))
            const(pool.iota(dist[:, 0:P], pattern=[[-1, P]], base=S, channel_multiplier=1))
            const(pool.iota(dist[:, P:3 * P], pattern=[[-1, 2 * P]], base=S + P, channel_multiplier=1))
            const(pool.iota(rows_i, pattern=[[0, P]], base=0, channel_multiplier=1))
            const(pool.iota(cols_i, pattern=[[1, P]], base=0, channel_multiplier=0))
            with pool.Fori(0, JOBS) as i:
                pool.wait_ge(sum_rdy, i + 1)
                pool.tensor_tensor(rstd[:, :], ssq[:, :], mhalf[:, :], ALU.pow).then_inc(rstd_rdy, 1)

        @block.scalar
        def _(act):
            act.wait_ge(dve_const, 1)
            act.activation(sc[:, :], colB[:, RB["c"][0]:NRB], ACT.Sigmoid).then_inc(act_const, 1)
            act.wait_ge(dve_const, 2)
            act.activation(lbt[:, 0:16], lbt[:, 0:16], ACT.Exp).then_inc(act_const, 1)
            act.wait_ge(dve_const, 3)
            act.activation(sin[:, :, :], ang, ACT.Sin).then_inc(act_const, 1)
            act.activation(cos[:, :, :], ang, ACT.Sin, scale=0.5).then_inc(act_const, 1)

            def hg_own(g, B0, s):
                if s == 4:
                    act.wait_ge(chunk_done, 4 * (B0 + 1))
                    act.activation(KN[:, :, :], PS[:, 0:2, :], ACT.Sigmoid).then_inc(q_sig, 1)
                if s == 8:
                    act.wait_ge(chunk_done, 4 * (B0 + 2))
                    act.wait_ge(pair_read[0], 3 * g + 1)
                    act.activation(KN[:, :, :], PS[:, 2:4, :], ACT.Sigmoid).then_inc(pair_read[1], 1)
                if s == 11:
                    act.wait_ge(hg_tr, 2 * g + 1)
                    if g:
                        act.wait_ge(lv_rdy, 8 * g)
                    for i in range(2):
                        c = act.activation(heads_t(qT, i), bank(2 + i), ACT.Copy)
                    c.then_inc(pair_read[1], 1)
                if s == 12:
                    act.wait_ge(chunk_done, 4 * (B0 + 3))
                    if g:
                        act.wait_ge(o_mm, g)
                    act.activation(VN[:, :, :], PS[:, 0:2, :], ACT.Copy).then_inc(pair_read[0], 1)
                if s == 15:
                    act.wait_ge(f_rdy, g + 1)
                    act.activation(E0[:, :, :], E0[:, :, :], ACT.Ln).then_inc(f_log, 1)

            def hg_stage(g, B0, s):
                if s == 0:
                    act.wait_ge(chunk_done, 4 * (B0 + 4))
                    if g:
                        act.wait_ge(o_out, g)
                    act.activation(GN[:, :, :], PS[:, 2:4, :], ACT.Sigmoid).then_inc(g_sig, 1)
                if 1 <= s < NLV:
                    E = (E0, E1)[s % 2]
                    act.wait_ge(diff_rdy, 8 * g + s)
                    act.activation(E[:, :, :], E[:, :, :], ACT.Exp).then_inc(exp_rdy, 1)
                if s == 11:
                    act.wait_ge(o_mm, g + 1)
                    act.activation(E1.rearrange("p h s -> p (h s)"), PS[:, 6:8, :], ACT.Square).then_inc(o_sq, 1)

            def at_own(n, B0, s):
                if s == 4:
                    act.wait_ge(chunk_done, 4 * (B0 + 1))
                    act.activation(QN[:, :, :], PS[:, 0:2, :], ACT.Square).then_inc(sq_act, 1)
                if s == 8:
                    act.wait_ge(chunk_done, 4 * (B0 + 2))
                    act.activation(KN[:, :, :], PS[:, 2:4, :], ACT.Square).then_inc(sq_act, 1)
                if s == 10:
                    act.wait_ge(n_tr, 2 * n + 1)
                    if isinstance(n, int) and n == 0:
                        act.wait_ge(lv_rdy, 8 * HG_GROUPS)
                    else:
                        act.wait_ge(s_mm, 4 * n)
                    for i in range(2):
                        c = act.activation(heads_t(qT, i), bank(i), ACT.Copy)
                    c.then_inc(pair_read[0], 1)
                if s == 11:
                    act.wait_ge(n_tr, 2 * n + 2)
                    for i in range(2):
                        c = act.activation(heads_t(kT, i), bank(2 + i), ACT.Copy)
                    c.then_inc(pair_read[1], 1)

            E0f = E0[:, :, :].rearrange("p h s -> p (h s)")
            AMf = AM[:, :, :, :].rearrange("p r h s -> p (r h s)")

            def at_stage(n, B0, s, stick):
                if s == 0:
                    act.wait_ge(chunk_done, 4 * (B0 + 3))
                    if isinstance(n, int) and n == 0:
                        act.wait_ge(o_mm, HG_GROUPS)
                    else:
                        act.wait_ge(pv_mm, 4 * n)
                    act.activation(VN[:, :, :], PS[:, 4:6, :], ACT.Copy).then_inc(pair_read[2], 1)
                if s >= 2 and s % 2 == 0 and s <= 2 * GH:
                    h = s // 2 - 1
                    if stick:
                        act.wait_ge(s_mm, 4 * n + h + 1)
                        act.activation(E0f[:, 0:384], bank(6, 0, 384), ACT.Abs)
                        act.drain()
                        act.activation(E0f[:, 0:384], E0f[:, 0:384], ACT.Exp, scale=-1.0)
                        act.drain()
                        act.activation(E0f[:, 0:384], E0f[:, 0:384], ACT.Ln, bias=one_c[:, 0:1]).then_inc(p_exp, 1)
                    else:
                        act.wait_ge(s_max, 4 * n + h + 1)
                        act.wait_ge(pT_mm, 4 * n + h)
                        act.activation(E0f[:, 384:512], E0f[:, 0:128], ACT.Exp, bias=nmx[:, 0:1])
                        act.activation(E0f[:, 512:768], E0f[:, 128:384], ACT.Exp, bias=nmx[:, 1:2]).then_inc(p_exp, 1)
                if s >= 3 and s % 2 == 1 and s <= 2 * GH + 1:
                    h = (s - 3) // 2
                    if stick:
                        act.wait_ge(arg_rdy, 4 * (n - AT_GROUPS) + h + 1)
                        act.activation(AMf[:, 0:384], AMf[:, 0:384], ACT.Exp).then_inc(pT_rdy, 1)
                    else:
                        act.wait_ge(pT_mm, 4 * n + h + 1)
                        act.activation(AMf[:, 0:384], bank(7, 0, 384), ACT.Copy).then_inc(pT_rdy, 1)

            turn_act(act, 0, GN)
            for j in range(CH):
                split_hi(act, 0, j)
            groups = proj_groups()
            for i, (kind, idx, B0, nb) in enumerate(groups + [(None, 0, OUT0, 3)]):
                for s in range(CH * nb):
                    if i:
                        pk, pi, pB, _ = groups[i - 1]
                        hg_stage(pi, pB, s) if pk == "hg" else at_stage(pi, pB, s, False)
                    if kind:
                        (hg_own if kind == "hg" else at_own)(idx, B0, s)
                        if B0 + s // CH + 1 < OUT0:
                            split_hi(act, B0 + s // CH + 1, s % CH)

            def gate(n, b, dst):
                act.wait_ge(gate_mm, n + 1)
                act.activation(dst, bank(6 + b % 2), ACT.Copy).then_inc(gate_rdy, 1)

            turn_act(act, 1, GN)
            for b in range(4):
                gate(b, b, (QN, KN)[b // 2][:, b % 2, :])
            for j in range(CH):
                split_hi(act, OUT0, j)
            with act.Fori(1, 4) as b:
                for j in range(CH):
                    split_hi(act, OUT0 + b, j)

            def mlp(m, M, last):
                def up(B, U):
                    for j in range(CH):
                        split_hi(act, B + 1, j)
                    act.wait_ge(chunk_done, 4 * (B + 1))
                    if not isinstance(U, int) or U:
                        act.wait_ge(sq_rdy, U)
                    act.activation(RE[:, :, :], PS[:, 0:2, :], ACT.Relu).then_inc(relu_rdy, 1)

                def turn(U, par):
                    act.wait_ge(h_tr, U + 1)
                    act.activation(H_hi[:, par, :, :].rearrange("p k s -> p (k s)"), PS[:, 6:8, :],
                                   ACT.Copy).then_inc(h_hi, 1)

                def down(B, U, par, end=False):
                    for j in range(CH):
                        if not end:
                            split_hi(act, B + 1, j)
                        if j == 1 and par is not None:
                            turn(U + 1, par)

                for j in range(CH):
                    split_hi(act, M, j)
                up(M, NU * m)
                turn(NU * m, 0)
                with act.Fori(0, NU // 2 - 1) as i:
                    for e in range(2):
                        up(M + 1 + 4 * i + 2 * e, NU * m + 1 + 2 * i + e)
                        down(M + 2 + 4 * i + 2 * e, NU * m + 2 * i + e, (e + 1) % 2)
                up(M + 2 * NU - 3, NU * m + NU - 1)
                down(M + 2 * NU - 2, NU * m + NU - 2, (NU - 1) % 2)

            turn_act(act, 2, SQ)
            mlp(0, MLP0, False)
            for b in range(4):
                gate(4 + b, b, SQ[:, b % 2, :])
            turn_act(act, 3, GN)
            for j in range(CH):
                split_hi(act, QKV0, j)

            def sb_group(g, first, last):
                B0 = QKV0 + 3 * g
                for s in range(12):
                    if not first:
                        at_stage(AT_GROUPS + g - 1, B0 - 3, s, True)
                    if not last:
                        at_own(AT_GROUPS + g, B0, s)
                        split_hi(act, B0 + s // CH + 1, s % CH)

            sb_group(0, True, False)
            with act.Fori(1, SB_GROUPS - 1) as g:
                sb_group(g, False, False)
            for s in range(12):
                at_stage(AT_GROUPS + SB_GROUPS - 2, QKV0 + 3 * (SB_GROUPS - 2), s, True)
                at_own(AT_GROUPS + SB_GROUPS - 1, QKV0 + 3 * (SB_GROUPS - 1), s)
                if s < 8:
                    split_hi(act, QKV0 + 3 * (SB_GROUPS - 1) + s // CH + 1, s % CH)
            for s in range(12):
                at_stage(AT_GROUPS + SB_GROUPS - 1, QKV0 + 3 * (SB_GROUPS - 1), s, True)
            turn_act(act, 4, GN)
            with act.Fori(0, 4) as b:
                for j in range(CH):
                    split_hi(act, WO0 + b, j)
            turn_act(act, 5, SQ)
            mlp(1, MLP1, True)

        @block.vector
        def _(dve):
            d = dve.drain
            for i in range(CH):
                dve.memset(ssq[:, 2 * i:2 * i + 2], 1.0).then_inc(ada_used, 1)
            dve.wait_ge(pool_const, N_CONST)
            dve.wait_ge(pe_const, 1)
            dve.tensor_copy(colA[:, :], bank(6, 0, P))
            dve.tensor_copy(colB[:, :], bank(6, P, P + NRB)).then_inc(dve_const, 1)
            d()
            l0 = RB["lb"][0]
            dve.tensor_tensor(lbt[:, 16:24], colB[:, l0:l0 + 8], colB[:, l0 + 8:l0 + 16], ALU.max)
            d()
            dve.tensor_tensor(lbt[:, 0:8], colB[:, l0:l0 + 8], lbt[:, 16:24], ALU.subtract)
            dve.tensor_tensor(lbt[:, 8:16], colB[:, l0 + 8:l0 + 16], lbt[:, 16:24], ALU.subtract).then_inc(dve_const, 1)
            dve.wait_ge(params_in, 16 * 11)
            dve.tensor_copy(posf, pos_i)
            d()
            for t in range(T):
                dve.tensor_scalar(ang[:, t, :], invf, posf[:, t:t + 1], None, ALU.mult)
            d()
            ROUND = 12582912.0
            dve.tensor_scalar(kk, ang, float(1 / (2 * np.pi)), ROUND, ALU.mult, ALU.add)
            d()
            dve.tensor_scalar(kk, kk, ROUND, None, ALU.subtract)
            d()
            c1 = 6.28125
            c2 = float(np.float32(np.round((2 * np.pi - c1) * 2 ** 21) / 2 ** 21))
            for c in (c1, c2, float(2 * np.pi - c1 - c2)):
                dve.scalar_tensor_tensor(out=ang, in0=kk, scalar=-c, in1=ang, op0=ALU.mult, op1=ALU.add)
                d()
            dve.tensor_scalar(ang, ang, 3.1415925, -3.1415925, ALU.min, ALU.max).then_inc(dve_const, 1)
            for mask, dst in ((3, f_a), (15, f_b)):
                dve.tensor_scalar(tmp_i, dist, mask, None, ALU.bitwise_and)
                d()
                dve.tensor_scalar(dst, tmp_i, 0.0, None, ALU.is_equal)
                d()
            dve.scalar_tensor_tensor(out=f_a, in0=dist, scalar=float(S + P), in1=f_a, op0=ALU.is_le, op1=ALU.add)
            d()
            dve.tensor_tensor(f_a, f_a, f_b, ALU.add)
            d()
            dve.scalar_tensor_tensor(out=count[:, :], in0=dist, scalar=float(S), in1=f_a, op0=ALU.is_ge, op1=ALU.mult)
            d()
            dve.tensor_scalar(maskadd[:, :], count[:, :], 0.5, None, ALU.is_gt)
            d()
            dve.tensor_scalar(maskadd[:, :], maskadd[:, :], -NEG, NEG, ALU.mult, ALU.add)
            dve.tensor_scalar(neg_s[:, :], above[:, :], -NEG, NEG, ALU.mult, ALU.add)
            dve.tensor_tensor(xor_i, rows_i, cols_i, ALU.bitwise_xor)
            d()
            dve.scalar_tensor_tensor(out=f_a[:, 0:P], in0=xor_i, scalar=1.0, in1=above[:, :], op0=ALU.add, op1=ALU.mult)
            dve.tensor_copy(lv_mask[:, 0, :], ident[:, :])
            d()
            for i, w in enumerate(LEVELS):
                dve.tensor_scalar(f_b[:, 0:P], f_a[:, 0:P], w + 1.0, None, ALU.is_ge)
                d()
                dve.scalar_tensor_tensor(out=lv_mask[:, 1 + i, :], in0=f_a[:, 0:P], scalar=2 * w + 1.0,
                                         in1=f_b[:, 0:P], op0=ALU.is_lt, op1=ALU.mult)
                d()
            dve.wait_ge(act_const, 4)
            dve.tensor_tensor(sc[:, :], sc[:, :], colB[:, RB["c"][0]:NRB], ALU.mult)
            dve.tensor_tensor(lbt[:, 16:24], lbt[:, 0:8], lbt[:, 8:16], ALU.add)
            dve.tensor_copy(gmix[:, 0:8], colB[:, 0:8])
            dve.tensor_scalar(gmix[:, 8:16], one_c[:, 0:8], colB[:, 8:9], None, ALU.mult)
            dve.tensor_tensor(cos[:, :, :], cos[:, :, :], cos[:, :, :], ALU.mult)
            d()
            dve.reciprocal(lbt[:, 16:24], lbt[:, 16:24])
            dve.tensor_scalar(cos[:, :, :], cos[:, :, :], -2.0, 1.0, ALU.mult, ALU.add)
            d()
            dve.tensor_tensor(lb[:, :], lbt[:, 0:8], lbt[:, 16:24], ALU.mult)
            dve.tensor_tensor(lb1[:, :], lbt[:, 8:16], lbt[:, 16:24], ALU.mult)
            d()
            with dve.Fori(0, 3) as i:
                for h in range(2):
                    dve.wait_ge(ada_sum, 2 * i + h)
                    for k in range(KT):
                        sl = ada_raw[:, k % CH, :]
                        dve.wait_ge(ada_in[k % CH], 16 * ((2 * i + h) * (KT // CH) + k // CH + 1))
                        if k == 0:
                            ins = dve.tensor_scalar(MS[:, h, :], sl, sc[:, k:k + 1], None, ALU.mult)
                        else:
                            ins = dve.scalar_tensor_tensor(out=MS[:, h, :], in0=sl, scalar=sc[:, k:k + 1],
                                                           in1=MS[:, h, :], op0=ALU.mult, op1=ALU.add)
                        ins.then_inc(ada_used, 1)
                        dve.wait_ge(ada_used, CH + KT * (2 * i + h) + k + 1)
            dve.wait_ge(ada_sum, 7)
            dve.tensor_tensor(mod[:, :, :].rearrange("p s k -> p (s k)"), bank(6, 0, 6 * KT),
                              colA[:, 0:6 * KT], ALU.add)
            d()
            for g_, sec, nm in ((g1, SCALE1, "norm1"), (g2, SCALE2, "norm2")):
                r0 = RA[nm][0]
                dve.scalar_tensor_tensor(out=g_[:, :], in0=mod[:, sec, :], scalar=1.0, in1=colA[:, r0:r0 + KT],
                                         op0=ALU.add, op1=ALU.mult)

            def rows_norm(Y):
                for t in range(T):
                    dve.tensor_tensor_reduce(Y[:, t, :], X[:, t, :], X[:, t, :], 1.0, 0.0, ALU.mult, ALU.add,
                                             ssq[:, t:t + 1])
                rsqrt(dve, T, 1.0 / D, EPS)
                for t in range(T):
                    ins = dve.tensor_scalar(Y[:, t, :], X[:, t, :], rstd[:, t:t + 1], None, ALU.mult)
                ins.then_inc(y_rdy_v, 1)

            def wide(tile):
                return tile.rearrange("p t (h d) -> p (t h) d", d=HD)

            def hg_own(g, B0, s):
                if s == 5:
                    dve.wait_ge(q_sig, g + 1)
                    dve.scalar_tensor_tensor(out=QN[:, :, :], in0=PS[:, 0:2, :], scalar=SCALE, in1=KN[:, :, :],
                                             op0=ALU.mult, op1=ALU.mult).then_inc(pair_read[0], 1)
                if s == 14:
                    dve.wait_ge(hg_tr, 2 * g + 2)
                    for h in range(GH):
                        hh = GH * g + h
                        ins = dve.tensor_scalar(E0[:, h, :], bank(h // 2, S * (h % 2), S * (h % 2) + S),
                                                lb1[:, hh:hh + 1], lb[:, hh:hh + 1], ALU.mult, ALU.add)
                    ins.then_inc(pair_read[0], 1)
                    d()
                    dve.tensor_scalar(kT[:, :, :], E0[:, :, :], -1.0, 1.0, ALU.mult, ALU.add).then_inc(f_rdy, 1)

            def hg_stage(g, B0, s):
                if s == 0:
                    dve.wait_ge(f_log, g + 1)
                    dve.memset(AM[:, 0:2, :, :], 0.0)
                    for h in range(GH):
                        for t in range(T):
                            dve.tensor_tensor_scan(bT[:, h, P * t:P * t + P], ones[:, :], E0[:, h, P * t:P * t + P],
                                                   0.0, ALU.mult, ALU.add)
                    d()
                if s == 1:
                    dve.wait_ge(g_sig, g + 1)
                    dve.tensor_tensor(GN[:, :, :], PS[:, 2:4, :], GN[:, :, :], ALU.mult).then_inc(pair_read[1], 1)
                d()
                bf = bT[:, :, :].rearrange("p h s -> p (h s)")
                Ef = [e.rearrange("p h s -> p (h s)") for e in (E0[:, :, :], E1)]

                def halves(flat, l):
                    w = P if l == 1 else LEVELS[l - 2]
                    v = flat.rearrange("p (n two w) -> p n two w", two=2, w=w)
                    return v[:, :, 0, :], v[:, :, 1, :], w

                if 1 <= s < NLV:
                    lo_b, hi_b, w = halves(bf, s)
                    lo_e, hi_e, _ = halves(Ef[s % 2], s)
                    mid = lo_b[:, :, w - 1:w].to_broadcast(list(lo_b.shape))
                    dve.tensor_tensor(lo_e, mid, lo_b, ALU.subtract)
                    if s == 1:
                        dve.tensor_copy(hi_e, hi_b).then_inc(diff_rdy, 1)
                    else:
                        dve.tensor_tensor(hi_e, hi_b, mid, ALU.subtract).then_inc(diff_rdy, 1)
                if 1 <= s - 1 < NLV:
                    l = s - 1
                    dve.wait_ge(exp_rdy, 8 * g + l)
                    dve.wait_ge(lv_mm, NLV * g + l)
                    lo_e, hi_e, _ = halves(Ef[l % 2], l)
                    lo_k, _, _ = halves(kT[:, :, :].rearrange("p h s -> p (h s)"), l)
                    _, hi_q, _ = halves(qT[:, :, :].rearrange("p h s -> p (h s)"), l)
                    lo_o, hi_o, _ = halves(QK.rearrange("p h s -> p (h s)"), l)
                    dve.tensor_tensor(lo_o, lo_k, lo_e, ALU.mult)
                    dve.tensor_tensor(hi_o, hi_q, hi_e, ALU.mult).then_inc(lv_rdy, 1)
                if 0 <= s - 2 < NLV:
                    l = s - 2
                    dve.wait_ge(lv_mm, NLV * g + l + 1)
                    b = level_bank(l)
                    if l == 1:
                        dve.tensor_copy(AM[:, 2, :, :].rearrange("p h s -> p (h s)"), bank(b)).then_inc(lv_cp, 1)
                    else:
                        src = PS[:, b:b + 2, :].rearrange("p b (h s) -> p (b h) s", s=P)
                        m = lv_mask[:, 0 if l == 0 else l - 1, :].unsqueeze(1).to_broadcast([P, 2 * GH, P])
                        dve.copy_predicated(AM[:, 0:2, :, :].rearrange("p r h s -> p (r h) s"), m,
                                            src).then_inc(lv_cp, 1)
                        d()
                if s == 11:
                    dve.wait_ge(o_sq, g + 1)
                    e1w = E1.rearrange("p h s -> p (h s)").rearrange("p (n d) -> p n d", d=HD)
                    dve.tensor_reduce(ssq[:, 0:8], e1w, AX_X, ALU.add)
                    rsqrt(dve, 8, 1.0 / HD, EPS)
                    dve.tensor_tensor(e1w, wide(PS[:, 6:8, :]), rstd[:, 0:8].unsqueeze(2).to_broadcast([P, 8, HD]), ALU.mult)
                    d()
                    dve.tensor_tensor(MIX[:, :, AW + NC_ * g:AW + NC_ * (g + 1)],
                                      E1.rearrange("p h s -> p (h s)").rearrange("p (t n) -> p t n", t=T),
                                      GN[:, :, :], ALU.mult).then_inc(o_out, 1)

            def head_norm(n, which, tile, b, w, scale2, rope):
                dve.wait_ge(sq_act, 2 * n + which + 1)
                dve.tensor_reduce(ssq[:, 0:8], wide(tile[:, :, :]), AX_X, ALU.add)
                rsqrt(dve, 8, scale2 / HD, scale2 * EPS)
                dve.tensor_tensor(wide(tile[:, :, :]), wide(PS[:, b:b + 2, :]),
                                  rstd[:, 0:8].unsqueeze(2).to_broadcast([P, 8, HD]), ALU.mult)
                d()
                ins = dve.tensor_tensor(wide(tile[:, :, :]), wide(tile[:, :, :]),
                                        w[:, :].unsqueeze(1).to_broadcast([P, 8, HD]), ALU.mult)
                if rope:
                    d()
                    for t in range(T):
                        v = tile[:, t, :].rearrange("p (h d) -> p h d", d=HD)
                        x1, x2 = v[:, :, 0:HALF], v[:, :, HALF:2 * HALF]
                        c, s_ = (z[:, t, :].unsqueeze(1).to_broadcast([P, GH, HALF]) for z in (cos, sin))
                        r = [rt[:, i, GH * HALF * t:GH * HALF * (t + 1)].rearrange("p (h f) -> p h f", f=HALF) for i in range(4)]
                        for i, (x, y) in enumerate(((x1, c), (x2, s_), (x2, c), (x1, s_))):
                            dve.tensor_tensor(r[i], x, y, ALU.mult)
                    d()
                    for t in range(T):
                        v = tile[:, t, :].rearrange("p (h d) -> p h d", d=HD)
                        r = [rt[:, i, GH * HALF * t:GH * HALF * (t + 1)].rearrange("p (h f) -> p h f", f=HALF) for i in range(4)]
                        dve.tensor_tensor(v[:, :, 0:HALF], r[0], r[1], ALU.subtract)
                        ins = dve.tensor_tensor(v[:, :, HALF:2 * HALF], r[2], r[3], ALU.add)
                ins.then_inc(n_rdy, 1)

            def at_own(n, B0, s, rope):
                if s == 4:
                    head_norm(n, 0, QN, 0, wq_b, 1.0 / SCALE ** 2, rope)
                if s == 8:
                    head_norm(n, 1, KN, 2, wk_b, 1.0, rope)

            E0f = E0[:, :, :].rearrange("p h s -> p (h s)")
            AMf = AM[:, :, :, :].rearrange("p r h s -> p (r h s)")

            def diag(x):
                return x.rearrange("p (b c) -> p b c", c=P)[:, 0:3:2, :]

            def at_stage(n, s, stick, col):
                d()
                if s >= 4 and s % 2 == 0 and s <= 2 * GH + 2:
                    h = s // 2 - 2
                    dve.wait_ge(pv_mm, 4 * n + h + 1)
                    dst, src = MIX[:, :, col(h)], bank(7, 0, 2 * HD).rearrange("p (t d) -> p t d", t=T)
                    if stick:
                        dve.tensor_copy(dst, src).then_inc(pv_out, 1)
                    else:
                        dve.tensor_tensor(dst, src, rl[:, h % 2, :].unsqueeze(2).to_broadcast([P, T, HD]),
                                          ALU.mult).then_inc(pv_out, 1)
                if s >= 2 and s % 2 == 0 and s <= 2 * GH:
                    h = s // 2 - 1
                    if stick:
                        dve.wait_ge(p_exp, 4 * n + h + 1)
                        dve.scalar_tensor_tensor(out=E0f[:, 384:768], in0=bank(6, 0, 384), scalar=0.0,
                                                 in1=E0f[:, 0:384], op0=ALU.max, op1=ALU.add)
                        dve.scalar_tensor_tensor(out=AMf[:, 384:768], in0=bank(6, 0, 384), scalar=0.0,
                                                 in1=E0f[:, 0:384], op0=ALU.min, op1=ALU.subtract).then_inc(s_max, 1)
                        d()
                        dve.tensor_tensor(diag(E0f[:, 384:768]), diag(E0f[:, 384:768]),
                                          above[:, :].unsqueeze(1).to_broadcast([P, 2, P]), ALU.mult).then_inc(p_rdy, 1)
                        dve.tensor_tensor(diag(AMf[:, 384:768]), diag(AMf[:, 384:768]),
                                          neg_s[:, :].unsqueeze(1).to_broadcast([P, 2, P]), ALU.add)
                        d()
                    else:
                        dve.wait_ge(s_mm, 4 * n + h + 1)
                        dve.tensor_tensor(E0f[:, 0:384], bank(6, 0, 384), maskadd[:, :], ALU.add)
                        d()
                        dve.tensor_reduce(mx[:, 0:1], E0f[:, 0:128], AX_X, ALU.max)
                        dve.tensor_reduce(mx[:, 1:2], E0f[:, 128:384], AX_X, ALU.max)
                        d()
                        dve.tensor_scalar(nmx[:, :], mx[:, :], -1.0, None, ALU.mult).then_inc(s_max, 1)
                        dve.wait_ge(p_exp, 4 * n + h + 1)
                        for t, (c0, c1_) in enumerate(((0, 128), (128, 384))):
                            pp = E0f[:, 384 + c0:384 + c1_]
                            ins = dve.tensor_tensor_reduce(pp, pp, count[:, c0:c1_], 1.0, 0.0, ALU.mult, ALU.add,
                                                           l_[:, t:t + 1])
                        ins.then_inc(p_rdy, 1)
                        d()
                        dve.reciprocal(rl[:, h % 2, :], l_[:, :])
                        d()
                if stick and s >= 3 and s % 2 == 1 and s <= 2 * GH + 1:
                    h = (s - 3) // 2
                    dve.wait_ge(pT_mm, 4 * n + h + 1)
                    dve.tensor_tensor(AMf[:, 0:384], AMf[:, 384:768], bank(7, 0, 384), ALU.subtract).then_inc(arg_rdy, 1)

            dve.wait_ge(x_in, 16)
            rows_norm(MIX)
            turn_dve(dve, 0, g1, mod[:, SHIFT1, :], GN)
            for j in range(CH):
                split_lo(dve, 0, j)
            dve.wait_ge(bcast_in, 32)
            groups = proj_groups()
            for i, (kind, idx, B0, nb) in enumerate(groups + [(None, 0, OUT0, 3)]):
                for s in range(CH * nb):
                    if i:
                        pk, pi, pB, _ = groups[i - 1]
                        if pk == "hg":
                            hg_stage(pi, pB, s)
                        else:
                            at_stage(pi, s, False, lambda h: slice(NC_ * pi + HD * h, NC_ * pi + HD * (h + 1)))
                    if kind:
                        hg_own(idx, B0, s) if kind == "hg" else at_own(idx, B0, s, True)
                        if B0 + s // CH + 1 < OUT0:
                            split_lo(dve, B0 + s // CH + 1, s % CH)
            d()
            for t in range(T):
                dve.tensor_tensor_reduce(QN[:, :, :].rearrange("p t n -> p (t n)"), MIX[:, t, 0:AW], MIX[:, t, 0:AW],
                                         1.0, 0.0, ALU.mult, ALU.add, ssq[:, t:t + 1])
                d()
            rsqrt(dve, T, 1.0 / AW, EPS)
            for t in range(T):
                ins = dve.tensor_scalar(MIX[:, t, 0:AW], MIX[:, t, 0:AW], rstd[:, t:t + 1], None, ALU.mult)
            ins.then_inc(y_rdy_v, 1)
            turn_dve(dve, 1, gmix, zero_c, GN)
            d()

            def gate_block(n, b, sec, dst):
                dve.tensor_tensor(dst.rearrange("p (k c) -> p k c", c=P), ident[:, :].unsqueeze(1).to_broadcast([P, 4, P]),
                                  mod[:, sec, 4 * b:4 * b + 4].unsqueeze(2).to_broadcast([P, 4, P]),
                                  ALU.mult).then_inc(gate_diag, 1)

            for b in range(4):
                if b >= 2:
                    dve.wait_ge(gate_mm, b - 1)
                gate_block(b, b, GATE1, GN[:, b % 2, :])
            for j in range(CH):
                split_lo(dve, OUT0, j)
            for b in range(4):
                if b < 3:
                    for j in range(CH):
                        split_lo(dve, OUT0 + b + 1, j)
                dve.wait_ge(gate_rdy, b + 1)
                dve.wait_ge(chunk_done, 4 * (OUT0 + b + 1))
                dve.tensor_tensor(VN[:, :, :], PS[:, 2 * (b % 2):2 * (b % 2) + 2, :],
                                  (QN, KN)[b // 2][:, b % 2, :].unsqueeze(1).to_broadcast([P, T, NC_]),
                                  ALU.mult).then_inc(pair_read[b % 2], 1)
                d()
                xs = X[:, :, NC_ * b:NC_ * (b + 1)]
                dve.tensor_tensor(xs, xs, VN[:, :, :], ALU.add)
                d()

            def mlp(m, M):
                def up(B, U):
                    for j in range(CH):
                        split_lo(dve, B + 1, j)
                    dve.wait_ge(relu_rdy, U + 1)
                    if not isinstance(U, int) or U:
                        dve.wait_ge(h_tr, U)
                    dve.tensor_tensor(SQ[:, :, :], PS[:, 0:2, :], RE[:, :, :], ALU.mult).then_inc(sq_rdy, 1)

                def turn(U, par):
                    dve.wait_ge(h_hi, U + 1)
                    flat = "p k s -> p (k s)"
                    dve.tensor_tensor(H_lo[:, par, :, :].rearrange(flat), PS[:, 6:8, :],
                                      H_hi[:, par, :, :].rearrange(flat).bitcast(F32), ALU.subtract).then_inc(h_lo, 1)

                def down(B, U, par, end=False):
                    for j in range(CH):
                        if not end:
                            split_lo(dve, B + 1, j)
                        else:
                            dve.wait_ge(chunk_done, 4 * B + j + 1)
                        ac = ACC[:, :, NC_ * j:NC_ * (j + 1)]
                        b = pairs[1 + j % 2]
                        dve.tensor_tensor(ac, ac, PS[:, b:b + 2, :], ALU.add).then_inc(acc_read, 1)
                        if j == 1 and par is not None:
                            turn(U + 1, par)

                for j in range(CH):
                    split_lo(dve, M, j)
                up(M, NU * m)
                turn(NU * m, 0)
                with dve.Fori(0, NU // 2 - 1) as i:
                    for e in range(2):
                        up(M + 1 + 4 * i + 2 * e, NU * m + 1 + 2 * i + e)
                        down(M + 2 + 4 * i + 2 * e, NU * m + 2 * i + e, (e + 1) % 2)
                up(M + 2 * NU - 3, NU * m + NU - 1)
                down(M + 2 * NU - 2, NU * m + NU - 2, (NU - 1) % 2)
                down(M + 2 * NU - 1, NU * m + NU - 1, None, True)
                d()

            rows_norm(ACC)
            turn_dve(dve, 2, g2, mod[:, SHIFT2, :], SQ)
            for t in range(T):
                dve.memset(ACC[:, t, :], 0.0).then_inc(acc_read, 1)
            mlp(0, MLP0)
            for b in range(4):
                gate_block(4 + b, b, GATE2, RE[:, b % 2, :])
                dve.wait_ge(gate_rdy, 4 + b + 1)
                cols = slice(NC_ * b, NC_ * (b + 1))
                dve.tensor_tensor(ACC[:, :, cols], ACC[:, :, cols], SQ[:, b % 2, :].unsqueeze(1).to_broadcast([P, T, NC_]), ALU.mult)
                d()
                dve.tensor_tensor(X[:, :, cols], X[:, :, cols], ACC[:, :, cols], ALU.add)
                d()
            rows_norm(MIX)
            turn_dve(dve, 3, colB[:, RB["nmix"][0]:RB["nmix"][0] + KT], zero_c, GN)
            for j in range(CH):
                split_lo(dve, QKV0, j)
            dve.wait_ge(sbw_in, 32)

            def sb_cols(g):
                return lambda h: bass.ds(NC_ * g + HD * h, HD)

            def sb_group(g, first):
                B0 = QKV0 + 3 * g
                for s in range(12):
                    if not first:
                        at_stage(AT_GROUPS + g - 1, s, True, sb_cols(g - 1))
                    at_own(AT_GROUPS + g, B0, s, False)
                    split_lo(dve, B0 + s // CH + 1, s % CH)

            sb_group(0, True)
            start_jobs = jobs.n
            with dve.Fori(1, SB_GROUPS - 1) as g:
                jobs.base, jobs.n = start_jobs + 2 * (g - 1), 0
                sb_group(g, False)
            jobs.base, jobs.n = 0, start_jobs + 2 * (SB_GROUPS - 2)
            g = SB_GROUPS - 1
            for s in range(12):
                at_stage(AT_GROUPS + g - 1, s, True, sb_cols(g - 1))
                at_own(AT_GROUPS + g, QKV0 + 3 * g, s, False)
                if s < 8:
                    split_lo(dve, QKV0 + 3 * g + s // CH + 1, s % CH)
            for s in range(12):
                at_stage(AT_GROUPS + g, s, True, sb_cols(g))
            d()
            dve.memset(rt[:, 0, 0:1], 0.0).then_inc(y_rdy_v, 1)
            turn_dve(dve, 4, one_c, zero_c, GN)
            for j in range(CH):
                split_lo(dve, WO0, j)
            for b in range(4):
                if b < 3:
                    for j in range(CH):
                        split_lo(dve, WO0 + b + 1, j)
                dve.wait_ge(chunk_done, 4 * (WO0 + b + 1))
                xs = X[:, :, NC_ * b:NC_ * (b + 1)]
                dve.tensor_tensor(xs, xs, PS[:, 2 * (b % 2):2 * (b % 2) + 2, :], ALU.add).then_inc(pair_read[b % 2], 1)
            d()
            rows_norm(ACC)
            turn_dve(dve, 5, colB[:, RB["nmlp"][0]:RB["nmlp"][0] + KT], zero_c, SQ)
            for t in range(T):
                dve.memset(ACC[:, t, :], 0.0).then_inc(acc_read, 1)
            mlp(1, MLP1)
            for t in range(T):
                dve.tensor_tensor(X[:, t, :], X[:, t, :], ACC[:, t, :], ALU.add).then_inc(x_final, 1)

        @block.tensor
        def _(pe):
            used = [0, 0, 0]

            def take(p):
                if not isinstance(used[p], int) or used[p]:
                    pe.wait_ge(pair_read[p], used[p])
                used[p] = used[p] + 1

            pe.wait_ge(pool_const, N_CONST)
            pe.wait_ge(params_in, 16 * 11)
            pe.transpose(bank(6, 0, P), setup[:, 0:P], ident[:, :])
            pe.transpose(bank(6, P, P + NRB), setup[0:NRB, P:2 * P], ident[0:NRB, 0:NRB]).then_inc(pe_const, 1)
            pe.wait_ge(dve_const, 1)
            pe.matmul(bank(6, 0, 1), ones[:, :], ones[:, 0:1], start=True, stop=True).then_inc(ada_sum, 1)
            with pe.Fori(0, 3) as i:
                for h in range(2):
                    pe.wait_ge(ada_used, CH + KT * (2 * i + h + 1))
                    for k in range(KT):
                        mm = pe.matmul(PS[:, 6, bass.ds(KT * (2 * i + h) + k, 1)], MS[:, h, k * P:k * P + P],
                                       ones[:, 0:1], start=True, stop=True)
                    mm.then_inc(ada_sum, 1)

            def turn_group(src, first_bank):
                for i in range(2):
                    for q in range(4):
                        h, t = 2 * i + q // 2, q % 2
                        mm = pe.transpose(bank(first_bank + i, P * q, P * q + P), src[:, t, HD * h:HD * (h + 1)], ident[:, :])
                return mm

            def hg_own(g, s):
                if s == 10:
                    take(1)
                    turn_group(QN, 2).then_inc(hg_tr, 1)
                if s == 13:
                    take(0)
                    turn_group(KN, 0).then_inc(hg_tr, 1)

            def hg_stage(g, s):
                l = 0 if s == 0 else s - 1
                if s == 0 or 1 <= l < NLV:
                    b = level_bank(l)
                    if l == 0:
                        pe.wait_ge(f_rdy, g + 1)
                        pe.wait_ge(pair_read[1], 3 * g + 2)
                        if g:
                            pe.wait_ge(o_out, g)
                        else:
                            pe.wait_ge(a_lo, KT // 2)
                    else:
                        pe.wait_ge(lv_rdy, 8 * g + l)
                        before = {1: 0, 2: 1, 3: 2, 4: 3, 5: 4, 6: 5, 7: 7, 8: 8}[l]
                        if NLV * g + before:
                            pe.wait_ge(lv_cp, NLV * g + before)
                    for h in range(GH):
                        if l == 1:
                            mm = pe.matmul(bank(b, P * h, P * h + P), QK[:, h, 0:P], QK[:, h, P:S], start=True, stop=True)
                        else:
                            for t in range(T):
                                k_, q_ = (kT, qT) if l == 0 else (QK, QK)
                                cols = slice(P * t, P * t + P)
                                mm = pe.matmul(bank(b + t, P * h, P * h + P), k_[:, h, cols], q_[:, h, cols], start=True, stop=True)
                    mm.then_inc(lv_mm, 1)
                if s == 10:
                    pe.wait_ge(lv_cp, NLV * (g + 1))
                    pe.wait_ge(pair_read[0], 3 * g + 2)
                    for h in range(GH):
                        cols = slice(HD * h, HD * (h + 1))
                        pe.matmul(bank(6, P * h, P * h + P), AM[:, 0, h, :], VN[:, 0, cols], start=True, stop=True)
                        pe.matmul(bank(7, P * h, P * h + P), AM[:, 2, h, :], VN[:, 0, cols], start=True, stop=False)
                        mm = pe.matmul(bank(7, P * h, P * h + P), AM[:, 1, h, :], VN[:, 1, cols], start=False, stop=True)
                    mm.then_inc(o_mm, 1)

            def at_own(n, s):
                if s == 9:
                    pe.wait_ge(n_rdy, 2 * n + 1)
                    turn_group(QN, 0).then_inc(n_tr, 1)
                if s == 10:
                    pe.wait_ge(n_rdy, 2 * n + 2)
                    turn_group(KN, 2).then_inc(n_tr, 1)

            E0f = E0[:, :, :].rearrange("p h s -> p (h s)")
            AMf = AM[:, :, :, :].rearrange("p r h s -> p (r h s)")

            def at_stage(n, s, stick):
                if s >= 1 and s % 2 == 1 and s <= 2 * GH - 1:
                    h = s // 2
                    if h == 0:
                        if isinstance(n, int) and n == 0:
                            pe.wait_ge(o_out, HG_GROUPS)
                        elif stick:
                            pe.wait_ge(a_lo, 4 * KT // 2)
                    if not (isinstance(n, int) and n == 0 and h == 0):
                        pe.wait_ge(p_rdy, 4 * n + h)
                    if stick:
                        pe.matmul(bank(6, 0, S), kT[:, h, 0:P], qT[:, h, :], start=True, stop=True)
                        mm = pe.matmul(bank(6, S, S + P), kT[:, h, P:S], qT[:, h, P:S], start=True, stop=True)
                    else:
                        pe.matmul(bank(6, 0, P), qT[:, h, 0:P], kT[:, h, 0:P], start=True, stop=True)
                        mm = pe.matmul(bank(6, P, 3 * P), qT[:, h, P:S], kT[:, h, :], start=True, stop=True)
                    mm.then_inc(s_mm, 1)
                if s >= 2 and s % 2 == 0 and s <= 2 * GH:
                    h = s // 2 - 1
                    pe.wait_ge(p_rdy, 4 * n + h + 1)
                    if not (isinstance(n, int) and n == 0 and h == 0):
                        pe.wait_ge(pv_out, 4 * n + h)
                    if stick:
                        L = E0f[:, 384:768]
                        pe.matmul(bank(7, 0, P), below[:, :], L[:, 0:P], start=True, stop=True)
                        pe.matmul(bank(7, P, S), below[:, :], L[:, P:S], start=True, stop=False)
                        pe.matmul(bank(7, P, S), ones[:, :], L[:, S:S + P], start=False, stop=True)
                        mm = pe.matmul(bank(7, S, S + P), below[:, :], L[:, S:S + P], start=True, stop=True)
                    else:
                        for i in range(3):
                            mm = pe.transpose(bank(7, P * i, P * i + P), E0f[:, 384 + P * i:512 + P * i], ident[:, :])
                    mm.then_inc(pT_mm, 1)
                if s >= 3 and s % 2 == 1 and s <= 2 * GH + 1:
                    h = (s - 3) // 2
                    cols = slice(HD * h, HD * (h + 1))
                    if h == 0:
                        pe.wait_ge(pair_read[2], n + 1)
                    pe.wait_ge(pT_rdy, 4 * n + h + 1)
                    pe.matmul(bank(7, 0, HD), AMf[:, 0:P], VN[:, 0, cols], start=True, stop=True)
                    pe.matmul(bank(7, HD, 2 * HD), AMf[:, P:2 * P], VN[:, 0, cols], start=True, stop=False)
                    pe.matmul(bank(7, HD, 2 * HD), AMf[:, 2 * P:3 * P], VN[:, 1, cols], start=False, stop=True).then_inc(pv_mm, 1)

            turns = [0]

            def turn(src):
                pe.wait_ge(y_rdy_v, turns[0] + 1)
                turn_pe(pe, turns[0], src)
                turns[0] += 1

            turn(MIX)
            groups = proj_groups()
            for i, (kind, idx, B0, nb) in enumerate(groups + [(None, 0, OUT0, 3)]):
                prev_used = list(used)
                for s in range(CH * nb):
                    if kind:
                        p = (s // CH) % 2 if kind == "hg" else s // CH
                        if s % CH == 0:
                            take(p)
                            if p == 2 and idx == 0:
                                pe.wait_ge(lv_cp, NLV * (HG_GROUPS - 1) + 6)
                        a_chunk(pe, B0 + s // CH, s % CH, pairs[p])
                    if i:
                        pk, pi, pB, _ = groups[i - 1]
                        if pk == "hg":
                            hg_stage(pi, s)
                        else:
                            if s == 1:
                                for p in range(2):
                                    pe.wait_ge(pair_read[p], prev_used[p])
                            at_stage(pi, s, False)
                    if kind:
                        (hg_own if kind == "hg" else at_own)(idx, s)

            def gates(n0, diag):
                for b in range(4):
                    pe.wait_ge(gate_diag, n0 + b + 1)
                    if n0 + b >= 2:
                        pe.wait_ge(gate_rdy, n0 + b - 1)
                    pe.matmul(bank(6 + b % 2), ones[:, :], diag[:, b % 2, :], start=True, stop=True).then_inc(gate_mm, 1)

            turn(MIX)
            pe.wait_ge(a_lo, 2 * KT // 2)
            gates(0, GN)
            for b in range(4):
                take(b % 2)
                for j in range(CH):
                    a_chunk(pe, OUT0 + b, j, 2 * (b % 2))

            def mlp(m, M):
                def up(B, U):
                    if not isinstance(U, int) or U:
                        pe.wait_ge(sq_rdy, U)
                    for j in range(CH):
                        a_chunk(pe, B, j, 0)

                def turn_unit(U):
                    pe.wait_ge(sq_rdy, U + 1)
                    if not isinstance(U, int) or U:
                        pe.wait_ge(h_lo, U)
                    turn_group(SQ, 6).then_inc(h_tr, 1)

                def down(B, U, par, turn_next):
                    pe.wait_ge(h_lo, U + 1)
                    for j in range(CH):
                        pe.wait_ge(acc_read, 4 * U + 2 * m + j + 1)
                        chunk(pe, B, j, pairs[1 + j % 2], lambda k, t: H_hi[:, par, k, P * t:P * t + P],
                              lambda k, t: H_lo[:, par, k, P * t:P * t + P], True, True)
                        if j == 1 and turn_next:
                            turn_unit(U + 1)

                up(M, NU * m)
                turn_unit(NU * m)
                with pe.Fori(0, NU // 2 - 1) as i:
                    for e in range(2):
                        up(M + 1 + 4 * i + 2 * e, NU * m + 1 + 2 * i + e)
                        down(M + 2 + 4 * i + 2 * e, NU * m + 2 * i + e, e, True)
                up(M + 2 * NU - 3, NU * m + NU - 1)
                down(M + 2 * NU - 2, NU * m + NU - 2, 0, True)
                down(M + 2 * NU - 1, NU * m + NU - 1, 1, False)

            turn(ACC)
            pe.wait_ge(a_lo, 3 * KT // 2)
            mlp(0, MLP0)
            gates(4, RE)
            turn(MIX)

            def sb_group(base, g, first):
                B0, n = QKV0 + 3 * g, AT_GROUPS + g
                used[0], used[1], used[2] = base[0] + g, base[1] + g, base[2] + g
                for s in range(12):
                    if s % CH == 0:
                        take(s // CH)
                    a_chunk(pe, B0 + s // CH, s % CH, pairs[s // CH])
                    if not first:
                        if s == 1:
                            for p in range(2):
                                pe.wait_ge(pair_read[p], base[p] + g)
                        at_stage(n - 1, s, True)
                    at_own(n, s)

            base = list(used)
            sb_group(base, 0, True)
            with pe.Fori(1, SB_GROUPS) as g:
                sb_group(base, g, False)
            for p in range(3):
                used[p] = base[p] + SB_GROUPS
            for p in range(2):
                pe.wait_ge(pair_read[p], used[p])
            for s in range(12):
                at_stage(AT_GROUPS + SB_GROUPS - 1, s, True)
            turn(MIX)
            pe.wait_ge(a_lo, 5 * KT // 2)
            for b in range(4):
                take(b % 2)
                for j in range(CH):
                    a_chunk(pe, WO0 + b, j, 2 * (b % 2))
            turn(ACC)
            pe.wait_ge(a_lo, 6 * KT // 2)
            mlp(1, MLP1)


def level_bank(l):
    return 4 if l in (1, 3, 5) else 6


def proj_groups():
    g = [("hg", i, PROJ0 + 4 * i, 4) for i in range(HG_GROUPS)]
    return g + [("at", i, PROJ0 + 4 * HG_GROUPS + 3 * i, 3) for i in range(AT_GROUPS)]


def proj_columns():
    cols = [3 * AW + part * HW + g * NC_ for g in range(HG_GROUPS) for part in range(4)]
    return cols + [part * AW + g * NC_ for g in range(AT_GROUPS) for part in range(3)]


_INS = ["x", "c", "positions", "norm1_w", "w_ada", "b_ada", "w_in", "q_norm_w", "k_norm_w", "attn_out_norm_w",
        "hg_lb_logits", "hg_norm_w", "w_out", "norm2_w", "w_ff1", "w_ff2", "norm_mix_g_2", "norm_mlp_g_2",
        "sb_w_qkv_2", "sb_q_norm_g_2", "sb_k_norm_g_2", "sb_w_o_2", "mlp_w_in_2", "mlp_w_out_2"]


def kernel(**inputs):
    from concourse import bacc
    from concourse.bass_utils import run_bass_kernel_spmd

    nc = bacc.Bacc("TRN2", target_bir_lowering=False, num_devices=1, dynamic_dma_scratch_size=1024)
    arrays, args = {}, {}
    for name in _INS:
        arr = np.ascontiguousarray(inputs[name])
        arrays[f"in_{name}_dram"] = arr
        args[name] = nc.dram_tensor(f"in_{name}_dram", arr.shape, mybir.dt.from_np(arr.dtype), kind="ExternalInput").ap()
    out = nc.dram_tensor("out_dram", (1, S, D), F32, kind="ExternalOutput").ap()
    build(nc, args, out)
    r = run_bass_kernel_spmd(nc, [arrays], core_ids=[0])
    return r.results[0]["out_dram"]
```

```python
from contextlib import ExitStack

import concourse.bass as bass
import numpy as np
from concourse import mybir

F32 = mybir.dt.float32
F32R = mybir.dt.float32r
I32 = mybir.dt.int32
U8 = mybir.dt.uint8
ALU = mybir.AluOpType
ACT = mybir.ActivationFunctionType
AX_X = mybir.AxisListType.X

P = 128
S, D = 256, 2048
T = S // P
KT = D // P
NC_ = 512
CH = 4
HD = 128
GH = NC_ // HD
AW = D // 2
HW = D - AW
NU = 4 * D // NC_
EPS = 1e-6
HALF = HD // 8
THETA = 500000.0
NEG = -1e30
SCALE = float(HD) ** -0.5

HG_GROUPS, AT_GROUPS, SB_GROUPS = HW // NC_, AW // NC_, D // NC_
PROJ0 = 0
OUT0 = PROJ0 + 4 * HG_GROUPS + 3 * AT_GROUPS
MLP0 = OUT0 + D // NC_
QKV0 = MLP0 + 2 * NU
WO0 = QKV0 + 3 * SB_GROUPS
MLP1 = WO0 + D // NC_
END = MLP1 + 2 * NU

RA = {"b_ada": (0, 96), "norm1": (96, 16), "norm2": (112, 16)}
RB = {"attn_out": (0, 8), "hgw": (8, 1), "lb": (9, 16), "nmix": (25, 16), "nmlp": (41, 16), "c": (57, 16)}
NRB = 73
SHIFT1, SCALE1, GATE1, SHIFT2, SCALE2, GATE2 = range(6)
ADA_BLOCKS = 4 * D // NC_
OUT_EARLY, WO_EARLY = 6, 9
OUT_ORDER = [(b, k) for b in range(3) for k in (2, 3)] + [(b, k) for b in range(3) for k in (0, 1)] + \
            [(3, k) for k in (2, 3, 0, 1)]
WO_ORDER = [(b, k) for b in range(3) for k in (0, 1, 2)] + [(b, 3) for b in range(3)] + [(3, k) for k in range(4)]
WIDE, NARROW = (6, 7, 4, 5, 2, 3), (6, 7)
EARLY1, LATE1 = (4, 5, 6, 7), (0, 1, 2, 3)
EARLY4, LATE4 = (0, 1, 2, 3, 4, 5), (6, 7)
ALL = tuple(range(KT // 2))
PIECES_BEFORE = {0: 0, 1: 4, 2: 6, 3: 10, 5: 14}
POWER_OF = {0: 1, 1: 2 + HG_GROUPS + 2 * AT_GROUPS}
POWER_OF.update({2: POWER_OF[1] + 1, 3: POWER_OF[1] + 2, 5: POWER_OF[1] + 3 + 2 * SB_GROUPS})
LEVELS = (64, 32, 16, 8, 4, 2, 1)
NLV = 2 + len(LEVELS)


def build(nc, a, out):
    ctx = ExitStack()
    with ctx:
        def sb(name, shape, dt=F32, c=ctx):
            return c.enter_context(nc.sbuf_tensor(name, shape, dt))

        def sem(name):
            return ctx.enter_context(nc.semaphore(name))

        X = sb("X", [P, T, D])
        A_hi, A_lo = sb("A_hi", [P, KT, S], F32R), sb("A_lo", [P, KT, S], F32R)
        raw = sb("raw", [P, CH, CH, NC_])
        w_hi, w_lo = sb("w_hi", [P, CH, CH, NC_], F32R), sb("w_lo", [P, CH, CH, NC_], F32R)
        ident, ones = sb("ident", [P, P]), sb("ones", [P, P])
        neg_s = sb("neg_s", [P, P])
        below, above = sb("below", [P, P]), sb("above", [P, P])
        count, maskadd = sb("count", [P, 3 * P]), sb("maskadd", [P, 3 * P])
        lv_mask = sb("lv_mask", [P, 1 + len(LEVELS), P], U8)
        wq_b, wk_b = sb("wq_b", [P, P]), sb("wk_b", [P, P])
        colA, colB = sb("colA", [P, P]), sb("colB", [P, NRB])
        mod = sb("mod", [P, 6, KT])
        g1, g2, gmix, zero_c, one_c = (sb(n, [P, KT]) for n in ("g1", "g2", "gmix", "zero_c", "one_c"))
        sc = sb("sc", [P, KT])
        lb, lb1 = sb("lb", [P, 8]), sb("lb1", [P, 8])
        cos, sin = sb("cos", [P, T, HALF]), sb("sin", [P, T, HALF])
        rt = sb("rt", [P, 4, T * GH * HALF])
        ssq, rstd, mhalf = sb("ssq", [P, 8]), sb("rstd", [P, 8]), sb("mhalf", [P, 8])
        ssq_blocks = sb("ssq_blocks", [P, D // NC_, T])
        mx, nmx, l_, rl = sb("mx", [P, T]), sb("nmx", [P, T]), sb("l_", [P, T]), sb("rl", [P, 2, T])
        ada_acc = sb("ada_acc", [P, 2, 2, NC_])
        ada_part = sb("ada_part", [P, ADA_BLOCKS, NC_ // 32])
        over = ExitStack()
        MIX = sb("MIX", [P, T, D], c=over)
        QN, KN, VN, GN = (sb(n, [P, T, NC_], c=over) for n in ("QN", "KN", "VN", "GN"))
        qT, bT, kT, E0 = (sb(n, [P, GH, S], c=over) for n in ("qT", "bT", "kT", "E0"))
        AM = sb("AM", [P, 3, GH, P], c=over)
        over.close()
        start = ExitStack()
        MS = sb("MS", [P, 2, D], c=start)
        ada_raw = sb("ada_raw", [P, CH, D], c=start)
        start.close()
        H_hi, H_lo = sb("H_hi", [P, 2, CH, S], F32R), sb("H_lo", [P, 2, CH, S], F32R)
        ACC = sb("ACC", [P, T, D])
        RE, SQ = sb("RE", [P, T, NC_]), sb("SQ", [P, T, NC_])
        ada_ring = X[:, :, :].rearrange("p t (h c n) -> p (t h) c n", c=2, n=NC_)
        DG = ada_acc[:, 0, :, :]
        Y0 = raw[:, 2:4, :, :].rearrange("p j k n -> p j (k n)")
        setup = MS[:, :, :].rearrange("p a n -> p (a n)")
        E1 = MIX[:, 0, 0:D // 2].rearrange("p (h s) -> p h s", h=GH)
        QK = MIX[:, 1, 0:D // 2].rearrange("p (h s) -> p h s", h=GH)

        PS = ctx.enter_context(nc.psum_tensor("PS", [P, 8, NC_], F32))

        params_in, bcast_in, x_in = sem("params_in"), sem("bcast_in"), sem("x_in")
        sbw_in = sem("sbw_in")
        raw_in = [sem(f"raw_in{j}") for j in range(CH)]
        hi_rdy, lo_rdy, chunk_done = sem("hi_rdy"), sem("lo_rdy"), sem("chunk_done")
        pool_const, dve_const, act_const, pe_const = (sem(n) for n in ("pool_const", "dve_const", "act_const", "pe_const"))
        ada_in = [sem(f"ada_in{j}") for j in range(CH)]
        ada_used, ada_sum, arg_rdy = sem("ada_used"), sem("ada_sum"), sem("arg_rdy")
        ring_in = [sem(f"ring_in{j}") for j in range(CH)]
        parts_rdy, prod_rdy, acc_rdy = sem("parts_rdy"), sem("prod_rdy"), sem("acc_rdy")
        ring_used, acc_turned, sel_rdy, mod_mm, mod_rdy = (sem(n) for n in ("ring_used", "acc_turned", "sel_rdy", "mod_mm", "mod_rdy"))
        sum_rdy, rstd_rdy = sem("sum_rdy"), sem("rstd_rdy")
        y_rdy = sem("y_rdy")
        a_tr, a_aff, a_hi, a_lo = sem("a_tr"), sem("a_aff"), sem("a_hi"), sem("a_lo")
        pair_read = [sem(f"pair_read{i}") for i in range(3)]
        gate_diag, gate_mm, gate_rdy = sem("gate_diag"), sem("gate_mm"), sem("gate_rdy")
        relu_rdy, sq_rdy, h_tr, h_hi, h_lo, acc_read = (sem(n) for n in ("relu_rdy", "sq_rdy", "h_tr", "h_hi", "h_lo", "acc_read"))
        q_sig, f_rdy, f_log, g_sig = (sem(n) for n in ("q_sig", "f_rdy", "f_log", "g_sig"))
        hg_tr, diff_rdy, exp_rdy, lv_rdy, lv_mm, lv_cp = (sem(n) for n in ("hg_tr", "diff_rdy", "exp_rdy", "lv_rdy", "lv_mm", "lv_cp"))
        o_mm, o_sq, o_out = sem("o_mm"), sem("o_sq"), sem("o_out")
        sq_act, n_rdy, n_tr = sem("sq_act"), sem("n_rdy"), sem("n_tr")
        s_mm, s_max, p_exp, p_rdy, pT_mm, pT_rdy, pv_mm, pv_out = (
            sem(n) for n in ("s_mm", "s_max", "p_exp", "p_rdy", "pT_mm", "pT_rdy", "pv_mm", "pv_out"))
        stored = sem("stored")

        pairs = (0, 2, 4)

        def bank(i, lo=0, hi=NC_):
            return PS[:, i, lo:hi]

        def heads_t(tile, i):
            return tile[:, 2 * i:2 * i + 2, :].rearrange("p h s -> p (h s)")

        def split_hi(act, B, j):
            act.wait_ge(raw_in[j], 16 * (B + 1))
            if not isinstance(B, int) or B >= 1:
                act.wait_ge(chunk_done, 4 * (B - 1) + j + 1)
            act.activation(w_hi[:, j, :, :], raw[:, j, :, :], ACT.Copy).then_inc(hi_rdy, 1)

        def split_lo(dve, B, j):
            dve.wait_ge(hi_rdy, 4 * B + j + 1)
            dve.tensor_tensor(w_lo[:, j, :, :], raw[:, j, :, :], w_hi[:, j, :, :].bitcast(F32),
                              ALU.subtract).then_inc(lo_rdy, 1)

        def chunk(pe, B, j, pair, hi, lo, start, stop):
            pe.wait_ge(lo_rdy, 4 * B + j + 1)
            for t in range(T):
                for k in range(CH):
                    h, l = hi(k, t), lo(k, t)
                    first, last = start and k == 0, stop and k == CH - 1
                    pe.matmul(bank(pair + t), h, w_hi[:, j, k, :], start=first, stop=False)
                    pe.matmul(bank(pair + t), h, w_lo[:, j, k, :], start=False, stop=False)
                    mm = pe.matmul(bank(pair + t), l, w_hi[:, j, k, :], start=False, stop=last)
            mm.then_inc(chunk_done, 1)

        def square_chunk(pe, B0, order, pos, take):
            b, k = order[pos]
            mine = [x for x, (b_, _) in enumerate(order) if b_ == b]
            if pos == mine[0]:
                take(b % 3)
            chunk(pe, B0 + pos // CH, pos % CH, pairs[b % 3], lambda i, t: A_hi[:, CH * k + i, P * t:P * t + P],
                  lambda i, t: A_lo[:, CH * k + i, P * t:P * t + P], pos == mine[0], pos == mine[-1])

        def last_of(order, b):
            return max(x for x, (b_, _) in enumerate(order) if b_ == b) + 1

        def a_chunk(pe, B, j, pair, turned=None):
            if turned is not None:
                pe.wait_ge(a_lo, KT // 2 * turned + 2 * (j + 1))
            chunk(pe, B, j, pair, lambda k, t: A_hi[:, CH * j + k, P * t:P * t + P],
                  lambda k, t: A_lo[:, CH * j + k, P * t:P * t + P], j == 0, j == CH - 1)

        def turn_pe(pe, n, src, steps=ALL, first=0, banks=WIDE):
            for pos, i in enumerate(steps):
                if n in PIECES_BEFORE and pos % 2 == 0 and not (n == 1 and first == 0):
                    pe.wait_ge(y_rdy, PIECES_BEFORE[n] + pos // 2 + 1)
                if pos >= len(banks):
                    pe.wait_ge(a_aff, KT // 2 * n + first + pos - len(banks) + 1)
                for q in range(4):
                    kt, t = 2 * i + q // 2, q % 2
                    mm = pe.transpose(bank(banks[pos % len(banks)], P * q, P * q + P), src[:, t, kt * P:kt * P + P], ident[:, :])
                mm.then_inc(a_tr, 1)

        def normalise(act, src, dst, c):
            for t in range(T):
                cols = slice(NC_ * c, NC_ * c + NC_)
                ins = act.activation(dst[:, t, cols], src[:, t, cols], ACT.Copy, scale=rstd[:, t:t + 1])
            ins.then_inc(y_rdy, 1)

        def turn_act(act, n, tmp, steps=ALL, first=0, norm=None, between=None):
            if norm:
                act.wait_ge(rstd_rdy, POWER_OF[n])
                for c in (0, 1):
                    normalise(act, *norm, c)
            for pos, i in enumerate(steps):
                if norm and pos in (2, 4) and 2 * len(steps) == KT:
                    normalise(act, *norm, pos // 2 + 1)
                act.wait_ge(a_aff, KT // 2 * n + first + pos + 1)
                act.activation(A_hi[:, 2 * i:2 * i + 2, :].rearrange("p k s -> p (k s)"), tmp[:, pos % 2, :],
                               ACT.Copy).then_inc(a_hi, 1)
                if between and pos in between:
                    between[pos]()

        def turn_dve(dve, n, g, s, tmp, steps=ALL, first=0, banks=WIDE, between=None):
            dve.drain()
            for pos in range(len(steps) + 1):
                if pos < len(steps):
                    i = steps[pos]
                    dve.wait_ge(a_tr, KT // 2 * n + first + pos + 1)
                    if pos >= 2:
                        dve.wait_ge(a_lo, KT // 2 * n + first + pos - 1)
                    for k in range(2):
                        kt = 2 * i + k
                        ins = dve.tensor_scalar(tmp[:, pos % 2, S * k:S * k + S],
                                                bank(banks[pos % len(banks)], S * k, S * k + S),
                                                g[:, kt:kt + 1], s[:, kt:kt + 1], ALU.mult, ALU.add)
                    ins.then_inc(a_aff, 1)
                if pos:
                    i = steps[pos - 1]
                    dve.wait_ge(a_hi, KT // 2 * n + first + pos)
                    flat = "p k s -> p (k s)"
                    dve.tensor_tensor(A_lo[:, 2 * i:2 * i + 2, :].rearrange(flat), tmp[:, (pos - 1) % 2, :],
                                      A_hi[:, 2 * i:2 * i + 2, :].rearrange(flat).bitcast(F32),
                                      ALU.subtract).then_inc(a_lo, 1)
                    if between and pos - 1 in between:
                        between[pos - 1]()
            dve.drain()

        class Jobs:
            def __init__(self):
                self.base, self.n = 0, 0

        jobs = Jobs()

        def rsqrt(dve, w, mul, add):
            dve.drain()
            dve.tensor_scalar(ssq[:, 0:w], ssq[:, 0:w], mul, add, ALU.mult, ALU.add).then_inc(sum_rdy, 1)
            jobs.n += 1
            dve.wait_ge(rstd_rdy, jobs.base + jobs.n)

        block = ctx.enter_context(nc.Block())

        @block.sync
        def _(sp):
            pa, pb = setup[:, 0:P], setup[:, P:2 * P]
            rows = [(pa, RA["b_ada"], a["b_ada"]), (pa, RA["norm1"], a["norm1_w"]), (pa, RA["norm2"], a["norm2_w"]),
                    (pb, RB["attn_out"], a["attn_out_norm_w"]), (pb, RB["hgw"], a["hg_norm_w"]),
                    (pb, RB["lb"], a["hg_lb_logits"]), (pb, RB["nmix"], a["norm_mix_g_2"]),
                    (pb, RB["nmlp"], a["norm_mlp_g_2"]), (pb, RB["c"], a["c"])]
            for tile, (r0, n), src in rows:
                sp.dma_start(tile[r0:r0 + n, :], src.rearrange("a (r p) -> (a r) p", p=P)).then_inc(params_in, 16)
            for t in range(T):
                sp.dma_start(rt[:, 0, t:t + 1].bitcast(I32),
                             a["positions"][0:1, P * t:P * t + P].rearrange("a (p b) -> (a p) b", b=1)).then_inc(params_in, 16)
            sp.dma_start(wq_b[:, :], a["q_norm_w"].to_broadcast([P, P])).then_inc(bcast_in, 16)
            sp.dma_start(wk_b[:, :], a["k_norm_w"].to_broadcast([P, P])).then_inc(bcast_in, 16)
            sp.dma_start(X[:, :, :], a["x"].rearrange("a (t p) d -> p (a t) d", p=P)).then_inc(x_in, 16)
            ada = a["w_ada"].rearrange("a (k p) (s n) -> p (a k) s n", p=P, n=D)
            with sp.Fori(0, 2) as i:
                for k in range(KT):
                    sp.wait_ge(ada_used, KT * i + k + 1)
                    sp.dma_start(ada_raw[:, k % CH, :], ada[:, k, i, :]).then_inc(ada_in[k % CH], 16)

            def load(B, j, src):
                if isinstance(B, int) and B == 0 and j == 2:
                    sp.wait_ge(a_tr, KT // 2)
                if not isinstance(B, int) or B >= 1:
                    sp.wait_ge(lo_rdy, 4 * (B - 1) + j + 1)
                sp.dma_start(raw[:, j, :, :], src).then_inc(raw_in[j], 16)

            ada_b = a["w_ada"].rearrange("a (k p) (b n) -> p (a k) b n", p=P, n=NC_)

            sp.wait_ge(y_rdy, 4)

            def ada_load(n, j):
                for q in range(8 * n + 2 * j, 8 * n + 2 * j + 2):
                    if q >= CH:
                        sp.wait_ge(ring_used, q - CH + 1)
                    sp.dma_start(ada_ring[:, q % CH, :, :],
                                 ada_b[:, 2 * (q % 8):2 * (q % 8) + 2, 2 * D // NC_ + n, :]).then_inc(ring_in[q % CH], 16)

            w_in = a["w_in"].rearrange("a (j k p) n -> p (a j) k n", j=CH, p=P)
            for B, c0 in enumerate(proj_columns()):
                for j in range(CH):
                    load(B, j, w_in[:, j, :, c0:c0 + NC_])
                    if B:
                        ada_load(B - 1, j)

            def mlp(M, w1, w2):
                v1 = w1.rearrange("a (j k p) (u n) -> p (a j) k u n", j=CH, p=P, n=NC_)
                v2 = w2.rearrange("a (u k p) (j n) -> p (a u) k j n", k=CH, p=P, n=NC_)

                def up(B, u):
                    for j in range(CH):
                        load(B, j, v1[:, j, :, u, :])

                def down(B, u):
                    for j in range(CH):
                        load(B, j, v2[:, u, :, j, :])

                up(M, 0)
                with sp.Fori(0, NU - 1) as u:
                    up(M + 1 + 2 * u, u + 1)
                    down(M + 2 + 2 * u, u)
                down(M + 2 * NU - 1, NU - 1)

            def square(B0, w, order, ada):
                v = w.rearrange("a (j k p) (b n) -> p (a j) k b n", j=CH, p=P, n=NC_)
                for pos, (b, k) in enumerate(order):
                    B, j = B0 + pos // CH, pos % CH
                    load(B, j, v[:, k, :, b, :])
                    if ada and B - 1 < ADA_BLOCKS:
                        ada_load(B - 1, j)
                    if ada and pos == CH * (ADA_BLOCKS + 1 - B0) - 1:
                        sp.wait_ge(ring_used, 8 * ADA_BLOCKS)
                        sp.dma_start(X[:, :, :], a["x"].rearrange("a (t p) d -> p (a t) d", p=P)).then_inc(x_in, 16)

            def mlp(M, w1, w2):
                v1 = w1.rearrange("a (j k p) (u n) -> p (a j) k u n", j=CH, p=P, n=NC_)
                v2 = w2.rearrange("a (u k p) (j n) -> p (a u) k j n", k=CH, p=P, n=NC_)

                def up(B, u):
                    for j in range(CH):
                        load(B, j, v1[:, j, :, u, :])

                def down(B, u):
                    for j in range(CH):
                        load(B, j, v2[:, u, :, j, :])

                up(M, 0)
                with sp.Fori(0, NU - 1) as u:
                    up(M + 1 + 2 * u, u + 1)
                    down(M + 2 + 2 * u, u)
                down(M + 2 * NU - 1, NU - 1)

            w_out = a["w_out"].rearrange("a (j k p) (b n) -> p (a j) k b n", j=CH, p=P, n=NC_)
            square(OUT0, a["w_out"], OUT_ORDER, True)
            mlp(MLP0, a["w_ff1"], a["w_ff2"])
            qkv = a["sb_w_qkv_2"].rearrange("a (j k p) (s g n) -> p (a j) k s g n", j=CH, p=P, s=3, n=NC_)
            sp.dma_start(wq_b[:, :], a["sb_q_norm_g_2"].to_broadcast([P, P])).then_inc(sbw_in, 16)
            sp.dma_start(wk_b[:, :], a["sb_k_norm_g_2"].to_broadcast([P, P])).then_inc(sbw_in, 16)
            with sp.Fori(0, SB_GROUPS) as g:
                for s_ in range(3):
                    for j in range(CH):
                        load(QKV0 + 3 * g + s_, j, qkv[:, j, :, s_, g, :])
            square(WO0, a["sb_w_o_2"], WO_ORDER, False)
            mlp(MLP1, a["mlp_w_in_2"], a["mlp_w_out_2"])
            for b in range(D // NC_):
                cols = slice(NC_ * b, NC_ * b + NC_)
                sp.wait_ge(acc_read, 4 * 2 * NU + 2 * 2 - 3 + b)
                sp.dma_start(out[:, :, cols].rearrange("a (t p) n -> p (a t) n", p=P), X[:, :, cols]).then_inc(stored, 16)
            sp.wait_ge(stored, 16 * D // NC_)

        ints = setup[:, 256:1024].bitcast(I32)
        dist, tmp_i = ints[:, 0:384], ints[:, 384:768]
        rows_i, cols_i, xor_i = (setup[:, c:c + P].bitcast(I32) for c in (1024, 1152, 1280))
        f_a, f_b = setup[:, 1408:1792], setup[:, 1792:2176]
        invf = setup[:, 2176:2176 + HALF]
        pos_i = rt[:, 0, 0:T].bitcast(I32)
        ang = setup[:, 2304:2304 + T * HALF].rearrange("p (t f) -> p t f", t=T)
        kk = setup[:, 2432:2432 + T * HALF].rearrange("p (t f) -> p t f", t=T)
        posf, lbt = setup[:, 2500:2502], setup[:, 2560:2584]

        N_CONST = 15
        JOBS = 1 + HG_GROUPS + 2 * AT_GROUPS + 1 + 1 + 1 + 2 * SB_GROUPS + 1

        @block.gpsimd
        def _(pool):
            def const(ins):
                ins.then_inc(pool_const, 1)

            const(pool.memset(ident[:, :], 0.0))
            const(pool.memset(ones[:, :], 1.0))
            const(pool.memset(below[:, :], 1.0))
            const(pool.memset(above[:, :], 1.0))
            const(pool.memset(mhalf[:, :], -0.5))
            const(pool.memset(zero_c[:, :], 0.0))
            const(pool.memset(one_c[:, :], 1.0))
            for f in range(HALF):
                ins = pool.memset(invf[:, f:f + 1], float(np.float32(THETA ** (-2.0 * f / (2 * HALF)))))
            const(ins)
            pool.wait_ge(pool_const, 8)
            const(pool.affine_select(out=ident[:, :], in_=ident[:, :], compare_op=ALU.not_equal, fill=1.0,
                                     base=0, pattern=[[-1, P]], channel_multiplier=1))
            const(pool.affine_select(out=below[:, :], in_=below[:, :], compare_op=ALU.is_gt, fill=0.0,
                                     base=0, pattern=[[-1, P]], channel_multiplier=1))
            const(pool.affine_select(out=above[:, :], in_=above[:, :], compare_op=ALU.is_gt, fill=0.0,
                                     base=0, pattern=[[1, P]], channel_multiplier=-1))
            const(pool.iota(dist[:, 0:P], pattern=[[-1, P]], base=S, channel_multiplier=1))
            const(pool.iota(dist[:, P:3 * P], pattern=[[-1, 2 * P]], base=S + P, channel_multiplier=1))
            const(pool.iota(rows_i, pattern=[[0, P]], base=0, channel_multiplier=1))
            const(pool.iota(cols_i, pattern=[[1, P]], base=0, channel_multiplier=0))

            def power(i):
                pool.wait_ge(sum_rdy, i + 1)
                pool.tensor_tensor(rstd[:, :], ssq[:, :], mhalf[:, :], ALU.pow).then_inc(rstd_rdy, 1)

            def ada_sums(n, j):
                acc = ada_acc[:, n % 2, :, :]
                for q in range(8 * n + 2 * j, 8 * n + 2 * j + 2):
                    w = ada_ring[:, q % CH, :, :]
                    pool.wait_ge(prod_rdy, q + 1)
                    if q % 8 == 0:
                        continue
                    if q % 8 == 1:
                        if n >= 2:
                            pool.wait_ge(acc_turned, n - 1)
                        pool.tensor_tensor(acc, ada_ring[:, (q - 1) % CH, :, :], w, ALU.add).then_inc(ring_used, 2)
                    else:
                        pool.tensor_tensor(acc, acc, w, ALU.add).then_inc(ring_used, 1)
                    pool.drain()
                if j == CH - 1:
                    pool.tensor_tensor(acc[:, 0, :], acc[:, 0, :], acc[:, 1, :], ALU.add).then_inc(acc_rdy, 1)

            power(0)
            done = 1
            groups = proj_groups()
            for i, (kind, idx, B0, nb) in enumerate(groups):
                for s in range(CH * nb):
                    if (i and groups[i - 1][0] == "hg" and s == 11) or (kind == "at" and s in (4, 8)):
                        power(done)
                        done += 1
                    ada_sums(B0 + s // CH, s % CH)
            for n in range(OUT0, ADA_BLOCKS):
                for j in range(CH):
                    ada_sums(n, j)
            power(done)
            power(done + 1)
            pool.wait_ge(a_tr, 3 * KT // 2)
            for t in range(T):
                pool.memset(ACC[:, t, :], 0.0).then_inc(acc_read, 1)
            with pool.Fori(done + 2, JOBS) as i:
                power(i)

        @block.scalar
        def _(act):
            act.wait_ge(dve_const, 1)
            act.activation(sc[:, :], colB[:, RB["c"][0]:NRB], ACT.Sigmoid).then_inc(act_const, 1)
            act.wait_ge(dve_const, 2)
            act.activation(lbt[:, 0:16], lbt[:, 0:16], ACT.Exp).then_inc(act_const, 1)
            act.wait_ge(dve_const, 3)
            act.activation(sin[:, :, :], ang, ACT.Sin).then_inc(act_const, 1)
            act.activation(cos[:, :, :], ang, ACT.Sin, scale=0.5).then_inc(act_const, 1)

            def ada_products(n, j):
                for q in range(8 * n + 2 * j, 8 * n + 2 * j + 2):
                    act.wait_ge(ring_in[q % CH], 16 * (q // CH + 1))
                    for c in range(2):
                        k, w = 2 * (q % 8) + c, ada_ring[:, q % CH, c, :]
                        ins = act.activation(w, w, ACT.Copy, scale=sc[:, k:k + 1])
                    ins.then_inc(prod_rdy, 1)

            def hg_own(g, B0, s):
                if s == 4:
                    act.wait_ge(chunk_done, 4 * (B0 + 1))
                    act.activation(KN[:, :, :], PS[:, 0:2, :], ACT.Sigmoid).then_inc(q_sig, 1)
                if s == 8:
                    act.wait_ge(chunk_done, 4 * (B0 + 2))
                    act.wait_ge(pair_read[0], 3 * g + 1)
                    act.activation(KN[:, :, :], PS[:, 2:4, :], ACT.Sigmoid).then_inc(pair_read[1], 1)
                if s == 11:
                    act.wait_ge(hg_tr, 2 * g + 1)
                    if g:
                        act.wait_ge(lv_rdy, 8 * g)
                    for i in range(2):
                        c = act.activation(heads_t(qT, i), bank(2 + i), ACT.Copy)
                    c.then_inc(pair_read[1], 1)
                if s == 12:
                    act.wait_ge(chunk_done, 4 * (B0 + 3))
                    if g:
                        act.wait_ge(o_mm, g)
                    act.activation(VN[:, :, :], PS[:, 0:2, :], ACT.Copy).then_inc(pair_read[0], 1)
                if s == 15:
                    act.wait_ge(f_rdy, g + 1)
                    act.activation(E0[:, :, :], E0[:, :, :], ACT.Ln).then_inc(f_log, 1)

            def hg_stage(g, B0, s):
                if s == 0:
                    act.wait_ge(chunk_done, 4 * (B0 + 4))
                    if g:
                        act.wait_ge(o_out, g)
                    act.activation(GN[:, :, :], PS[:, 2:4, :], ACT.Sigmoid).then_inc(g_sig, 1)
                if 1 <= s < NLV:
                    E = (E0, E1)[s % 2]
                    act.wait_ge(diff_rdy, 8 * g + s)
                    act.activation(E[:, :, :], E[:, :, :], ACT.Exp).then_inc(exp_rdy, 1)
                if s == 11:
                    act.wait_ge(o_mm, g + 1)
                    act.activation(E1.rearrange("p h s -> p (h s)"), PS[:, 6:8, :], ACT.Square).then_inc(o_sq, 1)

            def at_own(n, B0, s):
                if s == 4:
                    act.wait_ge(chunk_done, 4 * (B0 + 1))
                    act.activation(QN[:, :, :], PS[:, 0:2, :], ACT.Square).then_inc(sq_act, 1)
                if s == 8:
                    act.wait_ge(chunk_done, 4 * (B0 + 2))
                    act.activation(KN[:, :, :], PS[:, 2:4, :], ACT.Square).then_inc(sq_act, 1)
                if s == 10:
                    act.wait_ge(n_tr, 2 * n + 1)
                    if isinstance(n, int) and n == 0:
                        act.wait_ge(lv_rdy, 8 * HG_GROUPS)
                    else:
                        act.wait_ge(s_mm, 4 * n)
                    for i in range(2):
                        c = act.activation(heads_t(qT, i), bank(i), ACT.Copy)
                    c.then_inc(pair_read[0], 1)
                if s == 11:
                    act.wait_ge(n_tr, 2 * n + 2)
                    for i in range(2):
                        c = act.activation(heads_t(kT, i), bank(2 + i), ACT.Copy)
                    c.then_inc(pair_read[1], 1)

            E0f = E0[:, :, :].rearrange("p h s -> p (h s)")
            AMf = AM[:, :, :, :].rearrange("p r h s -> p (r h s)")

            def at_stage(n, B0, s, stick):
                if s == 0:
                    act.wait_ge(chunk_done, 4 * (B0 + 3))
                    if isinstance(n, int) and n == 0:
                        act.wait_ge(o_mm, HG_GROUPS)
                    else:
                        act.wait_ge(pv_mm, 4 * n)
                    act.activation(VN[:, :, :], PS[:, 4:6, :], ACT.Copy).then_inc(pair_read[2], 1)
                if s >= 2 and s % 2 == 0 and s <= 2 * GH:
                    h = s // 2 - 1
                    if stick:
                        act.wait_ge(s_mm, 4 * n + h + 1)
                        act.activation(E0f[:, 0:384], bank(6, 0, 384), ACT.Abs)
                        act.drain()
                        act.activation(E0f[:, 0:384], E0f[:, 0:384], ACT.Exp, scale=-1.0)
                        act.drain()
                        act.activation(E0f[:, 0:384], E0f[:, 0:384], ACT.Ln, bias=one_c[:, 0:1]).then_inc(p_exp, 1)
                    else:
                        act.wait_ge(s_max, 4 * n + h + 1)
                        act.wait_ge(pT_mm, 4 * n + h)
                        act.activation(E0f[:, 384:512], E0f[:, 0:128], ACT.Exp, bias=nmx[:, 0:1])
                        act.activation(E0f[:, 512:768], E0f[:, 128:384], ACT.Exp, bias=nmx[:, 1:2]).then_inc(p_exp, 1)
                if s >= 3 and s % 2 == 1 and s <= 2 * GH + 1:
                    h = (s - 3) // 2
                    if stick:
                        act.wait_ge(arg_rdy, 4 * (n - AT_GROUPS) + h + 1)
                        act.activation(AMf[:, 0:384], AMf[:, 0:384], ACT.Exp).then_inc(pT_rdy, 1)
                    else:
                        act.wait_ge(pT_mm, 4 * n + h + 1)
                        act.activation(AMf[:, 0:384], bank(7, 0, 384), ACT.Copy).then_inc(pT_rdy, 1)

            act.wait_ge(rstd_rdy, POWER_OF[0])
            for c in range(4):
                normalise(act, X, Y0, c)
            turn_act(act, 0, GN, between={1: lambda: split_hi(act, 0, 0), 4: lambda: split_hi(act, 0, 1)})
            for j in (2, 3):
                split_hi(act, 0, j)
            groups = proj_groups()
            for i, (kind, idx, B0, nb) in enumerate(groups):
                for s in range(CH * nb):
                    if i:
                        pk, pi, pB, _ = groups[i - 1]
                        hg_stage(pi, pB, s) if pk == "hg" else at_stage(pi, pB, s, False)
                    (hg_own if kind == "hg" else at_own)(idx, B0, s)
                    split_hi(act, B0 + s // CH + 1, s % CH)
                    ada_products(B0 + s // CH, s % CH)

            def tail(n, B0, stick, turn, steps, B, splits):
                at_stage(n, B0, 0, stick)
                turn_act(act, turn, GN, steps)
                for s in range(2, 12):
                    at_stage(n, B0, s, stick)
                    if 0 <= s - 3 < splits:
                        split_hi(act, B + 1 + (s - 3) // CH, (s - 3) % CH)
                    if turn == 1 and s - 3 < 2 * CH:
                        ada_products(OUT0 + (s - 3) // CH, (s - 3) % CH) if s >= 3 else None

            tail(AT_GROUPS - 1, OUT0 - 3, False, 1, EARLY1, OUT0, CH)

            def gate(n, b, dst):
                act.wait_ge(gate_mm, n + 1)
                act.activation(dst, bank(6 + b % 2), ACT.Copy).then_inc(gate_rdy, 1)

            turn_act(act, 1, GN, LATE1, len(EARLY1), norm=(MIX, MIX))
            for b in range(4):
                gate(b, b, (QN, KN)[b // 2][:, b % 2, :])
                if b % 2:
                    for j in (b - 1, b):
                        split_hi(act, OUT0 + 2, j)
            for B in (OUT0 + 3, OUT0 + 4):
                for j in range(CH):
                    split_hi(act, B, j)

            def mlp(m, M):
                def up(B, U):
                    for j in range(CH):
                        split_hi(act, B + 1, j)
                    act.wait_ge(chunk_done, 4 * (B + 1))
                    if not isinstance(U, int) or U:
                        act.wait_ge(sq_rdy, U)
                    act.activation(RE[:, :, :], PS[:, 0:2, :], ACT.Relu).then_inc(relu_rdy, 1)

                def turn(U, par):
                    act.wait_ge(h_tr, U + 1)
                    act.activation(H_hi[:, par, :, :].rearrange("p k s -> p (k s)"), PS[:, 6:8, :],
                                   ACT.Copy).then_inc(h_hi, 1)

                def down(B, U, par, end=False):
                    for j in range(CH):
                        if not end:
                            split_hi(act, B + 1, j)
                        if j == 1 and par is not None:
                            turn(U + 1, par)

                up(M, NU * m)
                turn(NU * m, 0)
                with act.Fori(0, NU // 2 - 1) as i:
                    for e in range(2):
                        up(M + 1 + 4 * i + 2 * e, NU * m + 1 + 2 * i + e)
                        down(M + 2 + 4 * i + 2 * e, NU * m + 2 * i + e, (e + 1) % 2)
                up(M + 2 * NU - 3, NU * m + NU - 1)
                down(M + 2 * NU - 2, NU * m + NU - 2, (NU - 1) % 2)

            turn_act(act, 2, SQ, norm=(X, ACC))
            mlp(0, MLP0)
            for b in range(4):
                gate(4 + b, b, (SQ, RE)[b // 2][:, b % 2, :])
                if b in (1, 2):
                    split_hi(act, QKV0, b - 1)
            turn_act(act, 3, GN, norm=(X, MIX))
            for j in (2, 3):
                split_hi(act, QKV0, j)

            def sb_group(g, first):
                B0 = QKV0 + 3 * g
                for s in range(12):
                    if not first:
                        at_stage(AT_GROUPS + g - 1, B0 - 3, s, True)
                    at_own(AT_GROUPS + g, B0, s)
                    split_hi(act, B0 + s // CH + 1, s % CH)

            sb_group(0, True)
            with act.Fori(1, SB_GROUPS) as g:
                sb_group(g, False)
            tail(AT_GROUPS + SB_GROUPS - 1, WO0 - 3, True, 4, EARLY4, WO0, 2 * CH)
            turn_act(act, 4, GN, LATE4, len(EARLY4))
            for B in (WO0 + 3, WO0 + 4):
                for j in range(CH):
                    split_hi(act, B, j)
            turn_act(act, 5, SQ, norm=(X, ACC))
            mlp(1, MLP1)

        @block.vector
        def _(dve):
            d = dve.drain

            def root(junk):
                for t in range(T):
                    dve.tensor_tensor_reduce(junk[:, t, :], X[:, t, :], X[:, t, :], 1.0, 0.0, ALU.mult, ALU.add,
                                             ssq[:, t:t + 1])
                rsqrt(dve, T, 1.0 / D, EPS)

            rtf = rt[:, :, :].rearrange("p i n -> p (i n)")

            def block_squares(b):
                for t in range(T):
                    xs = X[:, t, NC_ * b:NC_ * (b + 1)]
                    d()
                    dve.tensor_tensor_reduce(rtf, xs, xs, 1.0, 0.0, ALU.mult, ALU.add, ssq_blocks[:, b, t:t + 1])

            def root_of_blocks():
                d()
                dve.tensor_reduce(ssq[:, 0:T], ssq_blocks[:, :, :].rearrange("p b t -> p t b"), AX_X, ALU.add)
                rsqrt(dve, T, 1.0 / D, EPS)

            for i in range(CH):
                dve.memset(ssq[:, 2 * i:2 * i + 2], 1.0).then_inc(ada_used, 1)
            dve.wait_ge(pool_const, N_CONST)
            dve.wait_ge(pe_const, 1)
            dve.tensor_copy(colA[:, :], bank(6, 0, P))
            dve.tensor_copy(colB[:, :], bank(6, P, P + NRB)).then_inc(dve_const, 1)
            d()
            l0 = RB["lb"][0]
            dve.tensor_tensor(lbt[:, 16:24], colB[:, l0:l0 + 8], colB[:, l0 + 8:l0 + 16], ALU.max)
            d()
            dve.tensor_tensor(lbt[:, 0:8], colB[:, l0:l0 + 8], lbt[:, 16:24], ALU.subtract)
            dve.tensor_tensor(lbt[:, 8:16], colB[:, l0 + 8:l0 + 16], lbt[:, 16:24], ALU.subtract).then_inc(dve_const, 1)
            dve.wait_ge(params_in, 16 * 11)
            dve.tensor_copy(posf, pos_i)
            d()
            for t in range(T):
                dve.tensor_scalar(ang[:, t, :], invf, posf[:, t:t + 1], None, ALU.mult)
            d()
            ROUND = 12582912.0
            dve.tensor_scalar(kk, ang, float(1 / (2 * np.pi)), ROUND, ALU.mult, ALU.add)
            d()
            dve.tensor_scalar(kk, kk, ROUND, None, ALU.subtract)
            d()
            c1 = 6.28125
            c2 = float(np.float32(np.round((2 * np.pi - c1) * 2 ** 21) / 2 ** 21))
            for c in (c1, c2, float(2 * np.pi - c1 - c2)):
                dve.scalar_tensor_tensor(out=ang, in0=kk, scalar=-c, in1=ang, op0=ALU.mult, op1=ALU.add)
                d()
            dve.tensor_scalar(ang, ang, 3.1415925, -3.1415925, ALU.min, ALU.max).then_inc(dve_const, 1)
            for mask, dst in ((3, f_a), (15, f_b)):
                dve.tensor_scalar(tmp_i, dist, mask, None, ALU.bitwise_and)
                d()
                dve.tensor_scalar(dst, tmp_i, 0.0, None, ALU.is_equal)
                d()
            dve.scalar_tensor_tensor(out=f_a, in0=dist, scalar=float(S + P), in1=f_a, op0=ALU.is_le, op1=ALU.add)
            d()
            dve.tensor_tensor(f_a, f_a, f_b, ALU.add)
            d()
            dve.scalar_tensor_tensor(out=count[:, :], in0=dist, scalar=float(S), in1=f_a, op0=ALU.is_ge, op1=ALU.mult)
            d()
            dve.tensor_scalar(maskadd[:, :], count[:, :], 0.5, None, ALU.is_gt)
            d()
            dve.tensor_scalar(maskadd[:, :], maskadd[:, :], -NEG, NEG, ALU.mult, ALU.add)
            dve.tensor_scalar(neg_s[:, :], above[:, :], -NEG, NEG, ALU.mult, ALU.add)
            dve.tensor_tensor(xor_i, rows_i, cols_i, ALU.bitwise_xor)
            d()
            dve.scalar_tensor_tensor(out=f_a[:, 0:P], in0=xor_i, scalar=1.0, in1=above[:, :], op0=ALU.add, op1=ALU.mult)
            dve.tensor_copy(lv_mask[:, 0, :], ident[:, :])
            d()
            for i, w in enumerate(LEVELS):
                dve.tensor_scalar(f_b[:, 0:P], f_a[:, 0:P], w + 1.0, None, ALU.is_ge)
                d()
                dve.scalar_tensor_tensor(out=lv_mask[:, 1 + i, :], in0=f_a[:, 0:P], scalar=2 * w + 1.0,
                                         in1=f_b[:, 0:P], op0=ALU.is_lt, op1=ALU.mult)
                d()
            dve.wait_ge(act_const, 4)
            dve.tensor_tensor(sc[:, :], sc[:, :], colB[:, RB["c"][0]:NRB], ALU.mult)
            dve.tensor_tensor(lbt[:, 16:24], lbt[:, 0:8], lbt[:, 8:16], ALU.add)
            dve.tensor_copy(gmix[:, 0:8], colB[:, 0:8])
            dve.tensor_scalar(gmix[:, 8:16], one_c[:, 0:8], colB[:, 8:9], None, ALU.mult)
            dve.tensor_tensor(cos[:, :, :], cos[:, :, :], cos[:, :, :], ALU.mult)
            d()
            dve.reciprocal(lbt[:, 16:24], lbt[:, 16:24])
            dve.tensor_scalar(cos[:, :, :], cos[:, :, :], -2.0, 1.0, ALU.mult, ALU.add)
            d()
            dve.tensor_tensor(lb[:, :], lbt[:, 0:8], lbt[:, 16:24], ALU.mult)
            dve.tensor_tensor(lb1[:, :], lbt[:, 8:16], lbt[:, 16:24], ALU.mult)
            d()
            dve.wait_ge(x_in, 16)
            root(Y0)
            for h in range(2):
                for k in range(KT):
                    sl = ada_raw[:, k % CH, :]
                    dve.wait_ge(ada_in[k % CH], 16 * (h * (KT // CH) + k // CH + 1))
                    if k == 0:
                        ins = dve.tensor_scalar(MS[:, h, :], sl, sc[:, k:k + 1], None, ALU.mult)
                    else:
                        ins = dve.scalar_tensor_tensor(out=MS[:, h, :], in0=sl, scalar=sc[:, k:k + 1],
                                                       in1=MS[:, h, :], op0=ALU.mult, op1=ALU.add)
                    ins.then_inc(ada_used, 1)
                    dve.wait_ge(ada_used, CH + KT * h + k + 1)

            def modulation(sec0, sec1):
                n = KT * (sec1 - sec0)
                dve.tensor_tensor(mod[:, sec0:sec1, :].rearrange("p s k -> p (s k)"), bank(6, 0, n),
                                  colA[:, KT * sec0:KT * sec1], ALU.add).then_inc(mod_rdy, 1)

            def scale(g_, sec, nm):
                r0 = RA[nm][0]
                d()
                dve.scalar_tensor_tensor(out=g_[:, :], in0=mod[:, sec, :], scalar=1.0, in1=colA[:, r0:r0 + KT],
                                         op0=ALU.add, op1=ALU.mult)

            dve.wait_ge(ada_sum, 2)
            modulation(SHIFT1, GATE1)
            scale(g1, SCALE1, "norm1")

            def ada_collect(n):
                d()
                dve.wait_ge(acc_rdy, n + 1)
                dve.transpose(rtf, ada_acc[:, n % 2, 0, :]).then_inc(acc_turned, 1)
                d()
                ins = dve.tensor_reduce(ada_part[:, n, :], rtf.rearrange("p (b c) -> p b c", c=32), AX_X, ALU.add)
                if n == ADA_BLOCKS - 1:
                    ins.then_inc(parts_rdy, 1)
                d()

            def selector(Z):
                d()
                dve.memset(Z[:, 0:224], 0.0)
                d()
                dve.tensor_tensor(Z[:, 96:128], ident[:, 0:32], ident[:, 32:64], ALU.add)
                for c in (64, 96):
                    d()
                    ins = dve.tensor_tensor(Z[:, 96:128], Z[:, 96:128], ident[:, c:c + 32], ALU.add)
                ins.then_inc(sel_rdy, 1)

            def wide(tile):
                return tile.rearrange("p t (h d) -> p (t h) d", d=HD)

            def hg_own(g, B0, s):
                if s == 5:
                    dve.wait_ge(q_sig, g + 1)
                    dve.scalar_tensor_tensor(out=QN[:, :, :], in0=PS[:, 0:2, :], scalar=SCALE, in1=KN[:, :, :],
                                             op0=ALU.mult, op1=ALU.mult).then_inc(pair_read[0], 1)
                if s == 14:
                    dve.wait_ge(hg_tr, 2 * g + 2)
                    for h in range(GH):
                        hh = GH * g + h
                        ins = dve.tensor_scalar(E0[:, h, :], bank(h // 2, S * (h % 2), S * (h % 2) + S),
                                                lb1[:, hh:hh + 1], lb[:, hh:hh + 1], ALU.mult, ALU.add)
                    ins.then_inc(pair_read[0], 1)
                    d()
                    dve.tensor_scalar(kT[:, :, :], E0[:, :, :], -1.0, 1.0, ALU.mult, ALU.add).then_inc(f_rdy, 1)

            def hg_stage(g, B0, s):
                if s == 0:
                    dve.wait_ge(f_log, g + 1)
                    dve.memset(AM[:, 0:2, :, :], 0.0)
                    for h in range(GH):
                        for t in range(T):
                            dve.tensor_tensor_scan(bT[:, h, P * t:P * t + P], ones[:, :], E0[:, h, P * t:P * t + P],
                                                   0.0, ALU.mult, ALU.add)
                    d()
                if s == 1:
                    dve.wait_ge(g_sig, g + 1)
                    dve.tensor_tensor(GN[:, :, :], PS[:, 2:4, :], GN[:, :, :], ALU.mult).then_inc(pair_read[1], 1)
                d()
                bf = bT[:, :, :].rearrange("p h s -> p (h s)")
                Ef = [e.rearrange("p h s -> p (h s)") for e in (E0[:, :, :], E1)]

                def halves(flat, l):
                    w = P if l == 1 else LEVELS[l - 2]
                    v = flat.rearrange("p (n two w) -> p n two w", two=2, w=w)
                    return v[:, :, 0, :], v[:, :, 1, :], w

                if 1 <= s < NLV:
                    lo_b, hi_b, w = halves(bf, s)
                    lo_e, hi_e, _ = halves(Ef[s % 2], s)
                    mid = lo_b[:, :, w - 1:w].to_broadcast(list(lo_b.shape))
                    dve.tensor_tensor(lo_e, mid, lo_b, ALU.subtract)
                    if s == 1:
                        dve.tensor_copy(hi_e, hi_b).then_inc(diff_rdy, 1)
                    else:
                        dve.tensor_tensor(hi_e, hi_b, mid, ALU.subtract).then_inc(diff_rdy, 1)
                if 1 <= s - 1 < NLV:
                    l = s - 1
                    dve.wait_ge(exp_rdy, 8 * g + l)
                    dve.wait_ge(lv_mm, NLV * g + l)
                    lo_e, hi_e, _ = halves(Ef[l % 2], l)
                    lo_k, _, _ = halves(kT[:, :, :].rearrange("p h s -> p (h s)"), l)
                    _, hi_q, _ = halves(qT[:, :, :].rearrange("p h s -> p (h s)"), l)
                    lo_o, hi_o, _ = halves(QK.rearrange("p h s -> p (h s)"), l)
                    dve.tensor_tensor(lo_o, lo_k, lo_e, ALU.mult)
                    dve.tensor_tensor(hi_o, hi_q, hi_e, ALU.mult).then_inc(lv_rdy, 1)
                if 0 <= s - 2 < NLV:
                    l = s - 2
                    dve.wait_ge(lv_mm, NLV * g + l + 1)
                    b = level_bank(l)
                    if l == 1:
                        dve.tensor_copy(AM[:, 2, :, :].rearrange("p h s -> p (h s)"), bank(b)).then_inc(lv_cp, 1)
                    else:
                        src = PS[:, b:b + 2, :].rearrange("p b (h s) -> p (b h) s", s=P)
                        m = lv_mask[:, 0 if l == 0 else l - 1, :].unsqueeze(1).to_broadcast([P, 2 * GH, P])
                        dve.copy_predicated(AM[:, 0:2, :, :].rearrange("p r h s -> p (r h) s"), m,
                                            src).then_inc(lv_cp, 1)
                        d()
                if s == 11:
                    dve.wait_ge(o_sq, g + 1)
                    e1w = E1.rearrange("p h s -> p (h s)").rearrange("p (n d) -> p n d", d=HD)
                    dve.tensor_reduce(ssq[:, 0:8], e1w, AX_X, ALU.add)
                    rsqrt(dve, 8, 1.0 / HD, EPS)
                    dve.tensor_tensor(e1w, wide(PS[:, 6:8, :]), rstd[:, 0:8].unsqueeze(2).to_broadcast([P, 8, HD]), ALU.mult)
                    d()
                    dve.tensor_tensor(MIX[:, :, AW + NC_ * g:AW + NC_ * (g + 1)],
                                      E1.rearrange("p h s -> p (h s)").rearrange("p (t n) -> p t n", t=T),
                                      GN[:, :, :], ALU.mult).then_inc(o_out, 1)

            def head_norm(n, which, tile, b, w, scale2, rope):
                dve.wait_ge(sq_act, 2 * n + which + 1)
                dve.tensor_reduce(ssq[:, 0:8], wide(tile[:, :, :]), AX_X, ALU.add)
                rsqrt(dve, 8, scale2 / HD, scale2 * EPS)
                dve.tensor_tensor(wide(tile[:, :, :]), wide(PS[:, b:b + 2, :]),
                                  rstd[:, 0:8].unsqueeze(2).to_broadcast([P, 8, HD]), ALU.mult)
                d()
                ins = dve.tensor_tensor(wide(tile[:, :, :]), wide(tile[:, :, :]),
                                        w[:, :].unsqueeze(1).to_broadcast([P, 8, HD]), ALU.mult)
                if rope:
                    d()
                    for t in range(T):
                        v = tile[:, t, :].rearrange("p (h d) -> p h d", d=HD)
                        x1, x2 = v[:, :, 0:HALF], v[:, :, HALF:2 * HALF]
                        c, s_ = (z[:, t, :].unsqueeze(1).to_broadcast([P, GH, HALF]) for z in (cos, sin))
                        r = [rt[:, i, GH * HALF * t:GH * HALF * (t + 1)].rearrange("p (h f) -> p h f", f=HALF) for i in range(4)]
                        for i, (x, y) in enumerate(((x1, c), (x2, s_), (x2, c), (x1, s_))):
                            dve.tensor_tensor(r[i], x, y, ALU.mult)
                    d()
                    for t in range(T):
                        v = tile[:, t, :].rearrange("p (h d) -> p h d", d=HD)
                        r = [rt[:, i, GH * HALF * t:GH * HALF * (t + 1)].rearrange("p (h f) -> p h f", f=HALF) for i in range(4)]
                        dve.tensor_tensor(v[:, :, 0:HALF], r[0], r[1], ALU.subtract)
                        ins = dve.tensor_tensor(v[:, :, HALF:2 * HALF], r[2], r[3], ALU.add)
                ins.then_inc(n_rdy, 1)

            def at_own(n, B0, s, rope):
                if s == 4:
                    head_norm(n, 0, QN, 0, wq_b, 1.0 / SCALE ** 2, rope)
                if s == 8:
                    head_norm(n, 1, KN, 2, wk_b, 1.0, rope)

            E0f = E0[:, :, :].rearrange("p h s -> p (h s)")
            AMf = AM[:, :, :, :].rearrange("p r h s -> p (r h s)")

            def diag(x):
                return x.rearrange("p (b c) -> p b c", c=P)[:, 0:3:2, :]

            def at_stage(n, s, stick, col):
                d()
                if s >= 4 and s % 2 == 0 and s <= 2 * GH + 2:
                    h = s // 2 - 2
                    dve.wait_ge(pv_mm, 4 * n + h + 1)
                    dst, src = MIX[:, :, col(h)], bank(7, 0, 2 * HD).rearrange("p (t d) -> p t d", t=T)
                    if stick:
                        dve.tensor_copy(dst, src).then_inc(pv_out, 1)
                    else:
                        dve.tensor_tensor(dst, src, rl[:, h % 2, :].unsqueeze(2).to_broadcast([P, T, HD]),
                                          ALU.mult).then_inc(pv_out, 1)
                if s >= 2 and s % 2 == 0 and s <= 2 * GH:
                    h = s // 2 - 1
                    if stick:
                        dve.wait_ge(p_exp, 4 * n + h + 1)
                        dve.scalar_tensor_tensor(out=E0f[:, 384:768], in0=bank(6, 0, 384), scalar=0.0,
                                                 in1=E0f[:, 0:384], op0=ALU.max, op1=ALU.add)
                        dve.scalar_tensor_tensor(out=AMf[:, 384:768], in0=bank(6, 0, 384), scalar=0.0,
                                                 in1=E0f[:, 0:384], op0=ALU.min, op1=ALU.subtract).then_inc(s_max, 1)
                        d()
                        dve.tensor_tensor(diag(E0f[:, 384:768]), diag(E0f[:, 384:768]),
                                          above[:, :].unsqueeze(1).to_broadcast([P, 2, P]), ALU.mult).then_inc(p_rdy, 1)
                        dve.tensor_tensor(diag(AMf[:, 384:768]), diag(AMf[:, 384:768]),
                                          neg_s[:, :].unsqueeze(1).to_broadcast([P, 2, P]), ALU.add)
                        d()
                    else:
                        dve.wait_ge(s_mm, 4 * n + h + 1)
                        dve.tensor_tensor(E0f[:, 0:384], bank(6, 0, 384), maskadd[:, :], ALU.add)
                        d()
                        dve.tensor_reduce(mx[:, 0:1], E0f[:, 0:128], AX_X, ALU.max)
                        dve.tensor_reduce(mx[:, 1:2], E0f[:, 128:384], AX_X, ALU.max)
                        d()
                        dve.tensor_scalar(nmx[:, :], mx[:, :], -1.0, None, ALU.mult).then_inc(s_max, 1)
                        dve.wait_ge(p_exp, 4 * n + h + 1)
                        for t, (c0, c1_) in enumerate(((0, 128), (128, 384))):
                            pp = E0f[:, 384 + c0:384 + c1_]
                            ins = dve.tensor_tensor_reduce(pp, pp, count[:, c0:c1_], 1.0, 0.0, ALU.mult, ALU.add,
                                                           l_[:, t:t + 1])
                        ins.then_inc(p_rdy, 1)
                        d()
                        dve.reciprocal(rl[:, h % 2, :], l_[:, :])
                        d()
                if stick and s >= 3 and s % 2 == 1 and s <= 2 * GH + 1:
                    h = (s - 3) // 2
                    dve.wait_ge(pT_mm, 4 * n + h + 1)
                    dve.tensor_tensor(AMf[:, 0:384], AMf[:, 384:768], bank(7, 0, 384), ALU.subtract).then_inc(arg_rdy, 1)

            turn_dve(dve, 0, g1, mod[:, SHIFT1, :], GN,
                     between={1: lambda: split_lo(dve, 0, 0), 4: lambda: split_lo(dve, 0, 1)})
            for j in (2, 3):
                split_lo(dve, 0, j)
            dve.wait_ge(bcast_in, 32)
            groups = proj_groups()
            for i, (kind, idx, B0, nb) in enumerate(groups):
                for s in range(CH * nb):
                    if i:
                        pk, pi, pB, _ = groups[i - 1]
                        if pk == "hg":
                            hg_stage(pi, pB, s)
                        else:
                            at_stage(pi, s, False, lambda h: slice(NC_ * pi + HD * h, NC_ * pi + HD * (h + 1)))
                    hg_own(idx, B0, s) if kind == "hg" else at_own(idx, B0, s, True)
                    split_lo(dve, B0 + s // CH + 1, s % CH)
                    if s % CH == 2 and B0 + s // CH >= 1:
                        ada_collect(B0 + s // CH - 1)

            def tail(n, stick, col, turn, g_, steps, banks, B, splits, collects):
                turn_dve(dve, turn, g_, zero_c, GN, steps, 0, banks)
                for s in range(2, 12):
                    at_stage(n, s, stick, col)
                    if 0 <= s - 3 < splits:
                        split_lo(dve, B + 1 + (s - 3) // CH, (s - 3) % CH)
                    if s in collects:
                        ada_collect(collects[s])
                d()

            tail(AT_GROUPS - 1, False, lambda h: slice(AW - NC_ + HD * h, AW - NC_ + HD * (h + 1)), 1, gmix, EARLY1,
                 (0, 1, 2, 3), OUT0, CH, {5: OUT0 - 1, 8: OUT0, 11: OUT0 + 1})
            for t in range(T):
                d()
                dve.tensor_tensor_reduce(QN[:, :, :].rearrange("p t n -> p (t n)"), MIX[:, t, 0:AW], MIX[:, t, 0:AW],
                                         1.0, 0.0, ALU.mult, ALU.add, ssq[:, t:t + 1])
            rsqrt(dve, T, 1.0 / AW, EPS)
            turn_dve(dve, 1, gmix, zero_c, GN, LATE1, len(EARLY1), NARROW)
            selector(MIX[:, 0, :])
            dve.wait_ge(mod_mm, 1)
            modulation(GATE1, GATE2 + 1)
            scale(g2, SCALE2, "norm2")

            def gate_block(n, b, sec, dst):
                dve.tensor_tensor(dst.rearrange("p (k c) -> p k c", c=P), ident[:, :].unsqueeze(1).to_broadcast([P, 4, P]),
                                  mod[:, sec, 4 * b:4 * b + 4].unsqueeze(2).to_broadcast([P, 4, P]),
                                  ALU.mult).then_inc(gate_diag, 1)

            def out_block(b):
                dve.wait_ge(gate_rdy, b + 1)
                dve.wait_ge(x_in, 32)
                dve.wait_ge(chunk_done, CH * OUT0 + last_of(OUT_ORDER, b))
                p = b % 3
                dve.tensor_tensor(VN[:, :, :], PS[:, 2 * p:2 * p + 2, :],
                                  (QN, KN)[b // 2][:, b % 2, :].unsqueeze(1).to_broadcast([P, T, NC_]),
                                  ALU.mult).then_inc(pair_read[p], 1)
                d()
                xs = X[:, :, NC_ * b:NC_ * (b + 1)]
                dve.tensor_tensor(xs, xs, VN[:, :, :], ALU.add)
                block_squares(b)
                d()

            for b in range(4):
                if b >= 2:
                    dve.wait_ge(gate_mm, b - 1)
                gate_block(b, b, GATE1, GN[:, b % 2, :])
                if b % 2:
                    for j in (b - 1, b):
                        split_lo(dve, OUT0 + 2, j)
            for j in range(CH):
                if j % 2 == 0:
                    out_block(j // 2)
                split_lo(dve, OUT0 + 3, j)
            out_block(2)
            for j in range(3):
                split_lo(dve, MLP0, j)
            out_block(3)

            def mlp(m, M, total):
                def up(B, U):
                    for j in range(CH):
                        split_lo(dve, B + 1, j)
                    dve.wait_ge(relu_rdy, U + 1)
                    if not isinstance(U, int) or U:
                        dve.wait_ge(h_tr, U)
                    dve.tensor_tensor(SQ[:, :, :], PS[:, 0:2, :], RE[:, :, :], ALU.mult).then_inc(sq_rdy, 1)

                def turn(U, par):
                    dve.wait_ge(h_hi, U + 1)
                    flat = "p k s -> p (k s)"
                    dve.tensor_tensor(H_lo[:, par, :, :].rearrange(flat), PS[:, 6:8, :],
                                      H_hi[:, par, :, :].rearrange(flat).bitcast(F32), ALU.subtract).then_inc(h_lo, 1)

                def down(B, U, par):
                    for j in range(CH):
                        split_lo(dve, B + 1, j)
                        ac = total[:, :, NC_ * j:NC_ * (j + 1)]
                        b = pairs[1 + j % 2]
                        dve.tensor_tensor(ac, ac, PS[:, b:b + 2, :], ALU.add).then_inc(acc_read, 1)
                        if j == 1 and par is not None:
                            turn(U + 1, par)

                up(M, NU * m)
                turn(NU * m, 0)
                dve.wait_ge(acc_read, 4 * NU * m + 2 * (m + 1))
                with dve.Fori(0, NU // 2 - 1) as i:
                    for e in range(2):
                        up(M + 1 + 4 * i + 2 * e, NU * m + 1 + 2 * i + e)
                        down(M + 2 + 4 * i + 2 * e, NU * m + 2 * i + e, (e + 1) % 2)
                up(M + 2 * NU - 3, NU * m + NU - 1)
                down(M + 2 * NU - 2, NU * m + NU - 2, (NU - 1) % 2)

            root_of_blocks()
            turn_dve(dve, 2, g2, mod[:, SHIFT2, :], SQ)
            split_lo(dve, MLP0, 3)
            mlp(0, MLP0, ACC)
            d()
            gate_block(4, 0, GATE2, DG[:, 0, :])
            for b in range(4):
                cols = slice(NC_ * b, NC_ * (b + 1))
                if b < 3:
                    dve.wait_ge(gate_mm, 4 + b)
                    gate_block(4 + b + 1, b + 1, GATE2, DG[:, (b + 1) % 2, :])
                if b in (1, 2):
                    split_lo(dve, QKV0, b - 1)
                dve.wait_ge(chunk_done, 4 * (QKV0 - 1) + b + 1)
                pb, gb = pairs[1 + b % 2], (SQ, RE)[b // 2][:, b % 2, :]
                dve.tensor_tensor(ACC[:, :, cols], ACC[:, :, cols], PS[:, pb:pb + 2, :], ALU.add).then_inc(acc_read, 1)
                dve.wait_ge(gate_rdy, 4 + b + 1)
                d()
                dve.tensor_tensor(ACC[:, :, cols], ACC[:, :, cols], gb.unsqueeze(1).to_broadcast([P, T, NC_]), ALU.mult)
                d()
                dve.tensor_tensor(X[:, :, cols], X[:, :, cols], ACC[:, :, cols], ALU.add)
                block_squares(b)
            root_of_blocks()
            turn_dve(dve, 3, colB[:, RB["nmix"][0]:RB["nmix"][0] + KT], zero_c, GN)
            for j in (2, 3):
                split_lo(dve, QKV0, j)
            dve.wait_ge(sbw_in, 32)

            def sb_cols(g):
                return lambda h: bass.ds(NC_ * g + HD * h, HD)

            def sb_group(g, first):
                B0 = QKV0 + 3 * g
                for s in range(12):
                    if not first:
                        at_stage(AT_GROUPS + g - 1, s, True, sb_cols(g - 1))
                    at_own(AT_GROUPS + g, B0, s, False)
                    split_lo(dve, B0 + s // CH + 1, s % CH)

            sb_group(0, True)
            start_jobs = jobs.n
            with dve.Fori(1, SB_GROUPS) as g:
                jobs.base, jobs.n = start_jobs + 2 * (g - 1), 0
                sb_group(g, False)
            jobs.base, jobs.n = 0, start_jobs + 2 * (SB_GROUPS - 1)
            d()
            tail(AT_GROUPS + SB_GROUPS - 1, True, sb_cols(SB_GROUPS - 1), 4, one_c, EARLY4, (0, 1, 2, 3), WO0, 2 * CH, {})
            turn_dve(dve, 4, one_c, zero_c, GN, LATE4, len(EARLY4), NARROW)

            def wo_block(b):
                dve.wait_ge(chunk_done, CH * WO0 + last_of(WO_ORDER, b))
                xs, p = X[:, :, NC_ * b:NC_ * (b + 1)], b % 3
                dve.tensor_tensor(xs, xs, PS[:, 2 * p:2 * p + 2, :], ALU.add).then_inc(pair_read[p], 1)
                block_squares(b)

            for j in range(CH):
                split_lo(dve, WO0 + 3, j)
                if j < 3:
                    wo_block(j)
            for j in range(3):
                split_lo(dve, MLP1, j)
            wo_block(3)
            root_of_blocks()
            turn_dve(dve, 5, colB[:, RB["nmlp"][0]:RB["nmlp"][0] + KT], zero_c, SQ)
            split_lo(dve, MLP1, 3)
            dve.memset(ssq[:, 0:1], 1.0).then_inc(acc_read, 2)
            mlp(1, MLP1, X)
            for b in range(4):
                cols, pb = slice(NC_ * b, NC_ * (b + 1)), pairs[1 + b % 2]
                dve.wait_ge(chunk_done, 4 * (END - 1) + b + 1)
                dve.tensor_tensor(X[:, :, cols], X[:, :, cols], PS[:, pb:pb + 2, :], ALU.add).then_inc(acc_read, 1)

        @block.tensor
        def _(pe):
            used = [0, 0, 0]

            def take(p):
                if not isinstance(used[p], int) or used[p]:
                    pe.wait_ge(pair_read[p], used[p])
                used[p] = used[p] + 1

            pe.wait_ge(pool_const, N_CONST)
            pe.wait_ge(params_in, 16 * 11)
            pe.transpose(bank(6, 0, P), setup[:, 0:P], ident[:, :])
            pe.transpose(bank(6, P, P + NRB), setup[0:NRB, P:2 * P], ident[0:NRB, 0:NRB]).then_inc(pe_const, 1)
            pe.wait_ge(dve_const, 1)
            for h in range(2):
                pe.wait_ge(ada_used, CH + KT * (h + 1))
                for k in range(KT):
                    mm = pe.matmul(bank(6, KT * h + k, KT * h + k + 1), MS[:, h, k * P:k * P + P],
                                   ones[:, 0:1], start=True, stop=True)
                mm.then_inc(ada_sum, 1)

            def mod_columns(n0, n1, Z):
                pe.wait_ge(sel_rdy, 1)
                for r in range(4):
                    rhs = ada_part[:, n0:n1, :].rearrange("p n (c r) -> p (n c) r", r=4)[:, :, r]
                    mm = pe.matmul(bank(6, 0, 4 * (n1 - n0)), Z[:, 96 - 32 * r:224 - 32 * r], rhs,
                                   start=r == 0, stop=r == 3)
                mm.then_inc(mod_mm, 1)

            def turn_group(src, first_bank):
                for i in range(2):
                    for q in range(4):
                        h, t = 2 * i + q // 2, q % 2
                        mm = pe.transpose(bank(first_bank + i, P * q, P * q + P), src[:, t, HD * h:HD * (h + 1)], ident[:, :])
                return mm

            def hg_own(g, s):
                if s == 10:
                    take(1)
                    turn_group(QN, 2).then_inc(hg_tr, 1)
                if s == 13:
                    take(0)
                    turn_group(KN, 0).then_inc(hg_tr, 1)

            def hg_stage(g, s):
                l = 0 if s == 0 else s - 1
                if s == 0 or 1 <= l < NLV:
                    b = level_bank(l)
                    if l == 0:
                        pe.wait_ge(f_rdy, g + 1)
                        pe.wait_ge(pair_read[1], 3 * g + 2)
                        if g:
                            pe.wait_ge(o_out, g)
                        else:
                            pe.wait_ge(a_lo, KT // 2)
                    else:
                        pe.wait_ge(lv_rdy, 8 * g + l)
                        before = {1: 0, 2: 1, 3: 2, 4: 3, 5: 4, 6: 5, 7: 7, 8: 8}[l]
                        if NLV * g + before:
                            pe.wait_ge(lv_cp, NLV * g + before)
                    for h in range(GH):
                        if l == 1:
                            mm = pe.matmul(bank(b, P * h, P * h + P), QK[:, h, 0:P], QK[:, h, P:S], start=True, stop=True)
                        else:
                            for t in range(T):
                                k_, q_ = (kT, qT) if l == 0 else (QK, QK)
                                cols = slice(P * t, P * t + P)
                                mm = pe.matmul(bank(b + t, P * h, P * h + P), k_[:, h, cols], q_[:, h, cols], start=True, stop=True)
                    mm.then_inc(lv_mm, 1)
                if s == 10:
                    pe.wait_ge(lv_cp, NLV * (g + 1))
                    pe.wait_ge(pair_read[0], 3 * g + 2)
                    for h in range(GH):
                        cols = slice(HD * h, HD * (h + 1))
                        pe.matmul(bank(6, P * h, P * h + P), AM[:, 0, h, :], VN[:, 0, cols], start=True, stop=True)
                        pe.matmul(bank(7, P * h, P * h + P), AM[:, 2, h, :], VN[:, 0, cols], start=True, stop=False)
                        mm = pe.matmul(bank(7, P * h, P * h + P), AM[:, 1, h, :], VN[:, 1, cols], start=False, stop=True)
                    mm.then_inc(o_mm, 1)

            def at_own(n, s):
                if s == 9:
                    pe.wait_ge(n_rdy, 2 * n + 1)
                    turn_group(QN, 0).then_inc(n_tr, 1)
                if s == 10:
                    pe.wait_ge(n_rdy, 2 * n + 2)
                    turn_group(KN, 2).then_inc(n_tr, 1)

            E0f = E0[:, :, :].rearrange("p h s -> p (h s)")
            AMf = AM[:, :, :, :].rearrange("p r h s -> p (r h s)")

            def at_stage(n, s, stick):
                if s >= 1 and s % 2 == 1 and s <= 2 * GH - 1:
                    h = s // 2
                    if h == 0:
                        if isinstance(n, int) and n == 0:
                            pe.wait_ge(o_out, HG_GROUPS)
                        elif stick:
                            pe.wait_ge(a_lo, 4 * KT // 2)
                    if not (isinstance(n, int) and n == 0 and h == 0):
                        pe.wait_ge(p_rdy, 4 * n + h)
                    if stick:
                        pe.matmul(bank(6, 0, S), kT[:, h, 0:P], qT[:, h, :], start=True, stop=True)
                        mm = pe.matmul(bank(6, S, S + P), kT[:, h, P:S], qT[:, h, P:S], start=True, stop=True)
                    else:
                        pe.matmul(bank(6, 0, P), qT[:, h, 0:P], kT[:, h, 0:P], start=True, stop=True)
                        mm = pe.matmul(bank(6, P, 3 * P), qT[:, h, P:S], kT[:, h, :], start=True, stop=True)
                    mm.then_inc(s_mm, 1)
                if s >= 2 and s % 2 == 0 and s <= 2 * GH:
                    h = s // 2 - 1
                    pe.wait_ge(p_rdy, 4 * n + h + 1)
                    if not (isinstance(n, int) and n == 0 and h == 0):
                        pe.wait_ge(pv_out, 4 * n + h)
                    if stick:
                        L = E0f[:, 384:768]
                        pe.matmul(bank(7, 0, P), below[:, :], L[:, 0:P], start=True, stop=True)
                        pe.matmul(bank(7, P, S), below[:, :], L[:, P:S], start=True, stop=False)
                        pe.matmul(bank(7, P, S), ones[:, :], L[:, S:S + P], start=False, stop=True)
                        mm = pe.matmul(bank(7, S, S + P), below[:, :], L[:, S:S + P], start=True, stop=True)
                    else:
                        for i in range(3):
                            mm = pe.transpose(bank(7, P * i, P * i + P), E0f[:, 384 + P * i:512 + P * i], ident[:, :])
                    mm.then_inc(pT_mm, 1)
                if s >= 3 and s % 2 == 1 and s <= 2 * GH + 1:
                    h = (s - 3) // 2
                    cols = slice(HD * h, HD * (h + 1))
                    if h == 0:
                        pe.wait_ge(pair_read[2], n + 1)
                    pe.wait_ge(pT_rdy, 4 * n + h + 1)
                    pe.matmul(bank(7, 0, HD), AMf[:, 0:P], VN[:, 0, cols], start=True, stop=True)
                    pe.matmul(bank(7, HD, 2 * HD), AMf[:, P:2 * P], VN[:, 0, cols], start=True, stop=False)
                    pe.matmul(bank(7, HD, 2 * HD), AMf[:, 2 * P:3 * P], VN[:, 1, cols], start=False, stop=True).then_inc(pv_mm, 1)

            def turn(n, src, **parts):
                turn_pe(pe, n, src, **parts)

            pe.wait_ge(mod_rdy, 1)
            turn(0, Y0)
            groups = proj_groups()
            for i, (kind, idx, B0, nb) in enumerate(groups):
                prev_used = list(used)
                for s in range(CH * nb):
                    p = (s // CH) % 2 if kind == "hg" else s // CH
                    if s % CH == 0:
                        take(p)
                        if p == 2 and idx == 0:
                            pe.wait_ge(lv_cp, NLV * (HG_GROUPS - 1) + 6)
                    a_chunk(pe, B0 + s // CH, s % CH, pairs[p], 0 if i == 0 and s < CH else None)
                    if i:
                        pk, pi, pB, _ = groups[i - 1]
                        if pk == "hg":
                            hg_stage(pi, s)
                        else:
                            if s == 1:
                                for p in range(2):
                                    pe.wait_ge(pair_read[p], prev_used[p])
                            at_stage(pi, s, False)
                    (hg_own if kind == "hg" else at_own)(idx, s)

            def tail(n, stick, turned, steps, B, order, early):
                for p in range(2):
                    pe.wait_ge(pair_read[p], used[p])
                at_stage(n, 1, stick)
                if turned == 4:
                    pe.wait_ge(pv_out, 4 * n)
                turn(turned, MIX, steps=steps, banks=(0, 1, 2, 3))
                for s in range(2, 12):
                    at_stage(n, s, stick)
                    if s - 2 < early:
                        pe.wait_ge(a_lo, KT // 2 * turned + min(len(steps), 2 * (s - 1)))
                        if s == 2:
                            pe.wait_ge(a_lo, KT // 2 * turned + len(steps))
                        square_chunk(pe, B, order, s - 2, take)

            tail(AT_GROUPS - 1, False, 1, EARLY1, OUT0, OUT_ORDER, OUT_EARLY)

            def gate_spread(n, b, diag):
                pe.wait_ge(gate_diag, n + 1)
                if b >= 2:
                    pe.wait_ge(gate_rdy, n - 1)
                pe.matmul(bank(6 + b % 2), ones[:, :], diag, start=True, stop=True).then_inc(gate_mm, 1)

            pe.wait_ge(pv_out, 4 * AT_GROUPS)
            turn(1, MIX, steps=LATE1, first=len(EARLY1), banks=NARROW)
            pe.wait_ge(a_lo, 2 * KT // 2)
            mod_columns(0, ADA_BLOCKS, MIX[:, 0, :])
            for pos in range(OUT_EARLY, CH * 4):
                square_chunk(pe, OUT0, OUT_ORDER, pos, take)
                if pos < OUT_EARLY + 2:
                    pe.wait_ge(mod_rdy, 2)
                    for b in (2 * (pos - OUT_EARLY), 2 * (pos - OUT_EARLY) + 1):
                        gate_spread(b, b, GN[:, b % 2, :])

            def mlp(m, M):
                def up(B, U, turned=None):
                    if not isinstance(U, int) or U:
                        pe.wait_ge(sq_rdy, U)
                    for j in range(CH):
                        a_chunk(pe, B, j, 0, turned)

                def turn_unit(U):
                    pe.wait_ge(sq_rdy, U + 1)
                    if not isinstance(U, int) or U:
                        pe.wait_ge(h_lo, U)
                    turn_group(SQ, 6).then_inc(h_tr, 1)

                def down(B, U, par, turn_next, gates=False):
                    pe.wait_ge(h_lo, U + 1)
                    for j in range(CH):
                        if gates:
                            gate_spread(4 + j, j, DG[:, j % 2, :])
                        pe.wait_ge(acc_read, 4 * U + 2 * m + j + 1)
                        chunk(pe, B, j, pairs[1 + j % 2], lambda k, t: H_hi[:, par, k, P * t:P * t + P],
                              lambda k, t: H_lo[:, par, k, P * t:P * t + P], True, True)
                        if j == 1 and turn_next:
                            turn_unit(U + 1)

                up(M, NU * m, (2, 5)[m])
                turn_unit(NU * m)
                with pe.Fori(0, NU // 2 - 1) as i:
                    for e in range(2):
                        up(M + 1 + 4 * i + 2 * e, NU * m + 1 + 2 * i + e)
                        down(M + 2 + 4 * i + 2 * e, NU * m + 2 * i + e, e, True)
                up(M + 2 * NU - 3, NU * m + NU - 1)
                down(M + 2 * NU - 2, NU * m + NU - 2, 0, True)
                down(M + 2 * NU - 1, NU * m + NU - 1, 1, False, m == 0)

            turn(2, ACC)
            mlp(0, MLP0)
            turn(3, MIX)

            def sb_group(base, g, first):
                B0, n = QKV0 + 3 * g, AT_GROUPS + g
                used[0], used[1], used[2] = base[0] + g, base[1] + g, base[2] + g
                for s in range(12):
                    if s % CH == 0:
                        take(s // CH)
                    a_chunk(pe, B0 + s // CH, s % CH, pairs[s // CH], 3 if first and s < CH else None)
                    if not first:
                        if s == 1:
                            for p in range(2):
                                pe.wait_ge(pair_read[p], base[p] + g)
                        at_stage(n - 1, s, True)
                    at_own(n, s)

            base = list(used)
            sb_group(base, 0, True)
            with pe.Fori(1, SB_GROUPS) as g:
                sb_group(base, g, False)
            for p in range(3):
                used[p] = base[p] + SB_GROUPS
            tail(AT_GROUPS + SB_GROUPS - 1, True, 4, EARLY4, WO0, WO_ORDER, WO_EARLY)
            pe.wait_ge(pv_out, 4 * (AT_GROUPS + SB_GROUPS))
            turn(4, MIX, steps=LATE4, first=len(EARLY4), banks=NARROW)
            pe.wait_ge(a_lo, 5 * KT // 2)
            for pos in range(WO_EARLY, CH * 4):
                square_chunk(pe, WO0, WO_ORDER, pos, take)
            turn(5, ACC)
            mlp(1, MLP1)


def level_bank(l):
    return 4 if l in (1, 3, 5) else 6


def proj_groups():
    g = [("hg", i, PROJ0 + 4 * i, 4) for i in range(HG_GROUPS)]
    return g + [("at", i, PROJ0 + 4 * HG_GROUPS + 3 * i, 3) for i in range(AT_GROUPS)]


def proj_columns():
    cols = [3 * AW + part * HW + g * NC_ for g in range(HG_GROUPS) for part in range(4)]
    return cols + [part * AW + g * NC_ for g in range(AT_GROUPS) for part in range(3)]


_INS = ["x", "c", "positions", "norm1_w", "w_ada", "b_ada", "w_in", "q_norm_w", "k_norm_w", "attn_out_norm_w",
        "hg_lb_logits", "hg_norm_w", "w_out", "norm2_w", "w_ff1", "w_ff2", "norm_mix_g_2", "norm_mlp_g_2",
        "sb_w_qkv_2", "sb_q_norm_g_2", "sb_k_norm_g_2", "sb_w_o_2", "mlp_w_in_2", "mlp_w_out_2"]


def kernel(**inputs):
    from concourse import bacc
    from concourse.bass_utils import run_bass_kernel_spmd

    nc = bacc.Bacc("TRN2", target_bir_lowering=False, num_devices=1, dynamic_dma_scratch_size=1024)
    arrays, args = {}, {}
    for name in _INS:
        arr = np.ascontiguousarray(inputs[name])
        arrays[f"in_{name}_dram"] = arr
        args[name] = nc.dram_tensor(f"in_{name}_dram", arr.shape, mybir.dt.from_np(arr.dtype), kind="ExternalInput").ap()
    out = nc.dram_tensor("out_dram", (1, S, D), F32, kind="ExternalOutput").ap()
    build(nc, args, out)
    r = run_bass_kernel_spmd(nc, [arrays], core_ids=[0])
    return r.results[0]["out_dram"]
```

```python
from contextlib import ExitStack

import concourse.bass as bass
import numpy as np
from concourse import mybir

F32 = mybir.dt.float32
F32R = mybir.dt.float32r
I32 = mybir.dt.int32
U8 = mybir.dt.uint8
ALU = mybir.AluOpType
ACT = mybir.ActivationFunctionType
AX_X = mybir.AxisListType.X

P = 128
S, D = 256, 2048
T = S // P
KT = D // P
NC_ = 512
CH = 4
HD = 128
GH = NC_ // HD
AW = D // 2
HW = D - AW
NU = 4 * D // NC_
EPS = 1e-6
HALF = HD // 8
THETA = 500000.0
NEG = -1e30
SCALE = float(HD) ** -0.5

HG_GROUPS, AT_GROUPS, SB_GROUPS = HW // NC_, AW // NC_, D // NC_
PROJ0 = 0
OUT0 = PROJ0 + 4 * HG_GROUPS + 3 * AT_GROUPS
MLP0 = OUT0 + D // NC_
QKV0 = MLP0 + 2 * NU
WO0 = QKV0 + 3 * SB_GROUPS
MLP1 = WO0 + D // NC_
END = MLP1 + 2 * NU

RA = {"b_ada": (0, 96), "norm1": (96, 16), "norm2": (112, 16)}
RB = {"attn_out": (0, 8), "hgw": (8, 1), "lb": (9, 16), "nmix": (25, 16), "nmlp": (41, 16), "c": (57, 16)}
NRB = 73
SHIFT1, SCALE1, GATE1, SHIFT2, SCALE2, GATE2 = range(6)
ADA_BLOCKS = 4 * D // NC_
OUT_EARLY, WO_EARLY = 6, 9
ADA_SLOTS = 4 * ADA_BLOCKS
OUT_ORDER = [(b, k) for b in range(3) for k in (2, 3)] + [(b, k) for b in range(3) for k in (0, 1)] + \
            [(3, k) for k in (2, 3, 0, 1)]
WO_ORDER = [(b, k) for b in range(3) for k in (0, 1, 2)] + [(b, 3) for b in range(3)] + [(3, k) for k in range(4)]


def ada_quarters(slot):
    return [slot] if slot < ADA_SLOTS else []


def ada_collected(slot):
    return [q // 4 for q in ada_quarters(slot - 3) if q % 4 == 3] if slot >= 3 else []


WIDE, NARROW, TAIL = (6, 7, 4, 5, 2, 3), (6, 7), (2, 3, 7, 4, 5)
EARLY1, LATE1 = (4, 5, 6, 7), (0, 1, 2, 3)
EARLY4, LATE4 = (0, 1, 2, 3, 4, 5), (6, 7)
ALL = tuple(range(KT // 2))
PIECES_BEFORE = {0: 0, 1: 4, 2: 6}
POWER_OF = {0: 1, 1: 2 + HG_GROUPS + 2 * AT_GROUPS}
POWER_OF.update({2: POWER_OF[1] + 1, 3: POWER_OF[1] + 2, 5: POWER_OF[1] + 3 + 2 * SB_GROUPS})
LEVELS = (64, 32, 16, 8, 4, 2, 1)
NLV = 2 + len(LEVELS)


def build(nc, a, out):
    ctx = ExitStack()
    with ctx:
        def sb(name, shape, dt=F32, c=ctx):
            return c.enter_context(nc.sbuf_tensor(name, shape, dt))

        def sem(name):
            return ctx.enter_context(nc.semaphore(name))

        X = sb("X", [P, T, D])
        A_hi, A_lo = sb("A_hi", [P, KT, S], F32R), sb("A_lo", [P, KT, S], F32R)
        raw = sb("raw", [P, CH, CH, NC_])
        w_hi, w_lo = sb("w_hi", [P, CH, CH, NC_], F32R), sb("w_lo", [P, CH, CH, NC_], F32R)
        ident, ones = sb("ident", [P, P]), sb("ones", [P, P])
        neg_s = sb("neg_s", [P, P])
        below, above = sb("below", [P, P]), sb("above", [P, P])
        count, maskadd = sb("count", [P, 3 * P]), sb("maskadd", [P, 3 * P])
        lv_mask = sb("lv_mask", [P, 1 + len(LEVELS), P], U8)
        wq_b, wk_b = sb("wq_b", [P, P]), sb("wk_b", [P, P])
        colA, colB = sb("colA", [P, P]), sb("colB", [P, NRB])
        mod = sb("mod", [P, 6, KT])
        g1, g2, gmix, zero_c, one_c = (sb(n, [P, KT]) for n in ("g1", "g2", "gmix", "zero_c", "one_c"))
        sc = sb("sc", [P, KT])
        lb, lb1 = sb("lb", [P, 8]), sb("lb1", [P, 8])
        cos, sin = sb("cos", [P, T, HALF]), sb("sin", [P, T, HALF])
        rt = sb("rt", [P, 4, T * GH * HALF])
        ssq, rstd, mhalf = sb("ssq", [P, 8]), sb("rstd", [P, 8]), sb("mhalf", [P, 8])
        ssq_blocks = sb("ssq_blocks", [P, D // NC_, T])
        row_r = sb("row_r", [P, T])
        mx, nmx, l_, rl = sb("mx", [P, T]), sb("nmx", [P, T]), sb("l_", [P, T]), sb("rl", [P, 2, T])
        ada_acc = sb("ada_acc", [P, 2, 2, NC_])
        ada_part = sb("ada_part", [P, ADA_BLOCKS, NC_ // 32])
        over = ExitStack()
        MIX = sb("MIX", [P, T, D], c=over)
        QN, KN, VN, GN = (sb(n, [P, T, NC_], c=over) for n in ("QN", "KN", "VN", "GN"))
        qT, bT, kT, E0 = (sb(n, [P, GH, S], c=over) for n in ("qT", "bT", "kT", "E0"))
        AM = sb("AM", [P, 3, GH, P], c=over)
        over.close()
        start = ExitStack()
        MS = sb("MS", [P, 2, D], c=start)
        ada_raw = sb("ada_raw", [P, CH, D], c=start)
        start.close()
        H_hi, H_lo = sb("H_hi", [P, 2, CH, S], F32R), sb("H_lo", [P, 2, CH, S], F32R)
        ACC = sb("ACC", [P, T, D])
        RE, SQ = sb("RE", [P, T, NC_]), sb("SQ", [P, T, NC_])
        ada_ring = X[:, :, :].rearrange("p t (h c n) -> p (t h) c n", c=2, n=NC_)
        DT = ada_acc[:, 1, :, :]
        DG = ada_acc[:, 0, :, :]
        Y0 = raw[:, 2:4, :, :].rearrange("p j k n -> p j (k n)")
        setup = MS[:, :, :].rearrange("p a n -> p (a n)")
        E1 = MIX[:, 0, 0:D // 2].rearrange("p (h s) -> p h s", h=GH)
        QK = MIX[:, 1, 0:D // 2].rearrange("p (h s) -> p h s", h=GH)

        PS = ctx.enter_context(nc.psum_tensor("PS", [P, 8, NC_], F32))

        params_in, bcast_in, x_in = sem("params_in"), sem("bcast_in"), sem("x_in")
        sbw_in = sem("sbw_in")
        raw_in = [sem(f"raw_in{j}") for j in range(CH)]
        hi_rdy, lo_rdy, chunk_done = sem("hi_rdy"), sem("lo_rdy"), sem("chunk_done")
        pool_const, dve_const, act_const, pe_const = (sem(n) for n in ("pool_const", "dve_const", "act_const", "pe_const"))
        ada_in = [sem(f"ada_in{j}") for j in range(CH)]
        ada_used, ada_sum, arg_rdy = sem("ada_used"), sem("ada_sum"), sem("arg_rdy")
        ring_in = [sem(f"ring_in{j}") for j in range(CH)]
        parts_rdy, prod_rdy, acc_rdy = sem("parts_rdy"), sem("prod_rdy"), sem("acc_rdy")
        ring_used, acc_turned, sel_rdy, mod_mm, mod_rdy = (sem(n) for n in ("ring_used", "acc_turned", "sel_rdy", "mod_mm", "mod_rdy"))
        sum_rdy, rstd_rdy = sem("sum_rdy"), sem("rstd_rdy")
        y_rdy, x_block, row_rdy = sem("y_rdy"), sem("x_block"), sem("row_rdy")
        a_tr, a_aff, a_hi, a_lo = sem("a_tr"), sem("a_aff"), sem("a_hi"), sem("a_lo")
        pair_read = [sem(f"pair_read{i}") for i in range(3)]
        gate_diag, gate_mm, gate_rdy = sem("gate_diag"), sem("gate_mm"), sem("gate_rdy")
        relu_rdy, sq_rdy, h_tr, h_hi, h_lo, acc_read = (sem(n) for n in ("relu_rdy", "sq_rdy", "h_tr", "h_hi", "h_lo", "acc_read"))
        q_sig, f_rdy, f_log, g_sig = (sem(n) for n in ("q_sig", "f_rdy", "f_log", "g_sig"))
        hg_tr, diff_rdy, exp_rdy, lv_rdy, lv_mm, lv_cp = (sem(n) for n in ("hg_tr", "diff_rdy", "exp_rdy", "lv_rdy", "lv_mm", "lv_cp"))
        o_mm, o_sq, o_out = sem("o_mm"), sem("o_sq"), sem("o_out")
        sq_act, n_rdy, n_tr = sem("sq_act"), sem("n_rdy"), sem("n_tr")
        s_mm, s_max, p_exp, p_rdy, pT_mm, pT_rdy, pv_mm, pv_out = (
            sem(n) for n in ("s_mm", "s_max", "p_exp", "p_rdy", "pT_mm", "pT_rdy", "pv_mm", "pv_out"))
        stored = sem("stored")

        pairs = (0, 2, 4)

        def bank(i, lo=0, hi=NC_):
            return PS[:, i, lo:hi]

        def heads_t(tile, i):
            return tile[:, 2 * i:2 * i + 2, :].rearrange("p h s -> p (h s)")

        def split_hi(act, B, j):
            act.wait_ge(raw_in[j], 16 * (B + 1))
            if not isinstance(B, int) or B >= 1:
                act.wait_ge(chunk_done, 4 * (B - 1) + j + 1)
            act.activation(w_hi[:, j, :, :], raw[:, j, :, :], ACT.Copy).then_inc(hi_rdy, 1)

        def split_lo(dve, B, j):
            dve.wait_ge(hi_rdy, 4 * B + j + 1)
            dve.tensor_tensor(w_lo[:, j, :, :], raw[:, j, :, :], w_hi[:, j, :, :].bitcast(F32),
                              ALU.subtract).then_inc(lo_rdy, 1)

        def chunk(pe, B, j, pair, hi, lo, start, stop):
            pe.wait_ge(lo_rdy, 4 * B + j + 1)
            for t in range(T):
                for k in range(CH):
                    h, l = hi(k, t), lo(k, t)
                    first, last = start and k == 0, stop and k == CH - 1
                    pe.matmul(bank(pair + t), h, w_hi[:, j, k, :], start=first, stop=False)
                    pe.matmul(bank(pair + t), h, w_lo[:, j, k, :], start=False, stop=False)
                    mm = pe.matmul(bank(pair + t), l, w_hi[:, j, k, :], start=False, stop=last)
            mm.then_inc(chunk_done, 1)

        def square_chunk(pe, B0, order, pos, take):
            b, k = order[pos]
            mine = [x for x, (b_, _) in enumerate(order) if b_ == b]
            if pos == mine[0]:
                take(b % 3)
            chunk(pe, B0 + pos // CH, pos % CH, pairs[b % 3], lambda i, t: A_hi[:, CH * k + i, P * t:P * t + P],
                  lambda i, t: A_lo[:, CH * k + i, P * t:P * t + P], pos == mine[0], pos == mine[-1])

        def last_of(order, b):
            return max(x for x, (b_, _) in enumerate(order) if b_ == b) + 1

        def a_chunk(pe, B, j, pair, turned=None):
            if turned is not None:
                pe.wait_ge(a_lo, KT // 2 * turned + 2 * (j + 1))
            chunk(pe, B, j, pair, lambda k, t: A_hi[:, CH * j + k, P * t:P * t + P],
                  lambda k, t: A_lo[:, CH * j + k, P * t:P * t + P], j == 0, j == CH - 1)

        def turn_pe(pe, n, src, steps=ALL, first=0, banks=WIDE):
            for pos, i in enumerate(steps):
                if n in PIECES_BEFORE and pos % 2 == 0 and not (n == 1 and first == 0):
                    pe.wait_ge(y_rdy, PIECES_BEFORE[n] + pos // 2 + 1)
                if pos >= len(banks):
                    pe.wait_ge(a_aff, KT // 2 * n + first + pos - len(banks) + 1)
                for q in range(4):
                    kt, t = 2 * i + q // 2, q % 2
                    mm = pe.transpose(bank(banks[pos % len(banks)], P * q, P * q + P), src[:, t, kt * P:kt * P + P], ident[:, :])
                mm.then_inc(a_tr, 1)

        def block_steps(b):
            return {"steps": (2 * b, 2 * b + 1), "first": 2 * b}

        def normalise(act, src, dst, c):
            for t in range(T):
                cols = slice(NC_ * c, NC_ * c + NC_)
                ins = act.activation(dst[:, t, cols], src[:, t, cols], ACT.Copy, scale=rstd[:, t:t + 1])
            ins.then_inc(y_rdy, 1)

        def turn_act(act, n, tmp, steps=ALL, first=0, norm=None, between=None):
            if norm:
                act.wait_ge(rstd_rdy, POWER_OF[n])
                for c in (0, 1):
                    normalise(act, *norm, c)
            for pos, i in enumerate(steps):
                if norm and pos in (2, 4) and 2 * len(steps) == KT:
                    normalise(act, *norm, pos // 2 + 1)
                act.wait_ge(a_aff, KT // 2 * n + first + pos + 1)
                act.activation(A_hi[:, 2 * i:2 * i + 2, :].rearrange("p k s -> p (k s)"), tmp[:, pos % 2, :],
                               ACT.Copy).then_inc(a_hi, 1)
                if between and pos in between:
                    between[pos]()

        def turn_dve(dve, n, g, s, tmp, steps=ALL, first=0, banks=WIDE, between=None):
            dve.drain()
            for pos in range(len(steps) + 1):
                if pos < len(steps):
                    i = steps[pos]
                    dve.wait_ge(a_tr, KT // 2 * n + first + pos + 1)
                    if pos >= 2:
                        dve.wait_ge(a_lo, KT // 2 * n + first + pos - 1)
                    for k in range(2):
                        kt = 2 * i + k
                        ins = dve.tensor_scalar(tmp[:, pos % 2, S * k:S * k + S],
                                                bank(banks[pos % len(banks)], S * k, S * k + S),
                                                g[:, kt:kt + 1], s[:, kt:kt + 1], ALU.mult, ALU.add)
                    ins.then_inc(a_aff, 1)
                if pos:
                    i = steps[pos - 1]
                    dve.wait_ge(a_hi, KT // 2 * n + first + pos)
                    flat = "p k s -> p (k s)"
                    dve.tensor_tensor(A_lo[:, 2 * i:2 * i + 2, :].rearrange(flat), tmp[:, (pos - 1) % 2, :],
                                      A_hi[:, 2 * i:2 * i + 2, :].rearrange(flat).bitcast(F32),
                                      ALU.subtract).then_inc(a_lo, 1)
                    if between and pos - 1 in between:
                        between[pos - 1]()
            dve.drain()

        class Jobs:
            def __init__(self):
                self.base, self.n = 0, 0

        jobs = Jobs()

        def rsqrt(dve, w, mul, add, meanwhile=None):
            dve.drain()
            dve.tensor_scalar(ssq[:, 0:w], ssq[:, 0:w], mul, add, ALU.mult, ALU.add).then_inc(sum_rdy, 1)
            jobs.n += 1
            if meanwhile:
                meanwhile()
            dve.wait_ge(rstd_rdy, jobs.base + jobs.n)

        block = ctx.enter_context(nc.Block())

        @block.sync
        def _(sp):
            pa, pb = setup[:, 0:P], setup[:, P:2 * P]
            rows = [(pa, RA["b_ada"], a["b_ada"]), (pa, RA["norm1"], a["norm1_w"]), (pa, RA["norm2"], a["norm2_w"]),
                    (pb, RB["attn_out"], a["attn_out_norm_w"]), (pb, RB["hgw"], a["hg_norm_w"]),
                    (pb, RB["lb"], a["hg_lb_logits"]), (pb, RB["nmix"], a["norm_mix_g_2"]),
                    (pb, RB["nmlp"], a["norm_mlp_g_2"]), (pb, RB["c"], a["c"])]
            for tile, (r0, n), src in rows:
                sp.dma_start(tile[r0:r0 + n, :], src.rearrange("a (r p) -> (a r) p", p=P)).then_inc(params_in, 16)
            for t in range(T):
                sp.dma_start(rt[:, 0, t:t + 1].bitcast(I32),
                             a["positions"][0:1, P * t:P * t + P].rearrange("a (p b) -> (a p) b", b=1)).then_inc(params_in, 16)
            sp.dma_start(wq_b[:, :], a["q_norm_w"].to_broadcast([P, P])).then_inc(bcast_in, 16)
            sp.dma_start(wk_b[:, :], a["k_norm_w"].to_broadcast([P, P])).then_inc(bcast_in, 16)
            sp.dma_start(X[:, :, :], a["x"].rearrange("a (t p) d -> p (a t) d", p=P)).then_inc(x_in, 16)
            ada = a["w_ada"].rearrange("a (k p) (s n) -> p (a k) s n", p=P, n=D)
            with sp.Fori(0, 2) as i:
                for k in range(KT):
                    sp.wait_ge(ada_used, KT * i + k + 1)
                    sp.dma_start(ada_raw[:, k % CH, :], ada[:, k, i, :]).then_inc(ada_in[k % CH], 16)

            def load(B, j, src):
                if isinstance(B, int) and B == 0 and j == 2:
                    sp.wait_ge(a_tr, KT // 2)
                if not isinstance(B, int) or B >= 1:
                    sp.wait_ge(lo_rdy, 4 * (B - 1) + j + 1)
                sp.dma_start(raw[:, j, :, :], src).then_inc(raw_in[j], 16)

            ada_b = a["w_ada"].rearrange("a (k p) (b n) -> p (a k) b n", p=P, n=NC_)

            sp.wait_ge(y_rdy, 4)

            def ada_load(quarter):
                for q in (2 * quarter, 2 * quarter + 1):
                    n = q // 8
                    if q >= CH:
                        sp.wait_ge(ring_used, q - CH + 1)
                    sp.dma_start(ada_ring[:, q % CH, :, :],
                                 ada_b[:, 2 * (q % 8):2 * (q % 8) + 2, 2 * D // NC_ + n, :]).then_inc(ring_in[q % CH], 16)

            w_in = a["w_in"].rearrange("a (j k p) n -> p (a j) k n", j=CH, p=P)
            for B, c0 in enumerate(proj_columns()):
                for j in range(CH):
                    load(B, j, w_in[:, j, :, c0:c0 + NC_])
                    if B:
                        for quarter in ada_quarters(CH * (B - 1) + j):
                            ada_load(quarter)

            def mlp(M, w1, w2):
                v1 = w1.rearrange("a (j k p) (u n) -> p (a j) k u n", j=CH, p=P, n=NC_)
                v2 = w2.rearrange("a (u k p) (j n) -> p (a u) k j n", k=CH, p=P, n=NC_)

                def up(B, u):
                    for j in range(CH):
                        load(B, j, v1[:, j, :, u, :])

                def down(B, u):
                    for j in range(CH):
                        load(B, j, v2[:, u, :, j, :])

                up(M, 0)
                with sp.Fori(0, NU - 1) as u:
                    up(M + 1 + 2 * u, u + 1)
                    down(M + 2 + 2 * u, u)
                down(M + 2 * NU - 1, NU - 1)

            def square(B0, w, order, ada):
                v = w.rearrange("a (j k p) (b n) -> p (a j) k b n", j=CH, p=P, n=NC_)
                for pos, (b, k) in enumerate(order):
                    B, j = B0 + pos // CH, pos % CH
                    load(B, j, v[:, k, :, b, :])
                    if ada and B <= OUT0 + 1:
                        for quarter in ada_quarters(CH * (B - 1) + j):
                            ada_load(quarter)
                    if ada and pos == 2 * CH - 1:
                        for slot in range(CH * (OUT0 + 1), ADA_SLOTS):
                            for quarter in ada_quarters(slot):
                                ada_load(quarter)
                        sp.wait_ge(ring_used, 8 * ADA_BLOCKS)
                        sp.dma_start(X[:, :, :], a["x"].rearrange("a (t p) d -> p (a t) d", p=P)).then_inc(x_in, 16)

            def mlp(M, w1, w2):
                v1 = w1.rearrange("a (j k p) (u n) -> p (a j) k u n", j=CH, p=P, n=NC_)
                v2 = w2.rearrange("a (u k p) (j n) -> p (a u) k j n", k=CH, p=P, n=NC_)

                def up(B, u):
                    for j in range(CH):
                        load(B, j, v1[:, j, :, u, :])

                def down(B, u):
                    for j in range(CH):
                        load(B, j, v2[:, u, :, j, :])

                up(M, 0)
                with sp.Fori(0, NU - 1) as u:
                    up(M + 1 + 2 * u, u + 1)
                    down(M + 2 + 2 * u, u)
                down(M + 2 * NU - 1, NU - 1)

            w_out = a["w_out"].rearrange("a (j k p) (b n) -> p (a j) k b n", j=CH, p=P, n=NC_)
            square(OUT0, a["w_out"], OUT_ORDER, True)
            mlp(MLP0, a["w_ff1"], a["w_ff2"])
            qkv = a["sb_w_qkv_2"].rearrange("a (j k p) (s g n) -> p (a j) k s g n", j=CH, p=P, s=3, n=NC_)
            sp.dma_start(wq_b[:, 0:1], a["sb_q_norm_g_2"].rearrange("a (p b) -> (a p) b", b=1)).then_inc(sbw_in, 16)
            sp.dma_start(wk_b[:, 0:1], a["sb_k_norm_g_2"].rearrange("a (p b) -> (a p) b", b=1)).then_inc(sbw_in, 16)
            with sp.Fori(0, SB_GROUPS) as g:
                for s_ in range(3):
                    for j in range(CH):
                        load(QKV0 + 3 * g + s_, j, qkv[:, j, :, s_, g, :])
            square(WO0, a["sb_w_o_2"], WO_ORDER, False)
            mlp(MLP1, a["mlp_w_in_2"], a["mlp_w_out_2"])
            for b in range(D // NC_):
                cols = slice(NC_ * b, NC_ * b + NC_)
                sp.wait_ge(acc_read, 4 * 2 * NU + 2 * 2 - 3 + b)
                sp.dma_start(out[:, :, cols].rearrange("a (t p) n -> p (a t) n", p=P), X[:, :, cols]).then_inc(stored, 16)
            sp.wait_ge(stored, 16 * D // NC_)

        ints = setup[:, 256:1024].bitcast(I32)
        dist, tmp_i = ints[:, 0:384], ints[:, 384:768]
        rows_i, cols_i, xor_i = (setup[:, c:c + P].bitcast(I32) for c in (1024, 1152, 1280))
        f_a, f_b = setup[:, 1408:1792], setup[:, 1792:2176]
        invf = setup[:, 2176:2176 + HALF]
        pos_i = rt[:, 0, 0:T].bitcast(I32)
        ang = setup[:, 2304:2304 + T * HALF].rearrange("p (t f) -> p t f", t=T)
        kk = setup[:, 2432:2432 + T * HALF].rearrange("p (t f) -> p t f", t=T)
        posf, lbt = setup[:, 2500:2502], setup[:, 2560:2584]

        N_CONST = 15
        JOBS = 1 + HG_GROUPS + 2 * AT_GROUPS + 1 + 1 + 1 + 2 * SB_GROUPS + 1

        @block.gpsimd
        def _(pool):
            def const(ins):
                ins.then_inc(pool_const, 1)

            const(pool.memset(ident[:, :], 0.0))
            const(pool.memset(ones[:, :], 1.0))
            const(pool.memset(below[:, :], 1.0))
            const(pool.memset(above[:, :], 1.0))
            const(pool.memset(mhalf[:, :], -0.5))
            const(pool.memset(zero_c[:, :], 0.0))
            const(pool.memset(one_c[:, :], 1.0))
            for f in range(HALF):
                ins = pool.memset(invf[:, f:f + 1], float(np.float32(THETA ** (-2.0 * f / (2 * HALF)))))
            const(ins)
            pool.wait_ge(pool_const, 8)
            const(pool.affine_select(out=ident[:, :], in_=ident[:, :], compare_op=ALU.not_equal, fill=1.0,
                                     base=0, pattern=[[-1, P]], channel_multiplier=1))
            const(pool.affine_select(out=below[:, :], in_=below[:, :], compare_op=ALU.is_gt, fill=0.0,
                                     base=0, pattern=[[-1, P]], channel_multiplier=1))
            const(pool.affine_select(out=above[:, :], in_=above[:, :], compare_op=ALU.is_gt, fill=0.0,
                                     base=0, pattern=[[1, P]], channel_multiplier=-1))
            const(pool.iota(dist[:, 0:P], pattern=[[-1, P]], base=S, channel_multiplier=1))
            const(pool.iota(dist[:, P:3 * P], pattern=[[-1, 2 * P]], base=S + P, channel_multiplier=1))
            const(pool.iota(rows_i, pattern=[[0, P]], base=0, channel_multiplier=1))
            const(pool.iota(cols_i, pattern=[[1, P]], base=0, channel_multiplier=0))

            def power(i):
                pool.wait_ge(sum_rdy, i + 1)
                pool.tensor_tensor(rstd[:, :], ssq[:, :], mhalf[:, :], ALU.pow).then_inc(rstd_rdy, 1)

            def ada_sums(quarter):
                n, j = quarter // 4, quarter % 4
                acc = ada_acc[:, n % 2, :, :]
                for q in (2 * quarter, 2 * quarter + 1):
                    w = ada_ring[:, q % CH, :, :]
                    pool.wait_ge(prod_rdy, q + 1)
                    if q % 8 == 0:
                        continue
                    if q % 8 == 1:
                        if n >= 2:
                            pool.wait_ge(acc_turned, n - 1)
                        pool.tensor_tensor(acc, ada_ring[:, (q - 1) % CH, :, :], w, ALU.add).then_inc(ring_used, 2)
                    else:
                        pool.tensor_tensor(acc, acc, w, ALU.add).then_inc(ring_used, 1)
                    pool.drain()
                if j == CH - 1:
                    pool.tensor_tensor(acc[:, 0, :], acc[:, 0, :], acc[:, 1, :], ALU.add).then_inc(acc_rdy, 1)

            power(0)
            done = 1
            groups = proj_groups()
            for i, (kind, idx, B0, nb) in enumerate(groups):
                for s in range(CH * nb):
                    if (i and groups[i - 1][0] == "hg" and s == 11) or (kind == "at" and s in (4, 8)):
                        power(done)
                        done += 1
                    for quarter in ada_quarters(CH * B0 + s):
                        ada_sums(quarter)
            for slot in range(CH * OUT0, ADA_SLOTS - 1):
                for quarter in ada_quarters(slot):
                    ada_sums(quarter)
            power(done)
            for quarter in ada_quarters(ADA_SLOTS - 1):
                ada_sums(quarter)
            power(done + 1)
            pool.wait_ge(a_tr, 3 * KT // 2)
            for t in range(T):
                pool.memset(ACC[:, t, :], 0.0).then_inc(acc_read, 1)
            for b in range(D // NC_):
                cols = slice(NC_ * b, NC_ * b + NC_)
                pool.wait_ge(acc_read, 2 + 4 * (NU - 1) + b + 1)
                pool.wait_ge(gate_rdy, 4 + b + 1)
                pool.tensor_tensor(ACC[:, :, cols], ACC[:, :, cols],
                                   (SQ, RE)[b // 2][:, b % 2, :].unsqueeze(1).to_broadcast([P, T, NC_]), ALU.mult)
                pool.drain()
                pool.tensor_tensor(X[:, :, cols], X[:, :, cols], ACC[:, :, cols], ALU.add).then_inc(x_block, 1)
            with pool.Fori(done + 2, JOBS) as i:
                power(i)

        @block.scalar
        def _(act):
            act.wait_ge(dve_const, 1)
            act.activation(sc[:, :], colB[:, RB["c"][0]:NRB], ACT.Sigmoid).then_inc(act_const, 1)
            act.wait_ge(dve_const, 2)
            act.activation(lbt[:, 0:16], lbt[:, 0:16], ACT.Exp).then_inc(act_const, 1)
            act.wait_ge(dve_const, 3)
            act.activation(sin[:, :, :], ang, ACT.Sin).then_inc(act_const, 1)
            act.activation(cos[:, :, :], ang, ACT.Sin, scale=0.5).then_inc(act_const, 1)

            def ada_products(quarter):
                for q in (2 * quarter, 2 * quarter + 1):
                    act.wait_ge(ring_in[q % CH], 16 * (q // CH + 1))
                    for c in range(2):
                        k, w = 2 * (q % 8) + c, ada_ring[:, q % CH, c, :]
                        ins = act.activation(w, w, ACT.Copy, scale=sc[:, k:k + 1])
                    ins.then_inc(prod_rdy, 1)

            def hg_own(g, B0, s):
                if s == 4:
                    act.wait_ge(chunk_done, 4 * (B0 + 1))
                    act.activation(KN[:, :, :], PS[:, 0:2, :], ACT.Sigmoid).then_inc(q_sig, 1)
                if s == 8:
                    act.wait_ge(chunk_done, 4 * (B0 + 2))
                    act.wait_ge(pair_read[0], 3 * g + 1)
                    act.activation(KN[:, :, :], PS[:, 2:4, :], ACT.Sigmoid).then_inc(pair_read[1], 1)
                if s == 11:
                    act.wait_ge(hg_tr, 2 * g + 1)
                    if g:
                        act.wait_ge(lv_rdy, 8 * g)
                    for i in range(2):
                        c = act.activation(heads_t(qT, i), bank(2 + i), ACT.Copy)
                    c.then_inc(pair_read[1], 1)
                if s == 12:
                    act.wait_ge(chunk_done, 4 * (B0 + 3))
                    if g:
                        act.wait_ge(o_mm, g)
                    act.activation(VN[:, :, :], PS[:, 0:2, :], ACT.Copy).then_inc(pair_read[0], 1)
                if s == 15:
                    act.wait_ge(f_rdy, g + 1)
                    act.activation(E0[:, :, :], E0[:, :, :], ACT.Ln).then_inc(f_log, 1)

            def hg_stage(g, B0, s):
                if s == 0:
                    act.wait_ge(chunk_done, 4 * (B0 + 4))
                    if g:
                        act.wait_ge(o_out, g)
                    act.activation(GN[:, :, :], PS[:, 2:4, :], ACT.Sigmoid).then_inc(g_sig, 1)
                if 1 <= s < NLV:
                    E = (E0, E1)[s % 2]
                    act.wait_ge(diff_rdy, 8 * g + s)
                    act.activation(E[:, :, :], E[:, :, :], ACT.Exp).then_inc(exp_rdy, 1)
                if s == 11:
                    act.wait_ge(o_mm, g + 1)
                    act.activation(E1.rearrange("p h s -> p (h s)"), PS[:, 6:8, :], ACT.Square).then_inc(o_sq, 1)

            def from_pair(dst, p, func, by_row):
                if not by_row:
                    return act.activation(dst[:, :, :], PS[:, 2 * p:2 * p + 2, :], func)
                for t in range(T):
                    ins = act.activation(dst[:, t, :], bank(2 * p + t), func, scale=row_r[:, t:t + 1])
                return ins

            def at_own(n, B0, s, by_row=False):
                if s == 4:
                    if by_row:
                        act.wait_ge(row_rdy, 1)
                        act.wait_ge(sbw_in, 32)
                    act.wait_ge(chunk_done, 4 * (B0 + 1))
                    from_pair(QN, 0, ACT.Square, by_row).then_inc(sq_act, 1)
                if s == 8:
                    act.wait_ge(chunk_done, 4 * (B0 + 2))
                    from_pair(KN, 1, ACT.Square, by_row).then_inc(sq_act, 1)
                if s == 10:
                    act.wait_ge(n_tr, 2 * n + 1)
                    if isinstance(n, int) and n == 0:
                        act.wait_ge(lv_rdy, 8 * HG_GROUPS)
                    else:
                        act.wait_ge(s_mm, 4 * n)
                    for i in range(2):
                        c = act.activation(heads_t(qT, i), bank(i), ACT.Copy, scale=wq_b[:, 0:1] if by_row else 1.0)
                    c.then_inc(pair_read[0], 1)
                if s == 11:
                    act.wait_ge(n_tr, 2 * n + 2)
                    for i in range(2):
                        c = act.activation(heads_t(kT, i), bank(2 + i), ACT.Copy, scale=wk_b[:, 0:1] if by_row else 1.0)
                    c.then_inc(pair_read[1], 1)

            E0f = E0[:, :, :].rearrange("p h s -> p (h s)")
            AMf = AM[:, :, :, :].rearrange("p r h s -> p (r h s)")

            def at_stage(n, B0, s, stick):
                if s == 0:
                    act.wait_ge(chunk_done, 4 * (B0 + 3))
                    if isinstance(n, int) and n == 0:
                        act.wait_ge(o_mm, HG_GROUPS)
                    else:
                        act.wait_ge(pv_mm, 4 * n)
                    from_pair(VN, 2, ACT.Copy, stick).then_inc(pair_read[2], 1)
                if s >= 2 and s % 2 == 0 and s <= 2 * GH:
                    h = s // 2 - 1
                    if stick:
                        act.wait_ge(s_mm, 4 * n + h + 1)
                        act.activation(E0f[:, 0:384], bank(6, 0, 384), ACT.Abs)
                        act.drain()
                        act.activation(E0f[:, 0:384], E0f[:, 0:384], ACT.Exp, scale=-1.0)
                        act.drain()
                        act.activation(E0f[:, 0:384], E0f[:, 0:384], ACT.Ln, bias=one_c[:, 0:1]).then_inc(p_exp, 1)
                    else:
                        act.wait_ge(s_max, 4 * n + h + 1)
                        act.wait_ge(pT_mm, 4 * n + h)
                        act.activation(E0f[:, 384:512], E0f[:, 0:128], ACT.Exp, bias=nmx[:, 0:1])
                        act.activation(E0f[:, 512:768], E0f[:, 128:384], ACT.Exp, bias=nmx[:, 1:2]).then_inc(p_exp, 1)
                if s >= 3 and s % 2 == 1 and s <= 2 * GH + 1:
                    h = (s - 3) // 2
                    if stick:
                        act.wait_ge(arg_rdy, 4 * (n - AT_GROUPS) + h + 1)
                        act.activation(AMf[:, 0:384], AMf[:, 0:384], ACT.Exp).then_inc(pT_rdy, 1)
                    else:
                        act.wait_ge(pT_mm, 4 * n + h + 1)
                        act.activation(AMf[:, 0:384], bank(7, 0, 384), ACT.Copy).then_inc(pT_rdy, 1)

            act.wait_ge(rstd_rdy, POWER_OF[0])
            for c in range(4):
                normalise(act, X, Y0, c)
            turn_act(act, 0, GN, between={1: lambda: split_hi(act, 0, 0), 4: lambda: split_hi(act, 0, 1)})
            for j in (2, 3):
                split_hi(act, 0, j)
            groups = proj_groups()
            for i, (kind, idx, B0, nb) in enumerate(groups):
                for s in range(CH * nb):
                    if i:
                        pk, pi, pB, _ = groups[i - 1]
                        hg_stage(pi, pB, s) if pk == "hg" else at_stage(pi, pB, s, False)
                    (hg_own if kind == "hg" else at_own)(idx, B0, s)
                    split_hi(act, B0 + s // CH + 1, s % CH)
                    for quarter in ada_quarters(CH * B0 + s):
                        ada_products(quarter)

            def tail(n, B0, stick, turn, steps, B, splits):
                at_stage(n, B0, 0, stick)
                turn_act(act, turn, GN, steps)
                for s in range(2, 12):
                    at_stage(n, B0, s, stick)
                    if 0 <= s - 3 < splits:
                        split_hi(act, B + 1 + (s - 3) // CH, (s - 3) % CH)
                    if turn == 1:
                        for quarter in ada_quarters(CH * OUT0 + s - 2):
                            ada_products(quarter)

            tail(AT_GROUPS - 1, OUT0 - 3, False, 1, EARLY1, OUT0, CH)

            def gate(n, b, dst):
                act.wait_ge(gate_mm, n + 1)
                act.activation(dst, bank(6 + b % 2), ACT.Copy).then_inc(gate_rdy, 1)

            turn_act(act, 1, GN, LATE1, len(EARLY1), norm=(MIX, MIX))
            for j in range(3):
                split_hi(act, OUT0 + 2, j)
            for b in range(4):
                gate(b, b, (QN, KN)[b // 2][:, b % 2, :])
                if b == 1:
                    split_hi(act, OUT0 + 2, 3)
            for B in (OUT0 + 3, OUT0 + 4):
                for j in range(CH):
                    split_hi(act, B, j)

            def mlp(m, M):
                def relu(B, U, pair):
                    act.wait_ge(chunk_done, 4 * (B + 1))
                    if not isinstance(U, int) or U:
                        act.wait_ge(sq_rdy, U)
                    if m == 0:
                        act.activation(RE[:, :, :], PS[:, pair:pair + 2, :], ACT.Relu).then_inc(relu_rdy, 1)
                    else:
                        for t in range(T):
                            ins = act.activation(RE[:, t, :], bank(pair + t), ACT.Relu, scale=rstd[:, t:t + 1])
                        ins.then_inc(relu_rdy, 1)

                def up(B, U):
                    for j in range(CH):
                        split_hi(act, B + 1, j)
                    relu(B, U, 0)

                def turn(U, par):
                    act.wait_ge(h_tr, U + 1)
                    act.activation(H_hi[:, par, :, :].rearrange("p k s -> p (k s)"), PS[:, 6:8, :],
                                   ACT.Copy).then_inc(h_hi, 1)

                def down(B, U, par, end=False):
                    for j in range(CH):
                        if not end:
                            split_hi(act, B + 1, j)
                        if j == 1 and par is not None:
                            turn(U + 1, par)

                for j in range(CH):
                    split_hi(act, M + 1, j)
                if m:
                    act.wait_ge(rstd_rdy, POWER_OF[5])
                relu(M, NU * m, pairs[2])
                for j in range(CH):
                    split_hi(act, M + 2, j)
                    if j == 1:
                        turn(NU * m, 0)
                relu(M + 1, NU * m + 1, 0)
                down(M + 2, NU * m, 1)
                with act.Fori(0, NU // 2 - 1) as i:
                    for e in range(2):
                        up(M + 3 + 4 * i + 2 * e, NU * m + 2 + 2 * i + e)
                        down(M + 4 + 4 * i + 2 * e, NU * m + 1 + 2 * i + e, e)

            turn_act(act, 2, SQ, norm=(X, ACC))
            mlp(0, MLP0)
            for b in range(4):
                gate(4 + b, b, (SQ, RE)[b // 2][:, b % 2, :])
                if b in (1, 2):
                    split_hi(act, QKV0, b - 1)
            for b in (0, 1):
                turn_act(act, 3, DT, **block_steps(b))
            for b in (2, 3):
                split_hi(act, QKV0, b)
                turn_act(act, 3, DT, **block_steps(b))

            def sb_group(g, first):
                B0 = QKV0 + 3 * g
                for s in range(12):
                    if not first:
                        at_stage(AT_GROUPS + g - 1, B0 - 3, s, True)
                    at_own(AT_GROUPS + g, B0, s, True)
                    split_hi(act, B0 + s // CH + 1, s % CH)

            sb_group(0, True)
            with act.Fori(1, SB_GROUPS) as g:
                sb_group(g, False)
            tail(AT_GROUPS + SB_GROUPS - 1, WO0 - 3, True, 4, EARLY4, WO0, 2 * CH)
            turn_act(act, 4, GN, LATE4, len(EARLY4))
            for j in range(CH):
                split_hi(act, WO0 + 3, j)
            for b in range(4):
                split_hi(act, MLP1, b)
                turn_act(act, 5, SQ, **block_steps(b))
            mlp(1, MLP1)

        @block.vector
        def _(dve):
            d = dve.drain

            def root(junk):
                for t in range(T):
                    dve.tensor_tensor_reduce(junk[:, t, :], X[:, t, :], X[:, t, :], 1.0, 0.0, ALU.mult, ALU.add,
                                             ssq[:, t:t + 1])
                rsqrt(dve, T, 1.0 / D, EPS)

            rtf = rt[:, :, :].rearrange("p i n -> p (i n)")

            def block_squares(b, ready=0):
                if ready:
                    dve.wait_ge(x_block, ready)
                for t in range(T):
                    xs = X[:, t, NC_ * b:NC_ * (b + 1)]
                    d()
                    dve.tensor_tensor_reduce(rtf, xs, xs, 1.0, 0.0, ALU.mult, ALU.add, ssq_blocks[:, b, t:t + 1])

            def root_of_blocks():
                d()
                dve.tensor_reduce(ssq[:, 0:T], ssq_blocks[:, :, :].rearrange("p b t -> p t b"), AX_X, ALU.add)
                rsqrt(dve, T, 1.0 / D, EPS)

            for i in range(CH):
                dve.memset(ssq[:, 2 * i:2 * i + 2], 1.0).then_inc(ada_used, 1)
            dve.wait_ge(pool_const, N_CONST)
            dve.wait_ge(pe_const, 1)
            dve.tensor_copy(colA[:, :], bank(6, 0, P))
            dve.tensor_copy(colB[:, :], bank(6, P, P + NRB)).then_inc(dve_const, 1)
            d()
            l0 = RB["lb"][0]
            dve.tensor_tensor(lbt[:, 16:24], colB[:, l0:l0 + 8], colB[:, l0 + 8:l0 + 16], ALU.max)
            d()
            dve.tensor_tensor(lbt[:, 0:8], colB[:, l0:l0 + 8], lbt[:, 16:24], ALU.subtract)
            dve.tensor_tensor(lbt[:, 8:16], colB[:, l0 + 8:l0 + 16], lbt[:, 16:24], ALU.subtract).then_inc(dve_const, 1)
            dve.wait_ge(params_in, 16 * 11)
            dve.tensor_copy(posf, pos_i)
            d()
            for t in range(T):
                dve.tensor_scalar(ang[:, t, :], invf, posf[:, t:t + 1], None, ALU.mult)
            d()
            ROUND = 12582912.0
            dve.tensor_scalar(kk, ang, float(1 / (2 * np.pi)), ROUND, ALU.mult, ALU.add)
            d()
            dve.tensor_scalar(kk, kk, ROUND, None, ALU.subtract)
            d()
            c1 = 6.28125
            c2 = float(np.float32(np.round((2 * np.pi - c1) * 2 ** 21) / 2 ** 21))
            for c in (c1, c2, float(2 * np.pi - c1 - c2)):
                dve.scalar_tensor_tensor(out=ang, in0=kk, scalar=-c, in1=ang, op0=ALU.mult, op1=ALU.add)
                d()
            dve.tensor_scalar(ang, ang, 3.1415925, -3.1415925, ALU.min, ALU.max).then_inc(dve_const, 1)
            for mask, dst in ((3, f_a), (15, f_b)):
                dve.tensor_scalar(tmp_i, dist, mask, None, ALU.bitwise_and)
                d()
                dve.tensor_scalar(dst, tmp_i, 0.0, None, ALU.is_equal)
                d()
            dve.scalar_tensor_tensor(out=f_a, in0=dist, scalar=float(S + P), in1=f_a, op0=ALU.is_le, op1=ALU.add)
            d()
            dve.tensor_tensor(f_a, f_a, f_b, ALU.add)
            d()
            dve.scalar_tensor_tensor(out=count[:, :], in0=dist, scalar=float(S), in1=f_a, op0=ALU.is_ge, op1=ALU.mult)
            d()
            dve.tensor_scalar(maskadd[:, :], count[:, :], 0.5, None, ALU.is_gt)
            d()
            dve.tensor_scalar(maskadd[:, :], maskadd[:, :], -NEG, NEG, ALU.mult, ALU.add)
            dve.tensor_scalar(neg_s[:, :], above[:, :], -NEG, NEG, ALU.mult, ALU.add)
            dve.tensor_tensor(xor_i, rows_i, cols_i, ALU.bitwise_xor)
            d()
            dve.scalar_tensor_tensor(out=f_a[:, 0:P], in0=xor_i, scalar=1.0, in1=above[:, :], op0=ALU.add, op1=ALU.mult)
            dve.tensor_copy(lv_mask[:, 0, :], ident[:, :])
            d()
            for i, w in enumerate(LEVELS):
                dve.tensor_scalar(f_b[:, 0:P], f_a[:, 0:P], w + 1.0, None, ALU.is_ge)
                d()
                dve.scalar_tensor_tensor(out=lv_mask[:, 1 + i, :], in0=f_a[:, 0:P], scalar=2 * w + 1.0,
                                         in1=f_b[:, 0:P], op0=ALU.is_lt, op1=ALU.mult)
                d()
            dve.wait_ge(act_const, 4)
            dve.tensor_tensor(sc[:, :], sc[:, :], colB[:, RB["c"][0]:NRB], ALU.mult)
            dve.tensor_tensor(lbt[:, 16:24], lbt[:, 0:8], lbt[:, 8:16], ALU.add)
            dve.tensor_copy(gmix[:, 0:8], colB[:, 0:8])
            dve.tensor_scalar(gmix[:, 8:16], one_c[:, 0:8], colB[:, 8:9], None, ALU.mult)
            dve.tensor_tensor(cos[:, :, :], cos[:, :, :], cos[:, :, :], ALU.mult)
            d()
            dve.reciprocal(lbt[:, 16:24], lbt[:, 16:24])
            dve.tensor_scalar(cos[:, :, :], cos[:, :, :], -2.0, 1.0, ALU.mult, ALU.add)
            d()
            dve.tensor_tensor(lb[:, :], lbt[:, 0:8], lbt[:, 16:24], ALU.mult)
            dve.tensor_tensor(lb1[:, :], lbt[:, 8:16], lbt[:, 16:24], ALU.mult)
            d()
            dve.wait_ge(x_in, 16)
            root(Y0)
            for h in range(2):
                for k in range(KT):
                    sl = ada_raw[:, k % CH, :]
                    dve.wait_ge(ada_in[k % CH], 16 * (h * (KT // CH) + k // CH + 1))
                    if k == 0:
                        ins = dve.tensor_scalar(MS[:, h, :], sl, sc[:, k:k + 1], None, ALU.mult)
                    else:
                        ins = dve.scalar_tensor_tensor(out=MS[:, h, :], in0=sl, scalar=sc[:, k:k + 1],
                                                       in1=MS[:, h, :], op0=ALU.mult, op1=ALU.add)
                    ins.then_inc(ada_used, 1)
                    dve.wait_ge(ada_used, CH + KT * h + k + 1)

            def modulation(sec0, sec1):
                n = KT * (sec1 - sec0)
                dve.tensor_tensor(mod[:, sec0:sec1, :].rearrange("p s k -> p (s k)"), bank(6, 0, n),
                                  colA[:, KT * sec0:KT * sec1], ALU.add).then_inc(mod_rdy, 1)

            def scale(g_, sec, nm):
                r0 = RA[nm][0]
                d()
                dve.scalar_tensor_tensor(out=g_[:, :], in0=mod[:, sec, :], scalar=1.0, in1=colA[:, r0:r0 + KT],
                                         op0=ALU.add, op1=ALU.mult)

            dve.wait_ge(ada_sum, 2)
            modulation(SHIFT1, GATE1)
            scale(g1, SCALE1, "norm1")

            def ada_collect(n):
                d()
                dve.wait_ge(acc_rdy, n + 1)
                dve.transpose(rtf, ada_acc[:, n % 2, 0, :]).then_inc(acc_turned, 1)
                d()
                ins = dve.tensor_reduce(ada_part[:, n, :], rtf.rearrange("p (b c) -> p b c", c=32), AX_X, ALU.add)
                if n == ADA_BLOCKS - 1:
                    ins.then_inc(parts_rdy, 1)
                d()

            def selector(Z):
                d()
                dve.memset(Z[:, 0:224], 0.0)
                d()
                dve.tensor_tensor(Z[:, 96:128], ident[:, 0:32], ident[:, 32:64], ALU.add)
                for c in (64, 96):
                    d()
                    ins = dve.tensor_tensor(Z[:, 96:128], Z[:, 96:128], ident[:, c:c + 32], ALU.add)
                ins.then_inc(sel_rdy, 1)

            def wide(tile):
                return tile.rearrange("p t (h d) -> p (t h) d", d=HD)

            def hg_own(g, B0, s):
                if s == 5:
                    dve.wait_ge(q_sig, g + 1)
                    dve.scalar_tensor_tensor(out=QN[:, :, :], in0=PS[:, 0:2, :], scalar=SCALE, in1=KN[:, :, :],
                                             op0=ALU.mult, op1=ALU.mult).then_inc(pair_read[0], 1)
                if s == 14:
                    dve.wait_ge(hg_tr, 2 * g + 2)
                    for h in range(GH):
                        hh = GH * g + h
                        ins = dve.tensor_scalar(E0[:, h, :], bank(h // 2, S * (h % 2), S * (h % 2) + S),
                                                lb1[:, hh:hh + 1], lb[:, hh:hh + 1], ALU.mult, ALU.add)
                    ins.then_inc(pair_read[0], 1)
                    d()
                    dve.tensor_scalar(kT[:, :, :], E0[:, :, :], -1.0, 1.0, ALU.mult, ALU.add).then_inc(f_rdy, 1)

            def hg_stage(g, B0, s):
                if s == 0:
                    dve.wait_ge(f_log, g + 1)
                    dve.memset(AM[:, 0:2, :, :], 0.0)
                    for h in range(GH):
                        for t in range(T):
                            dve.tensor_tensor_scan(bT[:, h, P * t:P * t + P], ones[:, :], E0[:, h, P * t:P * t + P],
                                                   0.0, ALU.mult, ALU.add)
                    d()
                if s == 1:
                    dve.wait_ge(g_sig, g + 1)
                    dve.tensor_tensor(GN[:, :, :], PS[:, 2:4, :], GN[:, :, :], ALU.mult).then_inc(pair_read[1], 1)
                d()
                bf = bT[:, :, :].rearrange("p h s -> p (h s)")
                Ef = [e.rearrange("p h s -> p (h s)") for e in (E0[:, :, :], E1)]

                def halves(flat, l):
                    w = P if l == 1 else LEVELS[l - 2]
                    v = flat.rearrange("p (n two w) -> p n two w", two=2, w=w)
                    return v[:, :, 0, :], v[:, :, 1, :], w

                if 1 <= s < NLV:
                    lo_b, hi_b, w = halves(bf, s)
                    lo_e, hi_e, _ = halves(Ef[s % 2], s)
                    mid = lo_b[:, :, w - 1:w].to_broadcast(list(lo_b.shape))
                    dve.tensor_tensor(lo_e, mid, lo_b, ALU.subtract)
                    if s == 1:
                        dve.tensor_copy(hi_e, hi_b).then_inc(diff_rdy, 1)
                    else:
                        dve.tensor_tensor(hi_e, hi_b, mid, ALU.subtract).then_inc(diff_rdy, 1)
                if 1 <= s - 1 < NLV:
                    l = s - 1
                    dve.wait_ge(exp_rdy, 8 * g + l)
                    dve.wait_ge(lv_mm, NLV * g + l)
                    lo_e, hi_e, _ = halves(Ef[l % 2], l)
                    lo_k, _, _ = halves(kT[:, :, :].rearrange("p h s -> p (h s)"), l)
                    _, hi_q, _ = halves(qT[:, :, :].rearrange("p h s -> p (h s)"), l)
                    lo_o, hi_o, _ = halves(QK.rearrange("p h s -> p (h s)"), l)
                    dve.tensor_tensor(lo_o, lo_k, lo_e, ALU.mult)
                    dve.tensor_tensor(hi_o, hi_q, hi_e, ALU.mult).then_inc(lv_rdy, 1)
                if 0 <= s - 2 < NLV:
                    l = s - 2
                    dve.wait_ge(lv_mm, NLV * g + l + 1)
                    b = level_bank(l)
                    if l == 1:
                        dve.tensor_copy(AM[:, 2, :, :].rearrange("p h s -> p (h s)"), bank(b)).then_inc(lv_cp, 1)
                    else:
                        src = PS[:, b:b + 2, :].rearrange("p b (h s) -> p (b h) s", s=P)
                        m = lv_mask[:, 0 if l == 0 else l - 1, :].unsqueeze(1).to_broadcast([P, 2 * GH, P])
                        dve.copy_predicated(AM[:, 0:2, :, :].rearrange("p r h s -> p (r h) s"), m,
                                            src).then_inc(lv_cp, 1)
                        d()
                if s == 11:
                    dve.wait_ge(o_sq, g + 1)
                    e1w = E1.rearrange("p h s -> p (h s)").rearrange("p (n d) -> p n d", d=HD)
                    dve.tensor_reduce(ssq[:, 0:8], e1w, AX_X, ALU.add)
                    rsqrt(dve, 8, 1.0 / HD, EPS)
                    dve.tensor_tensor(e1w, wide(PS[:, 6:8, :]), rstd[:, 0:8].unsqueeze(2).to_broadcast([P, 8, HD]), ALU.mult)
                    d()
                    dve.tensor_tensor(MIX[:, :, AW + NC_ * g:AW + NC_ * (g + 1)],
                                      E1.rearrange("p h s -> p (h s)").rearrange("p (t n) -> p t n", t=T),
                                      GN[:, :, :], ALU.mult).then_inc(o_out, 1)

            def head_norm(n, which, tile, b, w, scale2, rope, by_row, meanwhile):
                dve.wait_ge(sq_act, 2 * n + which + 1)
                dve.tensor_reduce(ssq[:, 0:8], wide(tile[:, :, :]), AX_X, ALU.add)
                rsqrt(dve, 8, scale2 / HD, scale2 * EPS, meanwhile)
                if by_row:
                    r = rstd[:, 0:8].rearrange("p (t h) -> p t h", t=T)
                    dve.tensor_tensor(r, r, row_r[:, :].unsqueeze(2).to_broadcast([P, T, GH]), ALU.mult)
                    d()
                ins = dve.tensor_tensor(wide(tile[:, :, :]), wide(PS[:, b:b + 2, :]),
                                        rstd[:, 0:8].unsqueeze(2).to_broadcast([P, 8, HD]), ALU.mult)
                if rope:
                    d()
                    dve.tensor_tensor(wide(tile[:, :, :]), wide(tile[:, :, :]),
                                      w[:, :].unsqueeze(1).to_broadcast([P, 8, HD]), ALU.mult)
                    d()
                    for t in range(T):
                        v = tile[:, t, :].rearrange("p (h d) -> p h d", d=HD)
                        x1, x2 = v[:, :, 0:HALF], v[:, :, HALF:2 * HALF]
                        c, s_ = (z[:, t, :].unsqueeze(1).to_broadcast([P, GH, HALF]) for z in (cos, sin))
                        r = [rt[:, i, GH * HALF * t:GH * HALF * (t + 1)].rearrange("p (h f) -> p h f", f=HALF) for i in range(4)]
                        for i, (x, y) in enumerate(((x1, c), (x2, s_), (x2, c), (x1, s_))):
                            dve.tensor_tensor(r[i], x, y, ALU.mult)
                    d()
                    for t in range(T):
                        v = tile[:, t, :].rearrange("p (h d) -> p h d", d=HD)
                        r = [rt[:, i, GH * HALF * t:GH * HALF * (t + 1)].rearrange("p (h f) -> p h f", f=HALF) for i in range(4)]
                        dve.tensor_tensor(v[:, :, 0:HALF], r[0], r[1], ALU.subtract)
                        ins = dve.tensor_tensor(v[:, :, HALF:2 * HALF], r[2], r[3], ALU.add)
                ins.then_inc(n_rdy, 1)

            def at_own(n, B0, s, rope):
                meanwhile = lambda: split_lo(dve, B0 + s // CH + 1, s % CH)
                if s == 4:
                    head_norm(n, 0, QN, 0, wq_b, 1.0 / SCALE ** 2, rope, not rope, meanwhile)
                if s == 8:
                    head_norm(n, 1, KN, 2, wk_b, 1.0, rope, not rope, meanwhile)

            E0f = E0[:, :, :].rearrange("p h s -> p (h s)")
            AMf = AM[:, :, :, :].rearrange("p r h s -> p (r h s)")

            def diag(x):
                return x.rearrange("p (b c) -> p b c", c=P)[:, 0:3:2, :]

            def at_stage(n, s, stick, col):
                d()
                if s >= 4 and s % 2 == 0 and s <= 2 * GH + 2:
                    h = s // 2 - 2
                    dve.wait_ge(pv_mm, 4 * n + h + 1)
                    dst, src = MIX[:, :, col(h)], bank(7, 0, 2 * HD).rearrange("p (t d) -> p t d", t=T)
                    if stick:
                        dve.tensor_copy(dst, src).then_inc(pv_out, 1)
                    else:
                        dve.tensor_tensor(dst, src, rl[:, h % 2, :].unsqueeze(2).to_broadcast([P, T, HD]),
                                          ALU.mult).then_inc(pv_out, 1)
                if s >= 2 and s % 2 == 0 and s <= 2 * GH:
                    h = s // 2 - 1
                    if stick:
                        dve.wait_ge(p_exp, 4 * n + h + 1)
                        dve.scalar_tensor_tensor(out=E0f[:, 384:768], in0=bank(6, 0, 384), scalar=0.0,
                                                 in1=E0f[:, 0:384], op0=ALU.max, op1=ALU.add)
                        dve.scalar_tensor_tensor(out=AMf[:, 384:768], in0=bank(6, 0, 384), scalar=0.0,
                                                 in1=E0f[:, 0:384], op0=ALU.min, op1=ALU.subtract).then_inc(s_max, 1)
                        d()
                        dve.tensor_tensor(diag(E0f[:, 384:768]), diag(E0f[:, 384:768]),
                                          above[:, :].unsqueeze(1).to_broadcast([P, 2, P]), ALU.mult).then_inc(p_rdy, 1)
                        dve.tensor_tensor(diag(AMf[:, 384:768]), diag(AMf[:, 384:768]),
                                          neg_s[:, :].unsqueeze(1).to_broadcast([P, 2, P]), ALU.add)
                        d()
                    else:
                        dve.wait_ge(s_mm, 4 * n + h + 1)
                        dve.tensor_tensor(E0f[:, 0:384], bank(6, 0, 384), maskadd[:, :], ALU.add)
                        d()
                        dve.tensor_reduce(mx[:, 0:1], E0f[:, 0:128], AX_X, ALU.max)
                        dve.tensor_reduce(mx[:, 1:2], E0f[:, 128:384], AX_X, ALU.max)
                        d()
                        dve.tensor_scalar(nmx[:, :], mx[:, :], -1.0, None, ALU.mult).then_inc(s_max, 1)
                        dve.wait_ge(p_exp, 4 * n + h + 1)
                        for t, (c0, c1_) in enumerate(((0, 128), (128, 384))):
                            pp = E0f[:, 384 + c0:384 + c1_]
                            ins = dve.tensor_tensor_reduce(pp, pp, count[:, c0:c1_], 1.0, 0.0, ALU.mult, ALU.add,
                                                           l_[:, t:t + 1])
                        ins.then_inc(p_rdy, 1)
                        d()
                        dve.reciprocal(rl[:, h % 2, :], l_[:, :])
                        d()
                if stick and s >= 3 and s % 2 == 1 and s <= 2 * GH + 1:
                    h = (s - 3) // 2
                    dve.wait_ge(pT_mm, 4 * n + h + 1)
                    dve.tensor_tensor(AMf[:, 0:384], AMf[:, 384:768], bank(7, 0, 384), ALU.subtract).then_inc(arg_rdy, 1)

            turn_dve(dve, 0, g1, mod[:, SHIFT1, :], GN,
                     between={1: lambda: split_lo(dve, 0, 0), 4: lambda: split_lo(dve, 0, 1)})
            for j in (2, 3):
                split_lo(dve, 0, j)
            dve.wait_ge(bcast_in, 32)
            groups = proj_groups()
            for i, (kind, idx, B0, nb) in enumerate(groups):
                for s in range(CH * nb):
                    if i:
                        pk, pi, pB, _ = groups[i - 1]
                        if pk == "hg":
                            hg_stage(pi, pB, s)
                        else:
                            at_stage(pi, s, False, lambda h: slice(NC_ * pi + HD * h, NC_ * pi + HD * (h + 1)))
                    hg_own(idx, B0, s) if kind == "hg" else at_own(idx, B0, s, True)
                    if kind == "hg" or s not in (4, 8):
                        split_lo(dve, B0 + s // CH + 1, s % CH)
                    for done in ada_collected(CH * B0 + s):
                        ada_collect(done)

            def tail(n, stick, col, turn, g_, steps, banks, B, splits):
                turn_dve(dve, turn, g_, zero_c, GN, steps, 0, banks)
                for s in range(2, 12):
                    at_stage(n, s, stick, col)
                    if 0 <= s - 3 < splits:
                        split_lo(dve, B + 1 + (s - 3) // CH, (s - 3) % CH)
                    if turn == 1:
                        for done in ada_collected(CH * OUT0 + s - 2):
                            ada_collect(done)
                d()

            selector(bT[:, 0, :])
            tail(AT_GROUPS - 1, False, lambda h: slice(AW - NC_ + HD * h, AW - NC_ + HD * (h + 1)), 1, gmix, EARLY1,
                 TAIL, OUT0, CH)
            for t in range(T):
                d()
                dve.tensor_tensor_reduce(QN[:, :, :].rearrange("p t n -> p (t n)"), MIX[:, t, 0:AW], MIX[:, t, 0:AW],
                                         1.0, 0.0, ALU.mult, ALU.add, ssq[:, t:t + 1])
            rsqrt(dve, T, 1.0 / AW, EPS)
            turn_dve(dve, 1, gmix, zero_c, GN, LATE1, len(EARLY1), NARROW)
            for j in range(2):
                split_lo(dve, OUT0 + 2, j)
            dve.wait_ge(mod_mm, 1)
            modulation(GATE1, SHIFT2)
            d()

            def gate_block(n, b, sec, dst):
                dve.tensor_tensor(dst.rearrange("p (k c) -> p k c", c=P), ident[:, :].unsqueeze(1).to_broadcast([P, 4, P]),
                                  mod[:, sec, 4 * b:4 * b + 4].unsqueeze(2).to_broadcast([P, 4, P]),
                                  ALU.mult).then_inc(gate_diag, 1)

            def out_block(b):
                dve.wait_ge(gate_rdy, b + 1)
                dve.wait_ge(x_in, 32)
                dve.wait_ge(chunk_done, CH * OUT0 + last_of(OUT_ORDER, b))
                p = b % 3
                dve.tensor_tensor(VN[:, :, :], PS[:, 2 * p:2 * p + 2, :],
                                  (QN, KN)[b // 2][:, b % 2, :].unsqueeze(1).to_broadcast([P, T, NC_]),
                                  ALU.mult).then_inc(pair_read[p], 1)
                d()
                xs = X[:, :, NC_ * b:NC_ * (b + 1)]
                dve.tensor_tensor(xs, xs, VN[:, :, :], ALU.add)
                block_squares(b)
                d()

            for b in range(4):
                if b >= 2:
                    dve.wait_ge(gate_mm, b - 1)
                gate_block(b, b, GATE1, GN[:, b % 2, :])
                if b == 1:
                    for j in (2, 3):
                        split_lo(dve, OUT0 + 2, j)
            for j in range(CH):
                if j % 2 == 0:
                    out_block(j // 2)
                split_lo(dve, OUT0 + 3, j)
                if j == 1:
                    ada_collect(ADA_BLOCKS - 1)
            dve.wait_ge(mod_mm, 2)
            modulation(SHIFT2, GATE2 + 1)
            scale(g2, SCALE2, "norm2")
            out_block(2)
            for j in range(3):
                split_lo(dve, MLP0, j)
            out_block(3)

            def mlp(m, M, total):
                def square(U, pair):
                    dve.wait_ge(relu_rdy, U + 1)
                    if not isinstance(U, int) or U:
                        dve.wait_ge(h_tr, U)
                    other = RE[:, :, :] if m else PS[:, pair:pair + 2, :]
                    dve.tensor_tensor(SQ[:, :, :], other, RE[:, :, :], ALU.mult).then_inc(sq_rdy, 1)

                def up(B, U):
                    for j in range(CH):
                        split_lo(dve, B + 1, j)
                    square(U, 0)

                def turn(U, par):
                    dve.wait_ge(h_hi, U + 1)
                    flat = "p k s -> p (k s)"
                    dve.tensor_tensor(H_lo[:, par, :, :].rearrange(flat), PS[:, 6:8, :],
                                      H_hi[:, par, :, :].rearrange(flat).bitcast(F32), ALU.subtract).then_inc(h_lo, 1)

                def down(B, U, par):
                    for j in range(CH):
                        split_lo(dve, B + 1, j)
                        ac = total[:, :, NC_ * j:NC_ * (j + 1)]
                        b = pairs[1 + j % 2]
                        dve.tensor_tensor(ac, ac, PS[:, b:b + 2, :], ALU.add).then_inc(acc_read, 1)
                        if j == 1 and par is not None:
                            turn(U + 1, par)

                for j in range(CH):
                    split_lo(dve, M + 1, j)
                square(NU * m, pairs[2])
                for j in range(CH):
                    split_lo(dve, M + 2, j)
                    if j == 1:
                        turn(NU * m, 0)
                square(NU * m + 1, 0)
                dve.wait_ge(acc_read, 4 * NU * m + 2 * (m + 1))
                down(M + 2, NU * m, 1)
                with dve.Fori(0, NU // 2 - 1) as i:
                    for e in range(2):
                        up(M + 3 + 4 * i + 2 * e, NU * m + 2 + 2 * i + e)
                        down(M + 4 + 4 * i + 2 * e, NU * m + 1 + 2 * i + e, e)

            root_of_blocks()
            turn_dve(dve, 2, g2, mod[:, SHIFT2, :], SQ)
            split_lo(dve, MLP0, 3)
            mlp(0, MLP0, ACC)
            def mix_steps(b):
                turn_dve(dve, 3, colB[:, RB["nmix"][0]:RB["nmix"][0] + KT], zero_c, DT,
                         banks=(6, 7) if b else (0, 1), **block_steps(b))

            d()
            gate_block(4, 0, GATE2, DG[:, 0, :])
            for b in range(4):
                cols = slice(NC_ * b, NC_ * (b + 1))
                if b < 3:
                    dve.wait_ge(gate_mm, 4 + b)
                    gate_block(4 + b + 1, b + 1, GATE2, DG[:, (b + 1) % 2, :])
                if b in (1, 2):
                    split_lo(dve, QKV0, b - 1)
                dve.wait_ge(chunk_done, 4 * (QKV0 - 1) + b + 1)
                pb = pairs[1 + b % 2]
                dve.tensor_tensor(ACC[:, :, cols], ACC[:, :, cols], PS[:, pb:pb + 2, :], ALU.add).then_inc(acc_read, 1)
                if b in (1, 2):
                    block_squares(b - 1, b)
                if b == 2:
                    mix_steps(0)
            mix_steps(1)
            for b in (2, 3):
                split_lo(dve, QKV0, b)
                mix_steps(b)
            for b in (2, 3):
                block_squares(b, b + 1)
            root_of_blocks()
            dve.tensor_copy(row_r[:, :], rstd[:, 0:T]).then_inc(row_rdy, 1)

            def sb_cols(g):
                return lambda h: bass.ds(NC_ * g + HD * h, HD)

            def sb_group(g, first):
                B0 = QKV0 + 3 * g
                for s in range(12):
                    if not first:
                        at_stage(AT_GROUPS + g - 1, s, True, sb_cols(g - 1))
                    at_own(AT_GROUPS + g, B0, s, False)
                    if s not in (4, 8):
                        split_lo(dve, B0 + s // CH + 1, s % CH)

            sb_group(0, True)
            start_jobs = jobs.n
            with dve.Fori(1, SB_GROUPS) as g:
                jobs.base, jobs.n = start_jobs + 2 * (g - 1), 0
                sb_group(g, False)
            jobs.base, jobs.n = 0, start_jobs + 2 * (SB_GROUPS - 1)
            d()
            tail(AT_GROUPS + SB_GROUPS - 1, True, sb_cols(SB_GROUPS - 1), 4, one_c, EARLY4, TAIL, WO0, 2 * CH)
            turn_dve(dve, 4, one_c, zero_c, GN, LATE4, len(EARLY4), NARROW)

            def wo_block(b):
                dve.wait_ge(chunk_done, CH * WO0 + last_of(WO_ORDER, b))
                xs, p = X[:, :, NC_ * b:NC_ * (b + 1)], b % 3
                dve.tensor_tensor(xs, xs, PS[:, 2 * p:2 * p + 2, :], ALU.add).then_inc(pair_read[p], 1)

            def mlp_steps(b):
                turn_dve(dve, 5, colB[:, RB["nmlp"][0]:RB["nmlp"][0] + KT], zero_c, SQ, banks=NARROW, **block_steps(b))

            for j in range(CH):
                split_lo(dve, WO0 + 3, j)
                if j < 3:
                    wo_block(j)
                    block_squares(j)
            for b in range(4):
                split_lo(dve, MLP1, b)
                if b == 2:
                    wo_block(3)
                mlp_steps(b)
            block_squares(3)
            root_of_blocks()
            dve.memset(ssq[:, 0:1], 1.0).then_inc(acc_read, 2)
            mlp(1, MLP1, X)
            for b in range(4):
                cols, pb = slice(NC_ * b, NC_ * (b + 1)), pairs[1 + b % 2]
                dve.wait_ge(chunk_done, 4 * (END - 1) + b + 1)
                dve.tensor_tensor(X[:, :, cols], X[:, :, cols], PS[:, pb:pb + 2, :], ALU.add).then_inc(acc_read, 1)

        @block.tensor
        def _(pe):
            used = [0, 0, 0]

            def take(p):
                if not isinstance(used[p], int) or used[p]:
                    pe.wait_ge(pair_read[p], used[p])
                used[p] = used[p] + 1

            pe.wait_ge(pool_const, N_CONST)
            pe.wait_ge(params_in, 16 * 11)
            pe.transpose(bank(6, 0, P), setup[:, 0:P], ident[:, :])
            pe.transpose(bank(6, P, P + NRB), setup[0:NRB, P:2 * P], ident[0:NRB, 0:NRB]).then_inc(pe_const, 1)
            pe.wait_ge(dve_const, 1)
            for h in range(2):
                pe.wait_ge(ada_used, CH + KT * (h + 1))
                for k in range(KT):
                    mm = pe.matmul(bank(6, KT * h + k, KT * h + k + 1), MS[:, h, k * P:k * P + P],
                                   ones[:, 0:1], start=True, stop=True)
                mm.then_inc(ada_sum, 1)

            def mod_columns(n0, n1, Z):
                pe.wait_ge(sel_rdy, 1)
                for r in range(4):
                    rhs = ada_part[:, n0:n1, :].rearrange("p n (c r) -> p (n c) r", r=4)[:, :, r]
                    mm = pe.matmul(bank(6, 0, 4 * (n1 - n0)), Z[:, 96 - 32 * r:224 - 32 * r], rhs,
                                   start=r == 0, stop=r == 3)
                mm.then_inc(mod_mm, 1)

            def turn_group(src, first_bank):
                for i in range(2):
                    for q in range(4):
                        h, t = 2 * i + q // 2, q % 2
                        mm = pe.transpose(bank(first_bank + i, P * q, P * q + P), src[:, t, HD * h:HD * (h + 1)], ident[:, :])
                return mm

            def hg_own(g, s):
                if s == 10:
                    take(1)
                    turn_group(QN, 2).then_inc(hg_tr, 1)
                if s == 13:
                    take(0)
                    turn_group(KN, 0).then_inc(hg_tr, 1)

            def hg_stage(g, s):
                l = 0 if s == 0 else s - 1
                if s == 0 or 1 <= l < NLV:
                    b = level_bank(l)
                    if l == 0:
                        pe.wait_ge(f_rdy, g + 1)
                        pe.wait_ge(pair_read[1], 3 * g + 2)
                        if g:
                            pe.wait_ge(o_out, g)
                        else:
                            pe.wait_ge(a_lo, KT // 2)
                    else:
                        pe.wait_ge(lv_rdy, 8 * g + l)
                        before = {1: 0, 2: 1, 3: 2, 4: 3, 5: 4, 6: 5, 7: 7, 8: 8}[l]
                        if NLV * g + before:
                            pe.wait_ge(lv_cp, NLV * g + before)
                    for h in range(GH):
                        if l == 1:
                            mm = pe.matmul(bank(b, P * h, P * h + P), QK[:, h, 0:P], QK[:, h, P:S], start=True, stop=True)
                        else:
                            for t in range(T):
                                k_, q_ = (kT, qT) if l == 0 else (QK, QK)
                                cols = slice(P * t, P * t + P)
                                mm = pe.matmul(bank(b + t, P * h, P * h + P), k_[:, h, cols], q_[:, h, cols], start=True, stop=True)
                    mm.then_inc(lv_mm, 1)
                if s == 10:
                    pe.wait_ge(lv_cp, NLV * (g + 1))
                    pe.wait_ge(pair_read[0], 3 * g + 2)
                    for h in range(GH):
                        cols = slice(HD * h, HD * (h + 1))
                        pe.matmul(bank(6, P * h, P * h + P), AM[:, 0, h, :], VN[:, 0, cols], start=True, stop=True)
                        pe.matmul(bank(7, P * h, P * h + P), AM[:, 2, h, :], VN[:, 0, cols], start=True, stop=False)
                        mm = pe.matmul(bank(7, P * h, P * h + P), AM[:, 1, h, :], VN[:, 1, cols], start=False, stop=True)
                    mm.then_inc(o_mm, 1)

            def at_own(n, s):
                if s == 9:
                    pe.wait_ge(n_rdy, 2 * n + 1)
                    turn_group(QN, 0).then_inc(n_tr, 1)
                if s == 11:
                    pe.wait_ge(n_rdy, 2 * n + 2)
                    turn_group(KN, 2).then_inc(n_tr, 1)

            E0f = E0[:, :, :].rearrange("p h s -> p (h s)")
            AMf = AM[:, :, :, :].rearrange("p r h s -> p (r h s)")

            def at_stage(n, s, stick):
                if s >= 1 and s % 2 == 1 and s <= 2 * GH - 1:
                    h = s // 2
                    if h == 0:
                        if isinstance(n, int) and n == 0:
                            pe.wait_ge(o_out, HG_GROUPS)
                        elif stick:
                            pe.wait_ge(a_lo, 4 * KT // 2)
                    if not (isinstance(n, int) and n == 0 and h == 0):
                        pe.wait_ge(p_rdy, 4 * n + h)
                    if stick:
                        pe.matmul(bank(6, 0, S), kT[:, h, 0:P], qT[:, h, :], start=True, stop=True)
                        mm = pe.matmul(bank(6, S, S + P), kT[:, h, P:S], qT[:, h, P:S], start=True, stop=True)
                    else:
                        pe.matmul(bank(6, 0, P), qT[:, h, 0:P], kT[:, h, 0:P], start=True, stop=True)
                        mm = pe.matmul(bank(6, P, 3 * P), qT[:, h, P:S], kT[:, h, :], start=True, stop=True)
                    mm.then_inc(s_mm, 1)
                if s >= 2 and s % 2 == 0 and s <= 2 * GH:
                    h = s // 2 - 1
                    pe.wait_ge(p_rdy, 4 * n + h + 1)
                    if not (isinstance(n, int) and n == 0 and h == 0):
                        pe.wait_ge(pv_out, 4 * n + h)
                    if stick:
                        L = E0f[:, 384:768]
                        pe.matmul(bank(7, 0, P), below[:, :], L[:, 0:P], start=True, stop=True)
                        pe.matmul(bank(7, P, S), below[:, :], L[:, P:S], start=True, stop=False)
                        pe.matmul(bank(7, P, S), ones[:, :], L[:, S:S + P], start=False, stop=True)
                        mm = pe.matmul(bank(7, S, S + P), below[:, :], L[:, S:S + P], start=True, stop=True)
                    else:
                        for i in range(3):
                            mm = pe.transpose(bank(7, P * i, P * i + P), E0f[:, 384 + P * i:512 + P * i], ident[:, :])
                    mm.then_inc(pT_mm, 1)
                if s >= 3 and s % 2 == 1 and s <= 2 * GH + 1:
                    h = (s - 3) // 2
                    cols = slice(HD * h, HD * (h + 1))
                    if h == 0:
                        pe.wait_ge(pair_read[2], n + 1)
                    pe.wait_ge(pT_rdy, 4 * n + h + 1)
                    pe.matmul(bank(7, 0, HD), AMf[:, 0:P], VN[:, 0, cols], start=True, stop=True)
                    pe.matmul(bank(7, HD, 2 * HD), AMf[:, P:2 * P], VN[:, 0, cols], start=True, stop=False)
                    pe.matmul(bank(7, HD, 2 * HD), AMf[:, 2 * P:3 * P], VN[:, 1, cols], start=False, stop=True).then_inc(pv_mm, 1)

            def turn(n, src, **parts):
                turn_pe(pe, n, src, **parts)

            pe.wait_ge(mod_rdy, 1)
            turn(0, Y0)
            groups = proj_groups()
            for i, (kind, idx, B0, nb) in enumerate(groups):
                prev_used = list(used)
                for s in range(CH * nb):
                    p = (s // CH) % 2 if kind == "hg" else s // CH
                    if s % CH == 0:
                        take(p)
                        if p == 2 and idx == 0:
                            pe.wait_ge(lv_cp, NLV * (HG_GROUPS - 1) + 6)
                    a_chunk(pe, B0 + s // CH, s % CH, pairs[p], 0 if i == 0 and s < CH else None)
                    if i:
                        pk, pi, pB, _ = groups[i - 1]
                        if pk == "hg":
                            hg_stage(pi, s)
                        else:
                            if s == 1:
                                for p in range(2):
                                    pe.wait_ge(pair_read[p], prev_used[p])
                            at_stage(pi, s, False)
                    (hg_own if kind == "hg" else at_own)(idx, s)

            def tail(n, stick, turned, steps, B, order, early):
                for p in range(2):
                    pe.wait_ge(pair_read[p], used[p])
                at_stage(n, 1, stick)
                pe.wait_ge(pv_out, 4 * n)
                pe.wait_ge(pair_read[2], used[2])
                turn(turned, MIX, steps=steps, banks=TAIL)
                for s in range(2, 12):
                    if s - 2 < early:
                        pe.wait_ge(a_lo, KT // 2 * turned + min(len(steps), 2 * (s - 1)))
                        square_chunk(pe, B, order, s - 2, take)
                    at_stage(n, s, stick)

            tail(AT_GROUPS - 1, False, 1, EARLY1, OUT0, OUT_ORDER, OUT_EARLY)

            def gate_spread(n, b, diag):
                pe.wait_ge(gate_diag, n + 1)
                if b >= 2:
                    pe.wait_ge(gate_rdy, n - 1)
                pe.matmul(bank(6 + b % 2), ones[:, :], diag, start=True, stop=True).then_inc(gate_mm, 1)

            pe.wait_ge(pv_out, 4 * AT_GROUPS)
            turn(1, MIX, steps=LATE1, first=len(EARLY1), banks=NARROW)
            for pos in range(OUT_EARLY, CH * 4):
                if pos == CH * 3 - 1:
                    pe.wait_ge(gate_rdy, 4)
                    pe.wait_ge(parts_rdy, 1)
                    mod_columns(D // NC_, ADA_BLOCKS, bT[:, 0, :])
                if pos < OUT_EARLY + 2:
                    pe.wait_ge(a_lo, KT // 2 + len(EARLY1) + 2 * (pos - OUT_EARLY + 1))
                square_chunk(pe, OUT0, OUT_ORDER, pos, take)
                if pos == OUT_EARLY:
                    pe.wait_ge(a_aff, 2 * KT // 2)
                    mod_columns(0, D // NC_, bT[:, 0, :])
                if pos in (OUT_EARLY + 1, OUT_EARLY + 2):
                    pe.wait_ge(mod_rdy, 2)
                    for b in (2 * (pos - OUT_EARLY - 1), 2 * (pos - OUT_EARLY) - 1):
                        gate_spread(b, b, GN[:, b % 2, :])

            def mlp(m, M):
                def up(B, U, turned=None, pair=0, turn_last=False):
                    if turned is None and not turn_last:
                        pe.wait_ge(sq_rdy, U)
                    for j in range(CH):
                        a_chunk(pe, B, j, pair, turned)
                        if turned == 5 and j == 0:
                            mlp_turn(3)
                        if turn_last and j == 1:
                            turn_unit(U - 1)

                def turn_unit(U):
                    pe.wait_ge(sq_rdy, U + 1)
                    if not isinstance(U, int) or U:
                        pe.wait_ge(h_lo, U)
                    turn_group(SQ, 6).then_inc(h_tr, 1)

                def down(B, U, par, turn_next, gates=False):
                    pe.wait_ge(h_lo, U + 1)
                    for j in range(CH):
                        pe.wait_ge(acc_read, 4 * U + 2 * m + j + 1)
                        chunk(pe, B, j, pairs[1 + j % 2], lambda k, t: H_hi[:, par, k, P * t:P * t + P],
                              lambda k, t: H_lo[:, par, k, P * t:P * t + P], True, True)
                        if j == 1 and turn_next:
                            turn_unit(U + 1)
                        if gates:
                            for b in ((0,), (1,), (2, 3), ())[j]:
                                gate_spread(4 + b, b, DG[:, b % 2, :])
                        if gates and j >= 2:
                            mix_turn(j - 2)

                up(M, NU * m, (2, 5)[m], pair=pairs[2])
                up(M + 1, NU * m + 1, turn_last=True)
                down(M + 2, NU * m, 0, True)
                with pe.Fori(0, NU // 2 - 1) as i:
                    for e in range(2):
                        up(M + 3 + 4 * i + 2 * e, NU * m + 2 + 2 * i + e)
                        down(M + 4 + 4 * i + 2 * e, NU * m + 1 + 2 * i + e, 1 - e, True)
                down(M + 2 * NU - 1, NU * m + NU - 1, 1, False, m == 0)

            def mix_turn(b):
                pe.wait_ge(x_block, b + 1)
                if b == 1:
                    pe.wait_ge(gate_rdy, 8)
                if b > 1:
                    pe.wait_ge(a_aff, 3 * KT // 2 + 2 * b)
                turn(3, X, banks=(6, 7) if b else (0, 1), **block_steps(b))

            turn(2, ACC)
            mlp(0, MLP0)

            def sb_group(base, g, first):
                B0, n = QKV0 + 3 * g, AT_GROUPS + g
                used[0], used[1], used[2] = base[0] + g, base[1] + g, base[2] + g
                for s in range(12):
                    if s % CH == 0:
                        take(s // CH)
                    if first and s == 0:
                        pe.wait_ge(a_aff, 3 * KT // 2 + 2)
                    a_chunk(pe, B0 + s // CH, s % CH, pairs[s // CH], 3 if first and s < CH else None)
                    if first and s < 2:
                        mix_turn(s + 2)
                    if not first:
                        if s == 1:
                            for p in range(2):
                                pe.wait_ge(pair_read[p], base[p] + g)
                        at_stage(n - 1, s, True)
                    at_own(n, s)

            base = list(used)
            sb_group(base, 0, True)
            with pe.Fori(1, SB_GROUPS) as g:
                sb_group(base, g, False)
            for p in range(3):
                used[p] = base[p] + SB_GROUPS
            tail(AT_GROUPS + SB_GROUPS - 1, True, 4, EARLY4, WO0, WO_ORDER, WO_EARLY)
            pe.wait_ge(pv_out, 4 * (AT_GROUPS + SB_GROUPS))
            turn(4, MIX, steps=LATE4, first=len(EARLY4), banks=NARROW)
            pe.wait_ge(a_lo, 5 * KT // 2)
            def mlp_turn(b):
                pe.wait_ge(pair_read[b % 3], used[b % 3] - (b == 0))
                if b:
                    pe.wait_ge(a_aff, 5 * KT // 2 + 2 * b)
                turn(5, X, banks=NARROW, **block_steps(b))

            for pos in range(WO_EARLY, CH * 4):
                square_chunk(pe, WO0, WO_ORDER, pos, take)
                if pos > CH * 3:
                    mlp_turn(pos - CH * 3 - 1)
            mlp(1, MLP1)


def level_bank(l):
    return 4 if l in (1, 3, 5) else 6


def proj_groups():
    g = [("hg", i, PROJ0 + 4 * i, 4) for i in range(HG_GROUPS)]
    return g + [("at", i, PROJ0 + 4 * HG_GROUPS + 3 * i, 3) for i in range(AT_GROUPS)]


def proj_columns():
    cols = [3 * AW + part * HW + g * NC_ for g in range(HG_GROUPS) for part in range(4)]
    return cols + [part * AW + g * NC_ for g in range(AT_GROUPS) for part in range(3)]


_INS = ["x", "c", "positions", "norm1_w", "w_ada", "b_ada", "w_in", "q_norm_w", "k_norm_w", "attn_out_norm_w",
        "hg_lb_logits", "hg_norm_w", "w_out", "norm2_w", "w_ff1", "w_ff2", "norm_mix_g_2", "norm_mlp_g_2",
        "sb_w_qkv_2", "sb_q_norm_g_2", "sb_k_norm_g_2", "sb_w_o_2", "mlp_w_in_2", "mlp_w_out_2"]


def kernel(**inputs):
    from concourse import bacc
    from concourse.bass_utils import run_bass_kernel_spmd

    nc = bacc.Bacc("TRN2", target_bir_lowering=False, num_devices=1, dynamic_dma_scratch_size=1024)
    arrays, args = {}, {}
    for name in _INS:
        arr = np.ascontiguousarray(inputs[name])
        arrays[f"in_{name}_dram"] = arr
        args[name] = nc.dram_tensor(f"in_{name}_dram", arr.shape, mybir.dt.from_np(arr.dtype), kind="ExternalInput").ap()
    out = nc.dram_tensor("out_dram", (1, S, D), F32, kind="ExternalOutput").ap()
    build(nc, args, out)
    r = run_bass_kernel_spmd(nc, [arrays], core_ids=[0])
    return r.results[0]["out_dram"]
```
